# Optimizing a Trainium2 kernel written in Bass

```python
import math
import jax, jax.numpy as jnp
from jax import lax
import numpy as np

D_MODEL = 1024
BATCH = 1
SEQ = 256
DEPTH = 2

D_FF = 2816
D_POOL = 256
POOL_WINDOWS = (2, 4, 8, 16)
POOL_GROUP = D_POOL // len(POOL_WINDOWS)
D_CONV = 256
CONV_WIDTH = 3
NA_HEADS = 8
NA_HEAD_DIM = 64
D_NA = NA_HEADS * NA_HEAD_DIM
D_MIX = D_POOL + D_CONV + D_NA
GRID_W = 64
NA_ROWS = 8
NA_COLS = 16
D_IN = D_POOL + 3 * D_CONV + 3 * D_NA
ALPHA = (2.0 * DEPTH) ** 0.25
BETA = (8.0 * DEPTH) ** -0.25
LN_EPS = 1e-5
NEG_INF = -1e30


def layer_norm(x, g, b):
    xf = x.astype(jnp.float32)
    mu = jnp.mean(xf, axis=-1, keepdims=True)
    var = jnp.mean(jnp.square(xf - mu), axis=-1, keepdims=True)
    y = (xf - mu) * lax.rsqrt(var + LN_EPS)
    return (y * g.astype(jnp.float32) + b.astype(jnp.float32)).astype(x.dtype)

def swiglu(x, w_gate, w_up, w_down):
    return (jax.nn.silu(x @ w_gate) * (x @ w_up)) @ w_down

def pool_mixer(u, pool_w, pool_scale):
    bsz, s, _ = u.shape
    ng = len(POOL_WINDOWS)
    uf = u.astype(jnp.float32).reshape(bsz, s, ng, POOL_GROUP)
    cs = jnp.concatenate([jnp.zeros((bsz, 1, ng, POOL_GROUP), jnp.float32),
                          jnp.cumsum(uf, axis=1)], axis=1)
    t = jnp.arange(s)
    outs = []
    for g, w in enumerate(POOL_WINDOWS):
        lo = jnp.clip(t - w // 2, 0, s)
        hi = jnp.clip(t - w // 2 + w, 0, s)
        cnt = (hi - lo).astype(jnp.float32)[None, :, None]
        mean = (cs[:, hi, g] - cs[:, lo, g]) / cnt
        outs.append(mean - uf[:, :, g])
    p = jnp.stack(outs, axis=2).astype(u.dtype)
    y = jnp.einsum('bsgc,gcd->bsgd', p, pool_w) * pool_scale.reshape(ng, POOL_GROUP)
    return y.reshape(bsz, s, D_POOL)

def gated_conv_mixer(gate_b, gate_c, h, conv_w):
    z = gate_c * h
    zp = jnp.pad(z, ((0, 0), (1, 1), (0, 0)))
    y = conv_w[0] * zp[:, :-2] + conv_w[1] * zp[:, 1:-1] + conv_w[2] * zp[:, 2:]
    return gate_b * y

def neighbourhood_attention(q, k, v, rpb):
    bsz, s, _ = q.shape
    rows = s // GRID_W
    kr = min(NA_ROWS, rows)
    shp = (bsz, rows, GRID_W, NA_HEADS, NA_HEAD_DIM)
    q, k, v = q.reshape(shp), k.reshape(shp), v.reshape(shp)
    r = jnp.arange(rows)
    row_start = jnp.clip(r - kr // 2, 0, rows - kr)
    row_idx = row_start[:, None] + jnp.arange(kr)[None, :]
    kb = k[:, row_idx]
    vb = v[:, row_idx]
    c = jnp.arange(GRID_W)
    col_start = jnp.clip(c - NA_COLS // 2, 0, GRID_W - NA_COLS)
    col_valid = (c[None, :] >= col_start[:, None]) & (c[None, :] < col_start[:, None] + NA_COLS)
    dr = row_idx - r[:, None] + (NA_ROWS - 1)
    dc = jnp.clip(c[None, :] - c[:, None], -(NA_COLS - 1), NA_COLS - 1) + (NA_COLS - 1)
    bias = rpb[:, dr[:, None, :, None], dc[None, :, None, :]]
    scores = jnp.einsum('brqhd,brikhd->bhrqik', q, kb).astype(jnp.float32) * (NA_HEAD_DIM ** -0.5)
    scores = scores + bias.astype(jnp.float32)
    scores = jnp.where(col_valid[:, None, :], scores, NEG_INF)
    p = jax.nn.softmax(scores, axis=(-2, -1)).astype(v.dtype)
    o = jnp.einsum('bhrqik,brikhd->brqhd', p, vb)
    return o.reshape(bsz, s, D_NA)

def first_inputs(seed: int = 0) -> dict:
    key = jax.random.key(seed)
    ks = jax.random.split(key, 16)
    L, D, F = DEPTH, D_MODEL, D_FF
    nrm = lambda k, shp: jax.random.normal(k, shp, jnp.float32)
    x = nrm(ks[0], (BATCH, SEQ, D))
    ffn1_w_gate = nrm(ks[1], (L, D, F)) * D ** -0.5
    ffn1_w_up = nrm(ks[2], (L, D, F)) * D ** -0.5
    ffn1_w_down = nrm(ks[3], (L, F, D)) * (BETA * F ** -0.5)
    ffn2_w_gate = nrm(ks[4], (L, D, F)) * D ** -0.5
    ffn2_w_up = nrm(ks[5], (L, D, F)) * D ** -0.5
    ffn2_w_down = nrm(ks[6], (L, F, D)) * (BETA * F ** -0.5)
    col_scale = jnp.concatenate([
        jnp.ones((D_POOL + 2 * D_CONV,), jnp.float32),
        jnp.full((D_CONV,), BETA, jnp.float32),
        jnp.ones((2 * D_NA,), jnp.float32),
        jnp.full((D_NA,), BETA, jnp.float32)])
    w_in = nrm(ks[7], (L, D, D_IN)) * D ** -0.5 * col_scale
    pool_w = nrm(ks[8], (L, len(POOL_WINDOWS), POOL_GROUP, POOL_GROUP)) * POOL_GROUP ** -0.5
    pool_scale = 1.0 + 0.1 * nrm(ks[9], (L, D_POOL))
    conv_w = nrm(ks[10], (L, CONV_WIDTH, D_CONV)) * CONV_WIDTH ** -0.5
    rpb = 0.02 * nrm(ks[11], (L, NA_HEADS, 2 * NA_ROWS - 1, 2 * NA_COLS - 1))
    w_out = nrm(ks[12], (L, D_MIX, D)) * (BETA * D_MIX ** -0.5)
    ln_g = 1.0 + 0.05 * nrm(ks[13], (L, 3, D))
    ln_b = 0.02 * nrm(ks[14], (L, 3, D))
    return {"x": x,
            "ffn1_w_gate": ffn1_w_gate, "ffn1_w_up": ffn1_w_up, "ffn1_w_down": ffn1_w_down,
            "ffn2_w_gate": ffn2_w_gate, "ffn2_w_up": ffn2_w_up, "ffn2_w_down": ffn2_w_down,
            "w_in": w_in, "pool_w": pool_w, "pool_scale": pool_scale, "conv_w": conv_w,
            "rpb": rpb, "w_out": w_out, "ln_g": ln_g, "ln_b": ln_b}

def first_block(x, ffn1_w_gate, ffn1_w_up, ffn1_w_down, ffn2_w_gate, ffn2_w_up, ffn2_w_down,
              w_in, pool_w, pool_scale, conv_w, rpb, w_out, ln_g, ln_b):
    splits = np.cumsum([D_POOL, D_CONV, D_CONV, D_CONV, D_NA, D_NA])
    for l in range(DEPTH):
        x = layer_norm(ALPHA * x + 0.5 * swiglu(x, ffn1_w_gate[l], ffn1_w_up[l], ffn1_w_down[l]),
                       ln_g[l, 0], ln_b[l, 0])
        proj = x @ w_in[l]
        u, gb, gc, h, q, k, v = jnp.split(proj, splits, axis=-1)
        y_a = pool_mixer(u, pool_w[l], pool_scale[l])
        y_b = gated_conv_mixer(gb, gc, h, conv_w[l])
        y_c = neighbourhood_attention(q, k, v, rpb[l])
        y = jnp.concatenate([y_a, y_b, y_c], axis=-1) @ w_out[l]
        x = layer_norm(ALPHA * x + y, ln_g[l, 1], ln_b[l, 1])
        x = layer_norm(ALPHA * x + 0.5 * swiglu(x, ffn2_w_gate[l], ffn2_w_up[l], ffn2_w_down[l]),
                       ln_g[l, 2], ln_b[l, 2])
    return x


N_MEM = 256
N_BRANCH = 3
NORM_EPS = 1e-6
MLA_HEADS = 8
MLA_NOPE = 64
MLA_ROPE = 32
MLA_V = 64
MLA_Q_RANK = 256
MLA_KV_RANK = 128
ROPE_THETA = 10000.0
Q_BLOCK = 128
MLA_W = MLA_HEADS * MLA_V
GLA_HEADS = 4
GLA_DK = 64
GLA_DV = 128
GLA_GATE_RANK = 16
GLA_GATE_NORM = 16.0
GLA_CHUNK = 64
GLA_W = GLA_HEADS * GLA_DV
RWKV_HEADS = 8
RWKV_N = 64
RWKV_DECAY_RANK = 64
RWKV_ICLR_RANK = 64
RWKV_GATE_RANK = 160
RWKV_GN_EPS = 64e-5
RWKV_W = RWKV_HEADS * RWKV_N
RWKV_COLS = 3 * RWKV_W + RWKV_DECAY_RANK + RWKV_ICLR_RANK + RWKV_GATE_RANK
MEM_HEADS = 4
MEM_HD = D_MODEL // MEM_HEADS
IN_SPLITS = (MLA_Q_RANK, MLA_KV_RANK, MLA_ROPE,
             GLA_HEADS * GLA_DK, GLA_HEADS * GLA_DK, GLA_W, GLA_W, GLA_GATE_RANK,
             RWKV_COLS, N_BRANCH * D_MODEL)
D_IN_2 = sum(IN_SPLITS)
BRANCH_W = MLA_W + GLA_W + RWKV_W


def _offsets(sizes):
    out, acc = [], 0
    for s in sizes[:-1]:
        acc += s
        out.append(acc)
    return out

def _rmsnorm(x, g, eps=NORM_EPS):
    xf = x.astype(jnp.float32)
    y = xf * lax.rsqrt(jnp.mean(xf * xf, axis=-1, keepdims=True) + eps)
    return y.astype(x.dtype) * g

def _rope(t, cos, sin):
    t1, t2 = jnp.split(t, 2, axis=-1)
    return jnp.concatenate([t1 * cos - t2 * sin, t1 * sin + t2 * cos], axis=-1).astype(t.dtype)

def _swiglu(h, w_in, w_out):
    g, u = jnp.split(h @ w_in, 2, axis=-1)
    return (jax.nn.silu(g) * u) @ w_out

def _mla_branch(c_q, c_kv, k_rope_raw, q_norm, w_uq, kv_norm, w_ukv, cos, sin):
    B, S, _ = c_q.shape
    H = MLA_HEADS
    q = (_rmsnorm(c_q, q_norm) @ w_uq).reshape(B, S, H, MLA_NOPE + MLA_ROPE)
    q_nope = q[..., :MLA_NOPE]
    q_rot = _rope(q[..., MLA_NOPE:], cos[:, :, None, :], sin[:, :, None, :])
    kv = (_rmsnorm(c_kv, kv_norm) @ w_ukv).reshape(B, S, H, MLA_NOPE + MLA_V)
    k_nope, v = kv[..., :MLA_NOPE], kv[..., MLA_NOPE:]
    k_rot = _rope(k_rope_raw, cos, sin)
    scale = (MLA_NOPE + MLA_ROPE) ** -0.5
    nb = S // Q_BLOCK
    qn_b = q_nope.reshape(B, nb, Q_BLOCK, H, MLA_NOPE).swapaxes(0, 1)
    qr_b = q_rot.reshape(B, nb, Q_BLOCK, H, MLA_ROPE).swapaxes(0, 1)
    k_pos = jnp.arange(S)

    def block(args):
        qn, qr, blk = args
        s = (jnp.einsum('bqhd,bkhd->bhqk', qn, k_nope)
             + jnp.einsum('bqhr,bkr->bhqk', qr, k_rot)).astype(jnp.float32) * scale
        q_pos = blk * Q_BLOCK + jnp.arange(Q_BLOCK)
        s = jnp.where(k_pos[None, :] <= q_pos[:, None], s, -1e30)
        p = jax.nn.softmax(s, axis=-1).astype(v.dtype)
        return jnp.einsum('bhqk,bkhd->bqhd', p, v)

    o = lax.map(block, (qn_b, qr_b, jnp.arange(nb)))
    return o.swapaxes(0, 1).reshape(B, S, MLA_W)

def _gla_branch(q, k, v, g, a_lr, w_alpha, b_alpha, norm_g):
    B, S, _ = q.shape
    H, C = GLA_HEADS, GLA_CHUNK
    nc = S // C
    q = q.reshape(B, S, H, GLA_DK) * GLA_DK ** -0.5
    k = k.reshape(B, S, H, GLA_DK)
    v = v.reshape(B, S, H, GLA_DV)
    log_a = (jax.nn.log_sigmoid((a_lr @ w_alpha + b_alpha).astype(jnp.float32))
             / GLA_GATE_NORM).reshape(B, S, H, GLA_DK)

    def to_chunks(t):
        return t.reshape(B, nc, C, H, t.shape[-1]).transpose(1, 0, 3, 2, 4)

    causal = jnp.tril(jnp.ones((C, C), dtype=bool))[:, :, None]

    def step(state, inp):
        qc, kc, vc, lac = inp
        b = jnp.cumsum(lac, axis=2)
        b_last = b[:, :, -1:, :]
        diff = b[:, :, :, None, :] - b[:, :, None, :, :]
        decay = jnp.exp(jnp.where(causal, diff, -jnp.inf))
        attn = jnp.einsum('bhid,bhjd,bhijd->bhij', qc, kc, decay)
        o = (jnp.einsum('bhij,bhjv->bhiv', attn, vc)
             + jnp.einsum('bhid,bhdv->bhiv', qc * jnp.exp(b), state))
        state = (state * jnp.exp(b_last)[:, :, 0, :, None]
                 + jnp.einsum('bhjd,bhjv->bhdv', kc * jnp.exp(b_last - b), vc))
        return state, o

    s0 = jnp.zeros((B, H, GLA_DK, GLA_DV), jnp.float32)
    _, o = lax.scan(step, s0, (to_chunks(q), to_chunks(k), to_chunks(v), to_chunks(log_a)))
    o = o.transpose(1, 0, 3, 2, 4).reshape(B, S, H, GLA_DV).astype(v.dtype)
    o = _rmsnorm(o, norm_g).reshape(B, S, GLA_W)
    return o * jax.nn.silu(g)

def _rwkv_branch(z, mu, w0, w_decay, a0, w_iclr, w_gate, k_k, k_a, r_k, ln_w, ln_b):
    B, S, _ = z.shape
    H, N = RWKV_HEADS, RWKV_N
    z_prev = jnp.pad(z, ((0, 0), (1, 0), (0, 0)))[:, :-1]
    z = z + mu * (z_prev - z)
    r, k, v, xw, xa, xg = jnp.split(
        z, _offsets((RWKV_W, RWKV_W, RWKV_W, RWKV_DECAY_RANK, RWKV_ICLR_RANK, RWKV_GATE_RANK)), axis=-1)
    w_log = -jax.nn.softplus(-(w0 + jnp.tanh(xw) @ w_decay).astype(jnp.float32)) - 0.5
    decay = jnp.exp(-jnp.exp(w_log))
    a = jax.nn.sigmoid(a0 + xa @ w_iclr)
    g = jax.nn.sigmoid(xg) @ w_gate
    heads = lambda t: t.reshape(B, S, H, N)
    kk = heads(k * k_k).astype(jnp.float32)
    kk = kk / jnp.maximum(jnp.linalg.norm(kk, axis=-1, keepdims=True), 1e-12)
    k = k * (1 + (a - 1) * k_a)
    r_h, k_h, v_h, a_h, w_h = heads(r), heads(k), heads(v), heads(a), heads(decay)
    seq_major = lambda t: jnp.moveaxis(t.astype(jnp.float32), 1, 0)

    def step(state, inp):
        r_t, w_t, k_t, v_t, kk_t, a_t = inp
        sa = jnp.einsum('bhij,bhj->bhi', state, kk_t)
        state = (state * w_t[:, :, None, :]
                 - sa[..., None] * (kk_t * a_t)[:, :, None, :]
                 + v_t[..., None] * k_t[:, :, None, :])
        return state, jnp.einsum('bhij,bhj->bhi', state, r_t)

    s0 = jnp.zeros((B, H, N, N), jnp.float32)
    _, y = lax.scan(step, s0, (seq_major(r_h), seq_major(w_h), seq_major(k_h),
                               seq_major(v_h), seq_major(kk), seq_major(a_h)))
    y = jnp.moveaxis(y, 0, 1)
    mean = jnp.mean(y, axis=-1, keepdims=True)
    var = jnp.mean(jnp.square(y - mean), axis=-1, keepdims=True)
    yn = ((y - mean) * lax.rsqrt(var + RWKV_GN_EPS)).reshape(B, S, RWKV_W).astype(z.dtype) * ln_w + ln_b
    bonus = jnp.sum(r_h * k_h * r_k.reshape(H, N), axis=-1, keepdims=True) * v_h
    return (yn + bonus.reshape(B, S, RWKV_W)) * g

def _mixer_block(h, cos, sin, w_in, mla_q_norm, mla_w_uq, mla_kv_norm, mla_w_ukv,
                 gla_w_alpha, gla_b_alpha, gla_norm,
                 rwkv_mu, rwkv_w0, rwkv_w_decay, rwkv_a0, rwkv_w_iclr, rwkv_w_gate,
                 rwkv_k_k, rwkv_k_a, rwkv_r_k, rwkv_ln_w, rwkv_ln_b, w_branch, w_out):
    B, S, _ = h.shape
    (c_q, c_kv, k_rope, gla_q, gla_k, gla_v, gla_g, gla_a, rwkv_z, gate_logits) = jnp.split(
        h @ w_in, _offsets(IN_SPLITS), axis=-1)
    o_a = _mla_branch(c_q, c_kv, k_rope, mla_q_norm, mla_w_uq, mla_kv_norm, mla_w_ukv, cos, sin)
    o_b = _gla_branch(gla_q, gla_k, gla_v, gla_g, gla_a, gla_w_alpha, gla_b_alpha, gla_norm)
    o_c = _rwkv_branch(rwkv_z, rwkv_mu, rwkv_w0, rwkv_w_decay, rwkv_a0, rwkv_w_iclr, rwkv_w_gate,
                       rwkv_k_k, rwkv_k_a, rwkv_r_k, rwkv_ln_w, rwkv_ln_b)
    y_a = o_a @ w_branch[:MLA_W]
    y_b = o_b @ w_branch[MLA_W:MLA_W + GLA_W]
    y_c = o_c @ w_branch[MLA_W + GLA_W:]
    gates = jax.nn.sigmoid(gate_logits).reshape(B, S, N_BRANCH, D_MODEL)
    merged = gates[:, :, 0] * y_a + gates[:, :, 1] * y_b + gates[:, :, 2] * y_c
    return merged @ w_out

def _mem_attn(h, mem_n, wq, wkv, wo):
    B, S, _ = h.shape
    q = (h @ wq).reshape(B, S, MEM_HEADS, MEM_HD)
    kv = (mem_n @ wkv).reshape(B, mem_n.shape[1], 2, MEM_HEADS, MEM_HD)
    k, v = kv[:, :, 0], kv[:, :, 1]
    s = jnp.einsum('bqhd,bkhd->bhqk', q, k).astype(jnp.float32) * MEM_HD ** -0.5
    p = jax.nn.softmax(s, axis=-1).astype(v.dtype)
    return jnp.einsum('bhqk,bkhd->bqhd', p, v).reshape(B, S, D_MODEL) @ wo

def second_inputs(seed: int = 0) -> dict:
    key = jax.random.key(seed)
    ks = iter(jax.random.split(key, 48))
    f32 = jnp.float32
    L = DEPTH

    def nrm(shape, fan_in, s=1.0):
        return jax.random.normal(next(ks), shape, f32) * (s * fan_in ** -0.5)

    def gain(shape):
        return 1.0 + 0.05 * jax.random.normal(next(ks), shape, f32)

    def small(shape, s):
        return s * jax.random.normal(next(ks), shape, f32)

    def unif(shape, lo, hi):
        return jax.random.uniform(next(ks), shape, f32, lo, hi)

    x = jax.random.normal(next(ks), (BATCH, SEQ, D_MODEL), f32)
    mem = jax.random.normal(next(ks), (BATCH, N_MEM, D_MODEL), f32)
    start = jax.random.randint(next(ks), (BATCH, 1), 0, 4096, dtype=jnp.int32)
    positions = start + jnp.arange(SEQ, dtype=jnp.int32)[None, :]
    return {
        "x": x,
        "mem": mem,
        "positions": positions,
        "norm_g": gain((L, 8, D_MODEL)),
        "w_ffn_in": nrm((L, 2, D_MODEL, 2 * D_FF), D_MODEL),
        "w_ffn_out": nrm((L, 2, D_FF, D_MODEL), D_FF),
        "w_in": nrm((L, D_MODEL, D_IN_2), D_MODEL),
        "mla_q_norm": gain((L, MLA_Q_RANK)),
        "mla_w_uq": nrm((L, MLA_Q_RANK, MLA_HEADS * (MLA_NOPE + MLA_ROPE)), MLA_Q_RANK),
        "mla_kv_norm": gain((L, MLA_KV_RANK)),
        "mla_w_ukv": nrm((L, MLA_KV_RANK, MLA_HEADS * (MLA_NOPE + MLA_V)), MLA_KV_RANK),
        "gla_w_alpha": nrm((L, GLA_GATE_RANK, GLA_HEADS * GLA_DK), GLA_GATE_RANK),
        "gla_b_alpha": unif((L, GLA_HEADS * GLA_DK), -1.0, 4.0),
        "gla_norm": gain((L, GLA_DV)),
        "rwkv_mu": unif((L, RWKV_COLS), 0.0, 1.0),
        "rwkv_w0": unif((L, RWKV_W), -4.0, 0.0),
        "rwkv_w_decay": nrm((L, RWKV_DECAY_RANK, RWKV_W), RWKV_DECAY_RANK, 0.5),
        "rwkv_a0": small((L, RWKV_W), 0.1),
        "rwkv_w_iclr": nrm((L, RWKV_ICLR_RANK, RWKV_W), RWKV_ICLR_RANK, 0.5),
        "rwkv_w_gate": nrm((L, RWKV_GATE_RANK, RWKV_W), RWKV_GATE_RANK),
        "rwkv_k_k": 0.85 + small((L, RWKV_W), 0.1),
        "rwkv_k_a": gain((L, RWKV_W)),
        "rwkv_r_k": small((L, RWKV_W), 0.1),
        "rwkv_ln_w": gain((L, RWKV_W)),
        "rwkv_ln_b": small((L, RWKV_W), 0.02),
        "w_branch": nrm((L, BRANCH_W, D_MODEL), RWKV_W),
        "w_out": nrm((L, D_MODEL, D_MODEL), D_MODEL),
        "mem_norm": gain((L, D_MODEL)),
        "mem_wq": nrm((L, D_MODEL, D_MODEL), D_MODEL),
        "mem_wkv": nrm((L, D_MODEL, 2 * D_MODEL), D_MODEL),
        "mem_wo": nrm((L, D_MODEL, D_MODEL), D_MODEL),
    }

def second_block(x, mem, positions, norm_g, w_ffn_in, w_ffn_out, w_in,
              mla_q_norm, mla_w_uq, mla_kv_norm, mla_w_ukv,
              gla_w_alpha, gla_b_alpha, gla_norm,
              rwkv_mu, rwkv_w0, rwkv_w_decay, rwkv_a0, rwkv_w_iclr, rwkv_w_gate,
              rwkv_k_k, rwkv_k_a, rwkv_r_k, rwkv_ln_w, rwkv_ln_b,
              w_branch, w_out, mem_norm, mem_wq, mem_wkv, mem_wo):
    inv_freq = ROPE_THETA ** (-jnp.arange(0, MLA_ROPE, 2, dtype=jnp.float32) / MLA_ROPE)
    ang = positions.astype(jnp.float32)[..., None] * inv_freq
    cos, sin = jnp.cos(ang), jnp.sin(ang)
    for l in range(DEPTH):
        ng = norm_g[l]
        x = x + 0.5 * _rmsnorm(_swiglu(_rmsnorm(x, ng[0]), w_ffn_in[l, 0], w_ffn_out[l, 0]), ng[1])
        y = _mixer_block(_rmsnorm(x, ng[2]), cos, sin, w_in[l],
                         mla_q_norm[l], mla_w_uq[l], mla_kv_norm[l], mla_w_ukv[l],
                         gla_w_alpha[l], gla_b_alpha[l], gla_norm[l],
                         rwkv_mu[l], rwkv_w0[l], rwkv_w_decay[l], rwkv_a0[l], rwkv_w_iclr[l],
                         rwkv_w_gate[l], rwkv_k_k[l], rwkv_k_a[l], rwkv_r_k[l],
                         rwkv_ln_w[l], rwkv_ln_b[l], w_branch[l], w_out[l])
        x = x + _rmsnorm(y, ng[3])
        y = _mem_attn(_rmsnorm(x, ng[4]), _rmsnorm(mem, mem_norm[l]), mem_wq[l], mem_wkv[l], mem_wo[l])
        x = x + _rmsnorm(y, ng[5])
        x = x + 0.5 * _rmsnorm(_swiglu(_rmsnorm(x, ng[6]), w_ffn_in[l, 1], w_ffn_out[l, 1]), ng[7])
    return x


def setup_inputs(seed=0):
    out = dict(first_inputs(seed))
    for name, value in second_inputs(seed + 1).items():
        if name != "x":
            out[name + "_2"] = value
    return out


def reference(
    x, ffn1_w_gate, ffn1_w_up, ffn1_w_down, ffn2_w_gate, ffn2_w_up, ffn2_w_down, w_in, pool_w,
    pool_scale, conv_w, rpb, w_out, ln_g, ln_b, mem_2, positions_2, norm_g_2, w_ffn_in_2,
    w_ffn_out_2, w_in_2, mla_q_norm_2, mla_w_uq_2, mla_kv_norm_2, mla_w_ukv_2, gla_w_alpha_2,
    gla_b_alpha_2, gla_norm_2, rwkv_mu_2, rwkv_w0_2, rwkv_w_decay_2, rwkv_a0_2, rwkv_w_iclr_2,
    rwkv_w_gate_2, rwkv_k_k_2, rwkv_k_a_2, rwkv_r_k_2, rwkv_ln_w_2, rwkv_ln_b_2, w_branch_2,
    w_out_2, mem_norm_2, mem_wq_2, mem_wkv_2, mem_wo_2,
):
    x = first_block(
        x, ffn1_w_gate, ffn1_w_up, ffn1_w_down, ffn2_w_gate, ffn2_w_up, ffn2_w_down, w_in,
        pool_w, pool_scale, conv_w, rpb, w_out, ln_g, ln_b,
    )
    return second_block(
        x, mem_2, positions_2, norm_g_2, w_ffn_in_2, w_ffn_out_2, w_in_2, mla_q_norm_2,
        mla_w_uq_2, mla_kv_norm_2, mla_w_ukv_2, gla_w_alpha_2, gla_b_alpha_2, gla_norm_2,
        rwkv_mu_2, rwkv_w0_2, rwkv_w_decay_2, rwkv_a0_2, rwkv_w_iclr_2, rwkv_w_gate_2,
        rwkv_k_k_2, rwkv_k_a_2, rwkv_r_k_2, rwkv_ln_w_2, rwkv_ln_b_2, w_branch_2, w_out_2,
        mem_norm_2, mem_wq_2, mem_wkv_2, mem_wo_2,
    )


_drawn_inputs = setup_inputs


def setup_inputs(seed=0):
    import zlib

    import numpy as np

    out = dict(_drawn_inputs(seed))
    spreads = {}
    factors = {'rpb': 8.0,
     'mla_q_norm_2': 5.692,
     'mla_kv_norm_2': 3.02,
     'rwkv_ln_b_2': 14.844,
     'gla_norm_2': 3.162,
     'rwkv_w_decay_2': 4.166,
     'rwkv_a0_2': 3.785,
     'rwkv_k_k_2': 3.687,
     'rwkv_k_a_2': 3.153,
     'rwkv_ln_w_2': 3.571}
    for name, (base, spread) in spreads.items():
        noise = np.random.default_rng([zlib.crc32(name.encode()), seed]).standard_normal(out[name].shape)
        drawn = base * np.exp(spread * noise) if base else spread * noise
        out[name] = __import__('jax').numpy.asarray(drawn.astype(out[name].dtype))
    for name, factor in factors.items():
        out[name] = (out[name] * factor).astype(out[name].dtype)
    return out
```

```python
from contextlib import ExitStack

import concourse.bass as bass
import numpy as np
from concourse import mybir

F32 = mybir.dt.float32
I32 = mybir.dt.int32
ACT = mybir.ActivationFunctionType
ALU = mybir.AluOpType
AX = mybir.AxisListType

P = 128
D = 1024
S = 256
LAYERS = 2
KD = D // P
F = 2816
PAIRS = F // (2 * P)
ALPHA = (2.0 * LAYERS) ** 0.25
LN_EPS = 1e-5
RMS_EPS = 1e-6
NEG = -1e30

SLOTS = 6
SLOT = 2048
HALF = S // P
AHEAD = 4

GRID = 64
NA_HEADS = 8
NA_COLS = 16
RPB_R, RPB_C = 15, 31
STRIPS = 6
POOL_PAD = 8
POOL_W = (2, 4, 8, 16)

V1 = {"ln_g": 0, "ln_b": 24, "pool_scale": 48, "conv_w": 50}
V1_N = 56


DECAY_SCALE = float(np.exp(-0.5))
GLA_GATE = 16.0
CHUNK = 64
CHUNKS = S // CHUNK
MIX_SLOTS = 28
Q_IN, Q_BRANCH, Q_OUT, Q_KV, Q_Q, Q_O = 0, 28, 40, 44, 52, 56
MLA_HEADS, MEM_HEADS, GLA_HEADS, RWKV_HEADS = 8, 4, 4, 8
PI = float(np.pi)
ROUND = 1.5 * 2.0 ** 23
TURN1 = 6.28125
TURN2 = float(np.float32(np.floor((2 * np.pi - TURN1) * 2.0 ** 21) / 2.0 ** 21))
TURN3 = float(np.float32(2 * np.pi - TURN1 - TURN2))
V2, V2_N = {}, 0
for _name, _width in (("norm_g", 64), ("mem_norm", 8), ("mla_q_norm", 2), ("mla_kv_norm", 1), ("gla_b_alpha", 2),
                      ("gla_norm", 1), ("rwkv_mu", 15), ("rwkv_w0", 4), ("rwkv_a0", 4), ("rwkv_k_k", 4),
                      ("rwkv_k_a", 4), ("rwkv_r_k", 4), ("rwkv_ln_w", 4), ("rwkv_ln_b", 4)):
    V2[_name] = V2_N
    V2_N += _width


def const_layout():
    at, n = {}, 0
    for name, width in (("ident", P), ("na_mask", GRID), ("pool_cnt", 2 * S), ("causal", 2 * S), ("eps_ln", 1),
                        ("eps_rms", 1), ("eps_gn", 1), ("eps_0", 1), ("inv_freq", 1),
                        ("rope_sign", 1), ("halves", P), ("gla_full", 256), ("gla_half", P), ("strict", P),
                        ("lower", CHUNK), ("eye2", CHUNK)):
        at[name] = n
        n += width
    return at, n


CONST, CONST_N = const_layout()


def constants():
    c = np.zeros((P, CONST_N), np.float32)

    def put(name, a):
        a = np.asarray(a, np.float32)
        c[:a.shape[0], CONST[name]:CONST[name] + a.shape[1]] = a

    put("ident", np.eye(P))
    col = np.arange(GRID)
    start = np.clip(col - NA_COLS // 2, 0, GRID - NA_COLS)
    ok = (col[None] >= start[:, None]) & (col[None] < start[:, None] + NA_COLS)
    put("na_mask", np.tile(np.where(ok, -NEG, NEG), (2, 1))[:, ::-1])
    t = np.arange(S)
    cnt = np.zeros((P, 2, S))
    for g, w in enumerate(POOL_W):
        n = np.clip(t - w // 2 + w, 0, S) - np.clip(t - w // 2, 0, S)
        cnt[64 * (g % 2):64 * (g % 2) + 64, g // 2] = 1.0 / n
    put("pool_cnt", cnt.reshape(P, -1))
    q = np.arange(P)[:, None, None] + P * np.arange(2)[None, :, None]
    put("causal", np.where(np.arange(S)[None, None] <= q, 0.0, NEG).reshape(P, -1))
    put("eps_ln", np.full((P, 1), LN_EPS))
    put("eps_rms", np.full((P, 1), RMS_EPS))
    put("eps_gn", np.full((P, 1), 64e-5))
    freq = np.float32(10000.0) ** (-np.arange(0, 32, 2, dtype=np.float32) / np.float32(32))
    put("inv_freq", np.tile(freq.astype(np.float32), 8)[:, None])
    put("rope_sign", np.tile(np.repeat([-1.0, 1.0], 16), 4)[:, None])
    put("halves", np.kron(np.eye(2), np.ones((64, 64))))
    j, i = np.arange(P)[:, None], np.arange(CHUNK)[None]
    late = (j <= i + 64).astype(np.float32)
    put("gla_full", np.concatenate([late, np.ones((P, 2 * CHUNK)), late], axis=1))
    put("gla_half", np.tile(j[:64] <= i, (1, 2)))
    j = j % 64
    put("strict", np.concatenate([j < i, j <= i], axis=1))
    put("lower", j > i)
    put("eye2", j == i)
    return c


class Ring:

    def __init__(self):
        self.turn, self.uses, self.free = 0, [0] * SLOTS, [None] * SLOTS

    def take(self, slot, freed):
        n, before = self.uses[slot], self.free[slot]
        self.uses[slot] += 1
        self.free[slot] = freed
        return slot, n, before

    def next(self, freed):
        slot = self.turn
        self.turn = (slot + 1) % SLOTS
        return self.take(slot, freed)


def plan(stages):
    ring, out, n_lin = Ring(), [], 0
    for kind, k in stages:
        if kind == "ffn":
            base = k * 2 * PAIRS
            out.append([[ring.take(3 * (p % 2) + i, ("gu", base + 2 * p + 2) if i < 2 else
                                   ("h_used", AHEAD + base + 2 * p + 2)) for i in range(3)] for p in range(PAIRS)])
            ring.turn = 3
        else:
            out.append([ring.next(("lin", n_lin + i + 1)) for i in range(k)])
            n_lin += k
    return out


def build(nc, a, out, stop=None):
    ctx = ExitStack()
    with ctx:
        def sb(name, shape, dt=F32):
            return ctx.enter_context(nc.sbuf_tensor(name, shape, dt))

        sems = {}

        def sem(name):
            if name not in sems:
                sems[name] = ctx.enter_context(nc.semaphore(name))
            return sems[name]

        WHOLE = ("arrived", "all_arrived", "cleared", "loaded", "stored", "bias_here", "pool_w_cleared", "rope_set", "angle_ready",
                 "rope_sin", "rope_step", "ones_set")
        arrived, all_arrived, cleared, loaded, stored, bias_here, sem_pw, rope_set, _, _, _, ones_set = [sem(n) for n in WHOLE]

        ps = ctx.enter_context(nc.psum_tensor("ps", [P, 8, 512], F32))
        ring = sb("ring", [P, SLOTS, SLOT])
        const = sb("const", [P, CONST_N])
        ones = sb("ones", [P, S])
        xT = sb("xT", [P, KD, S])
        zT = sb("zT", [P, KD, S])
        yT = sb("yT", [P, KD, S])
        sq = sb("sq", [P, KD, S])
        std = sb("std", [P, S])
        rstd = sb("rstd", [P, S])
        work = sb("work", [P, 16 * S])
        silu = work[:, 0:2 * S].rearrange("p (a t) -> p a t", a=2)
        hid = work[:, 2 * S:6 * S].rearrange("p (a t) -> p a t", a=4)
        att_p = work[:, 6 * S:12 * S].rearrange("p (b c t) -> p b c t", b=3, c=2)
        att_pT = work[:, 12 * S:16 * S].rearrange("p (b c t) -> p b c t", b=2, c=2)
        vec1 = sb("vec1", [P, V1_N])
        att_max = sb("att_max", [P, 3, 2])
        att_sum = sb("att_sum", [P, 3, 2])
        att_rec = sb("att_rec", [P, 3, 2])
        pos_i = sb("pos_i", [P, S], I32)
        arena = sb("arena", [P, 25232])

        def view(lo, *shape, of=None):
            n = int(np.prod(shape))
            v = (arena if of is None else of)[:, lo:lo + n]
            names = "abcd"[:len(shape)]
            return v if len(shape) == 1 else v.rearrange(
                f"p ({' '.join(names)}) -> p {' '.join(names)}", **dict(zip(names[1:], shape[1:])))

        def cst(name, n, p=P):
            return const[0:p, CONST[name]:CONST[name] + n]

        ident = cst("ident", P)

        pool_in = view(0, 2, S + 2 * POOL_PAD)
        sum2 = view(544, 2, S + 2 * POOL_PAD)
        sum4 = view(1088, 2, S + 2 * POOL_PAD)
        sum8 = view(1632, 1, S + 2 * POOL_PAD)
        sum16 = view(1904, 1, S + 2 * POOL_PAD)
        pooled = view(2176, 2, S)
        gate_b = view(2688, 2, S)
        gate_c = view(3200, 2, S)
        conv_h = view(3712, 2, S)
        conv_z = view(4224, 2, S + 2)
        conv_y = view(4740, 2, S)
        na_q = view(5252, 4, S)
        na_k = view(6276, 4, S)
        na_v = view(7300, 2, 512)
        na_bias = view(8324, NA_HEADS, STRIPS * GRID)
        mix1 = view(11396, KD, S)
        pool_w = view(13444, 2, P)
        na_raw = view(16384, LAYERS, NA_HEADS * STRIPS, GRID)

        hT = view(0, KD, S)
        gates = view(2048, 3 * KD, S)
        branch_in = view(8192, 3, 4, S)
        o_mla, o_gla, o_rwkv = (branch_in[:, b] for b in range(3))
        w_uq = view(11264, 2, 1024)
        w_ukv = view(13312, 1024)
        w_alpha = view(14336, S)
        w_lora = view(14592, 512)
        w_rgate = view(15104, 2, 512)
        vec2 = view(16128, V2_N)
        cos = view(16256, S)
        sin = view(16512, S)
        c_q = view(16768, 2, S)
        c_kv = view(17280, 1, S)
        k_rope = view(17536, 2, S)
        gla_q = view(18048, 2, S)
        gla_k = view(18560, 2, S)
        gla_v = view(19072, 2, 512)
        gla_g = view(20096, 4, S)
        rz = view(21120, 15, S + 1)
        mla_qn = yT[:, 0:4, :]
        mla_qr = yT[:, 4:8, :]
        mla_kn = sq[:, 0:4, :]
        mla_v = sq[:, 4:8, :].rearrange("p (c k) t -> p c (k t)", c=2)
        gla_b = view(0, 2, S + 1, of=work)
        gla_ek = view(514, 2, 640, of=work)
        gla_kd = view(1794, 2, 640, of=work)
        gla_mid = view(3074, 2, 2, CHUNKS, of=work)
        gla_qd = view(3090, 2, S, of=work)
        gla_at = yT[:, :, :].rearrange("p k t -> p (k t)")[:, 0:4 * 384].rearrange("p (h c) -> p h c", h=4)
        gla_tmp = zT[:, 0:6, :].rearrange("p (a c) t -> p a c t", a=3)
        rw_pr = view(11264, 4, 2, S)
        rw_kh = view(13312, 4, S)
        rw_bh = view(16768, 4, S)
        rw_a = view(17792, 4, S)
        rw_kk = view(18816, 4, S)
        rw_L = view(19840, 4, S + 1)
        rw_edge = view(20868, 3, 4, CHUNKS)
        rw_c = view(0, 4, 4, CHUNK, of=work)
        rw_g = view(1024, 2, 4, 2 * CHUNK, of=work)
        rw_tok = view(2048, 3, 4, CHUNK, of=work)
        rw_st = view(24976, 4, CHUNK)
        rw_pow = yT[:, 0:4, :].rearrange("p a (k t) -> p a k t", k=4)
        rw_t = yT[:, 4:6, :].rearrange("p a (k t) -> p a k t", k=4)
        rw_x = yT[:, 6, :].rearrange("p (k t) -> p k t", k=4)
        rw_u = yT[:, 7, :].rearrange("p (k t) -> p k t", k=4)
        rw_tmp = zT[:, 4:8, :]
        mem_n = view(16768, KD, S)
        mem_q = view(2048, KD, S)
        mem_k = view(4096, KD, S)
        mem_v = view(6144, 2, D)
        mem_o = view(8192, KD, S)

        stages1 = [("ffn", 0), ("lin", 10), ("lin", 4), ("ffn", 1)]
        ffn1_at, win_at, wout_at, ffn2_at = plan(stages1)
        stages2 = [("ffn", 0), ("lin", 28), ("lin", 12), ("lin", 4), ("lin", 8), ("lin", 4), ("lin", 4), ("ffn", 1)]
        f1_at, win2_at, branch_at, wout2_at, wkv_at, wq_at, wo_at, f2_at = plan(stages2)
        HERE = [sem(f"weights_here{s}") for s in range(SLOTS)]

        def slot(s, k=KD):
            return ring[:, s, :].rearrange("p (k c) -> p k c", k=k)

        block = ctx.enter_context(nc.Block())

        def freed_sem(kind):
            return sem({"gu": "gate_up_ready", "h_used": "hidden_used", "lin": "linear_ready"}[kind])

        def sp_load(sp, place, src, dst):
            s, _, before = place
            if before is not None:
                sp.wait_ge(freed_sem(before[0]), before[1])
            sp.dma_start(dst, src).then_inc(HERE[s], 16)

        def sp_ffn(sp, places, w_gate, w_up, w_down):
            def pair(p, at, it, step):
                for i, w in enumerate((w_gate, w_up, w_down)):
                    s, _, before = at[i]
                    if before is not None:
                        sp.wait_ge(freed_sem(before[0]), before[1] + it * step)
                    k = KD if i < 2 else 2
                    sp.dma_start(slot(s, k), w(p * 2 * P + it * (4 * P))).then_inc(HERE[s], 16)

            for p in (0, 1):
                pair(p, places[p], 0, 0)
            with sp.Fori(0, (PAIRS - 3) // 2) as it:
                for p in (2, 3):
                    pair(p, places[p], it, 4)
            pair(PAIRS - 1, places[PAIRS - 1], 0, 0)

        def sp_linear(sp, places, views):
            for place, (src, dst) in zip(places, views):
                sp_load(sp, place, src, dst(place[0]))

        def here(pe, place, it=0):
            pe.wait_ge(HERE[place[0]], 16 * (place[1] + 1) + it * 16)

        def pe_ffn(pe, n, places, src):
            base = n * 2 * PAIRS

            def gate_up(p, at, it=0):
                here(pe, at[0], it)
                here(pe, at[1], it)
                for jj in range(2):
                    bank = 4 + 2 * (p % 2) + jj
                    pe.wait_ge(sem("hidden_ready"), base + 2 * p + jj + 1 + it * 4)
                    for i in range(2):
                        w = slot(at[i][0])
                        for k in range(KD):
                            mm = nc.tensor.matmul(ps[:, bank, i * S:(i + 1) * S], w[:, k, jj * P:(jj + 1) * P],
                                                  src[:, k, :], start=(k == 0), stop=(k == KD - 1))
                    mm.then_inc(sem("gate_up_ready"), 1)

            def down(p, at, it=0, last=False):
                here(pe, at[2], it)
                w = slot(at[2][0], 2)
                for jj in range(2):
                    pe.wait_ge(sem("hidden_ready"), AHEAD + base + 2 * p + jj + 1 + it * 4)
                    for i in range(KD):
                        first = p == 0 and jj == 0
                        mm = nc.tensor.matmul(ps[:, i // 2, (i % 2) * S:(i % 2 + 1) * S],
                                              w[:, jj, i * P:(i + 1) * P], hid[:, (2 * p + jj) % 4, :],
                                              start=first and i % 2 == 0, stop=last and jj == 1,
                                              skip_group_check=True)
                    mm.then_inc(sem("hidden_used"), 1)

            gate_up(0, places[0])
            gate_up(1, places[1])
            down(0, places[0])
            with pe.Fori(0, (PAIRS - 3) // 2) as it:
                for p in (2, 3):
                    gate_up(p, places[p], it)
                    down(p - 1, places[p - 1], it)
            gate_up(PAIRS - 1, places[PAIRS - 1])
            down(PAIRS - 2, places[PAIRS - 2])
            down(PAIRS - 1, places[PAIRS - 1], last=True)

        def pe_linear(pe, q0, places, groups):
            for i, (place, group) in enumerate(zip(places, groups)):
                q = q0 + i
                here(pe, place)
                if q >= 4:
                    pe.wait_ge(sem("linear_taken"), q - 3)
                for o, lhsT, rhs, first, last in group(4 + q % 4, place[0]):
                    mm = nc.tensor.matmul(o, lhsT, rhs, start=first, stop=last)
                mm.then_inc(sem("linear_ready"), 1)

        def features(src):
            def group(bank, s):
                for c in range(2):
                    for k in range(KD):
                        yield (ps[:, bank, c * S:(c + 1) * S], slot(s)[:, k, c * P:(c + 1) * P], src[:, k, :],
                               k == 0, k == KD - 1)
            return group

        def tokens(src):
            def group(bank, s):
                for t in range(HALF):
                    for k in range(KD):
                        yield (ps[:, bank, t * S:(t + 1) * S], src[:, k, t * P:(t + 1) * P], slot(s)[:, k, :],
                               k == 0, k == KD - 1)
            return group

        def pe_sum(pe, tag, src, tiles, bank):
            for k in range(tiles):
                mm = nc.tensor.matmul(ps[:, bank, 0:S], ones[:, 0:P], src[:, k, :], start=(k == 0), stop=(k == tiles - 1))
            mm.then_inc(sem(tag), 1)

        def pe_ln(pe, n):
            pe.wait_ge(sem("ln_in"), n + 1)
            pe_sum(pe, "ln_mean", zT, KD, 0)
            pe.wait_ge(sem("ln_square"), n + 1)
            pe_sum(pe, "ln_var", sq, KD, 1)

        def pe_attention(pe, tag, heads, scores, values):
            for i in range(heads + 2):
                if i < heads:
                    if i >= 2:
                        pe.wait_ge(sem(tag + "_biased"), i - 1)
                    for t in range(HALF):
                        pieces = scores(i, t)
                        for m, (q, k) in enumerate(pieces):
                            mm = nc.tensor.matmul(ps[:, 4 + i % 2, t * S:(t + 1) * S], q, k,
                                                  start=(m == 0), stop=(m == len(pieces) - 1))
                    mm.then_inc(sem(tag + "_scores"), 1)
                h = i - 1
                if 0 <= h < heads:
                    pe.wait_ge(sem(tag + "_probs"), h + 1)
                    if h >= 2:
                        pe.wait_ge(sem(tag + "_turned"), h - 1)
                    for t in range(HALF):
                        for kt in range(HALF):
                            mm = nc.tensor.transpose(ps[:, 6 + h % 2, kt * S + t * P:kt * S + (t + 1) * P],
                                                     att_p[:, h % 3, t, kt * P:(kt + 1) * P], ident)
                    mm.then_inc(sem(tag + "_transposed"), 1)
                h = i - 2
                if 0 <= h < heads:
                    pe.wait_ge(sem(tag + "_turned"), h + 1)
                    if h >= 2:
                        pe.wait_ge(sem(tag + "_out"), h - 1)
                    for o, v in values(h):
                        for kt in range(HALF):
                            mm = nc.tensor.matmul(o, v(kt), att_pT[:, h % 2, kt, :], start=(kt == 0),
                                                  stop=(kt == HALF - 1))
                    mm.then_inc(sem(tag + "_values"), 1)

        def act_ffn(act, n):
            base = n * 2 * PAIRS

            def one(j, it=0):
                act.wait_ge(sem("gate_up_ready"), base + j + 1 + it * 4)
                act.wait_ge(sem("hidden_ready"), AHEAD + base + j - 1 + it * 4)
                nc.scalar.activation(silu[:, j % 2, :], ps[:, 4 + j % 4, 0:S], ACT.Silu).then_inc(sem("silu_ready"), 1)

            for j in (0, 1):
                one(j)
            with act.Fori(0, (PAIRS - 1) // 2) as it:
                for j in range(2, 6):
                    one(j, it)

        def act_take_y(act, n, scale):
            act.wait_ge(sem("hidden_used"), AHEAD + (n + 1) * 2 * PAIRS)
            for b in range(4):
                nc.scalar.activation(yT[:, 2 * b:2 * b + 2, :], ps[:, b, :].rearrange("p (c t) -> p c t", c=2),
                                     ACT.Copy, scale=scale).then_inc(sem("y_taken"), 1)

        def act_linear(act, q0, dests):
            for i, dst in enumerate(dests):
                act.wait_ge(sem("linear_ready"), q0 + i + 1)
                src = ps[:, 4 + (q0 + i) % 4, :].rearrange("p (c t) -> p c t", c=2)
                nc.scalar.activation(dst, src, ACT.Copy).then_inc(sem("linear_taken"), 1)

        def act_ln(act, n):
            act.wait_ge(sem("ln_centred"), n + 1)
            nc.scalar.activation(sq[:, :, :], zT[:, :, :], ACT.Square).then_inc(sem("ln_square"), 1)
            act.wait_ge(sem("ln_var"), n + 1)
            nc.scalar.activation(std[:, :], ps[:, 1, 0:S], ACT.Sqrt, bias=cst("eps_ln", 1),
                                 scale=1.0 / D).then_inc(sem("ln_std"), 1)

        def act_attention(act, tag, heads, outs):
            for i in range(heads + 2):
                if i < heads:
                    act.wait_ge(sem(tag + "_biased"), i + 1)
                    for t in range(HALF):
                        e = nc.scalar.activation(att_p[:, i % 3, t, :], att_p[:, i % 3, t, :], ACT.Exp,
                                                 bias=att_max[:, i % 3, t:t + 1], accum_out=att_sum[:, i % 3, t:t + 1])
                        e.then_inc(sem(tag + "_exp"), 1)
                h = i - 1
                if 0 <= h < heads:
                    act.wait_ge(sem(tag + "_transposed"), h + 1)
                    if h >= 2:
                        act.wait_ge(sem(tag + "_values"), h - 1)
                    nc.scalar.activation(att_pT[:, h % 2, :, :], ps[:, 6 + h % 2, :].rearrange("p (c t) -> p c t", c=2),
                                         ACT.Copy).then_inc(sem(tag + "_turned"), 1)
                h = i - 2
                if 0 <= h < heads:
                    act.wait_ge(sem(tag + "_values"), h + 1)
                    dst, src = outs(h)
                    nc.scalar.activation(dst, src, ACT.Copy).then_inc(sem(tag + "_out"), 1)

        class Steps:

            def __init__(self, eng, name):
                self.eng, self.sem, self.n = eng, sem(name), 0

            def link(self, ins):
                self.n += 1
                ins.then_inc(self.sem, 1)
                self.eng.wait_ge(self.sem, self.n)

        def dve_ffn(dve, n):
            base = n * 2 * PAIRS

            def one(j, it=0):
                dve.wait_ge(sem("silu_ready"), base + j + 1 + it * 4)
                dve.wait_ge(sem("hidden_used"), base + j + 1 + it * 4)
                nc.vector.tensor_tensor(hid[:, j % 4, :], silu[:, j % 2, :], ps[:, 4 + j % 4, S:2 * S],
                                        ALU.mult).then_inc(sem("hidden_ready"), 1)

            for j in (0, 1):
                one(j)
            with dve.Fori(0, (PAIRS - 1) // 2) as it:
                for j in range(2, 6):
                    one(j, it)

        def over_tiles(v, n=KD):
            return v.rearrange("p (o t) -> p o t", o=1).broadcast_to([P, n, S])

        def dve_ln(dve, steps, n, ready):
            ready()
            nc.vector.scalar_tensor_tensor(zT[:, :, :], xT[:, :, :], ALPHA, yT[:, :, :], ALU.mult,
                                           ALU.add).then_inc(sem("ln_in"), 1)
            dve.wait_ge(sem("ln_mean"), n + 1)
            dve.wait_ge(sem("ln_in"), n + 1)
            nc.vector.tensor_scalar(rstd[:, :], ps[:, 0, 0:S], 1.0 / D, None, ALU.mult).then_inc(sem("ln_mu"), 1)
            dve.wait_ge(sem("ln_mu"), n + 1)
            nc.vector.tensor_tensor(zT[:, :, :], zT[:, :, :], over_tiles(rstd[:, :]),
                                    ALU.subtract).then_inc(sem("ln_centred"), 1)
            dve.wait_ge(sem("ln_std"), n + 1)
            dve.wait_ge(sem("ln_centred"), n + 1)
            steps.link(nc.vector.reciprocal(rstd[:, :], std[:, :]))
            steps.link(nc.vector.tensor_tensor(zT[:, :, :], zT[:, :, :], over_tiles(rstd[:, :]), ALU.mult))
            g, b = V1["ln_g"] + n * KD, V1["ln_b"] + n * KD
            for k in range(KD):
                nc.vector.tensor_scalar(xT[:, k, :], zT[:, k, :], vec1[:, g + k:g + k + 1], vec1[:, b + k:b + k + 1],
                                        ALU.mult, ALU.add).then_inc(sem("x_ready"), 1)

        def dve_attention(dve, steps, tag, heads, scale, bias):
            for i in range(heads + 1):
                if i < heads:
                    dve.wait_ge(sem(tag + "_scores"), i + 1)
                    if i >= 3:
                        dve.wait_ge(sem(tag + "_transposed"), i - 2)
                    for t in range(HALF):
                        s = ps[:, 4 + i % 2, t * S:(t + 1) * S]
                        b = bias(i, t)
                        if b is None:
                            ins = nc.vector.tensor_scalar(att_p[:, i % 3, t, :], s, scale, None, ALU.mult)
                        else:
                            ins = nc.vector.scalar_tensor_tensor(att_p[:, i % 3, t, :], s, scale, b, ALU.mult, ALU.add)
                    steps.link(ins)
                    nc.vector.tensor_reduce(att_max[:, i % 3, :], att_p[:, i % 3, :, :], AX.X, ALU.max,
                                            negate=True).then_inc(sem(tag + "_biased"), 1)
                h = i - 1
                if 0 <= h < heads:
                    dve.wait_ge(sem(tag + "_exp"), HALF * (h + 1))
                    steps.link(nc.vector.reciprocal(att_rec[:, h % 3, :], att_sum[:, h % 3, :]))
                    for t in range(HALF):
                        ins = nc.vector.tensor_scalar(att_p[:, h % 3, t, :], att_p[:, h % 3, t, :],
                                                      att_rec[:, h % 3, t:t + 1], None, ALU.mult)
                    ins.then_inc(sem(tag + "_probs"), 1)

        def col2(name, i=0, p=P, lo=0):
            return vec2[lo:lo + p, V2[name] + i:V2[name] + i + 1]

        def bank2(b, p=P, lo=0):
            return ps[lo:lo + p, b:b + 2, :].rearrange("p b (c t) -> p (b c) t", c=2)

        def pe_rms(pe, n):
            pe.wait_ge(sem("rms_square"), n + 1)
            pe_sum(pe, "rms_sum", sq, KD, 0)

        def act_rms(act, n, src, ready):
            ready()
            nc.scalar.activation(sq[:, :, :], src, ACT.Square).then_inc(sem("rms_square"), 1)

        def act_rms_std(act, n):
            act.wait_ge(sem("rms_sum"), n + 1)
            nc.scalar.activation(std[:, :], ps[:, 0, 0:S], ACT.Sqrt, bias=cst("eps_rms", 1),
                                 scale=1.0 / D).then_inc(sem("rms_std"), 1)

        def dve_rms(dve, steps, n, src, gain, dst, done):
            dve.wait_ge(sem("rms_std"), n + 1)
            steps.link(nc.vector.reciprocal(rstd[:, :], std[:, :]))
            for k in range(KD):
                nc.vector.scalar_tensor_tensor(dst[:, k, :], src[:, k, :], gain(k), rstd[:, :], ALU.mult,
                                               ALU.mult).then_inc(sem(done), 1)

        def dve_residual(dve, steps, n, gain, scale):
            dve.wait_ge(sem("rms_std"), n + 1)
            steps.link(nc.vector.reciprocal(rstd[:, :], std[:, :]))
            for k in range(KD):
                ins = nc.vector.scalar_tensor_tensor(zT[:, k, :], yT[:, k, :], gain(k), rstd[:, :], ALU.mult, ALU.mult)
            steps.link(ins)
            nc.vector.scalar_tensor_tensor(xT[:, :, :], zT[:, :, :], scale, xT[:, :, :], ALU.mult,
                                           ALU.add).then_inc(sem("x_ready"), 1)

        ROPE = 32

        def pe_mla(pe):
            pe.wait_ge(sem("mla_square"), 2)
            for i, tiles in enumerate(((0, 1), (2,))):
                for t in tiles:
                    mm = nc.tensor.matmul(ps[:, 0, i * S:(i + 1) * S], ones[:, 0:P], sq[:, t, :], start=(t == tiles[0]),
                                          stop=(t == tiles[-1]))
            mm.then_inc(sem("mla_sum"), 1)
            pe.wait_ge(sem("mla_normed"), 3)
            pe.wait_ge(sem("small_here"), 8 * 16)
            for t in range(8):
                for k in range(2):
                    mm = nc.tensor.matmul(ps[:, t // 2, (t % 2) * S:(t % 2 + 1) * S], w_uq[:, k, t * P:(t + 1) * P],
                                          c_q[:, k, :], start=(k == 0), stop=(k == 1))
            mm.then_inc(sem("mla_q_ready"), 1)
            pe.wait_ge(sem("linear_taken"), MIX_SLOTS)
            for t in range(4):
                nc.tensor.matmul(ps[:, 4 + t // 2, (t % 2) * S:(t % 2 + 1) * S], w_ukv[:, t * P:(t + 1) * P], c_kv[:, 0, :],
                                 start=True, stop=True)
            for t in range(HALF):
                mm = nc.tensor.matmul(ps[:, 6 + t, :], c_kv[:, 0, t * P:(t + 1) * P], w_ukv[:, 512:1024], start=True,
                                      stop=True)
            mm.then_inc(sem("mla_kv_ready"), 1)
            pe.wait_ge(sem("mla_taken"), 4)
            pe.wait_ge(sem("mla_rope"), 2)

            def scores(h, t):
                o, r = 64 * (h % 2), ROPE * (h % 4)
                return [(mla_qn[o:o + 64, h // 2, t * P:(t + 1) * P], mla_kn[o:o + 64, h // 2, :]),
                        (mla_qr[r:r + ROPE, h // 4, t * P:(t + 1) * P], k_rope[r:r + ROPE, 0, :])]

            def values(h):
                o = 64 * (h % 2)
                return [(ps[o:o + 64, h % 2, 0:S], lambda kt: mla_v[:, kt, h * 64:(h + 1) * 64])]

            pe_attention(pe, "mla", MLA_HEADS, scores, values)

        def act_mla(act):
            act.wait_ge(sem("linear_taken"), 2)
            act.wait_ge(sem("narrow_taken"), 1)
            nc.scalar.activation(sq[:, 0:2, :], c_q[:, :, :], ACT.Square).then_inc(sem("mla_square"), 1)
            nc.scalar.activation(sq[:, 2:3, :], c_kv[:, :, :], ACT.Square).then_inc(sem("mla_square"), 1)
            act.wait_ge(sem("mla_sum"), 1)
            nc.scalar.activation(zT[:, 0, :], ps[:, 0, 0:S], ACT.Sqrt, bias=cst("eps_rms", 1), scale=1.0 / 256)\
                .then_inc(sem("mla_std"), 1)
            nc.scalar.activation(zT[:, 1, :], ps[:, 0, S:2 * S], ACT.Sqrt, bias=cst("eps_rms", 1), scale=1.0 / P)\
                .then_inc(sem("mla_std"), 1)
            act.wait_ge(sem("mla_q_ready"), 1)
            nc.scalar.activation(mla_qr[:, :, :], bank2(2), ACT.Copy).then_inc(sem("mla_taken"), 1)
            nc.scalar.activation(mla_qn[:, :, :], bank2(0), ACT.Copy).then_inc(sem("mla_taken"), 1)
            act.wait_ge(sem("mla_kv_ready"), 1)
            nc.scalar.activation(mla_kn[:, :, :], bank2(4), ACT.Copy).then_inc(sem("mla_taken"), 1)
            nc.scalar.activation(mla_v[:, :, :], ps[:, 6:8, :], ACT.Copy).then_inc(sem("mla_taken"), 1)

            def outs(h):
                o = 64 * (h % 2)
                return o_mla[o:o + 64, h // 2, :], ps[o:o + 64, h % 2, 0:S]

            act_attention(act, "mla", MLA_HEADS, outs)

        def dve_mla(dve, steps):
            dve.wait_ge(sem("mla_std"), 2)
            steps.link(nc.vector.reciprocal(zT[:, 2:4, :], zT[:, 0:2, :]))
            for k in range(2):
                nc.vector.scalar_tensor_tensor(c_q[:, k, :], c_q[:, k, :], col2("mla_q_norm", k), zT[:, 2, :], ALU.mult,
                                               ALU.mult).then_inc(sem("mla_normed"), 1)
            nc.vector.scalar_tensor_tensor(c_kv[:, 0, :], c_kv[:, 0, :], col2("mla_kv_norm"), zT[:, 3, :], ALU.mult,
                                           ALU.mult).then_inc(sem("mla_normed"), 1)
            cos1, sin1 = cos.rearrange("p (o t) -> p o t", o=1), sin.rearrange("p (o t) -> p o t", o=1)
            dve.wait_ge(sem("linear_taken"), 3)
            for buf, n, ready in ((k_rope, 1, None), (mla_qr, 2, sem("mla_taken"))):
                if ready is not None:
                    dve.wait_ge(ready, 1)
                nc.vector.tensor_tensor(buf[:, 0:n, :], buf[:, 0:n, :], cos1.broadcast_to([P, n, S]), ALU.mult)
                steps.link(nc.vector.tensor_tensor(buf[:, n:2 * n, :], buf[:, n:2 * n, :], sin1.broadcast_to([P, n, S]),
                                                   ALU.mult))
                nc.vector.tensor_tensor(buf[:, 0:n, :], buf[:, 0:n, :], buf[:, n:2 * n, :], ALU.add)\
                    .then_inc(sem("mla_rope"), 1)
            causal = cst("causal", 2 * S)
            dve_attention(dve, steps, "mla", MLA_HEADS, 96 ** -0.5, lambda h, t: causal[:, t * S:(t + 1) * S])

        GLA_AT = [CHUNK * i * (i + 1) // 2 for i in range(CHUNKS)]
        PIECES = [(1, 0, P, 0), (2, 0, P, 64), (3, 0, P, 128), (3, 1, P, 192), (0, 0, 64, 256), (2, 1, 64, 320)]

        def pe_gla(pe):
            for c in range(2):
                mm = nc.tensor.matmul(ps[:, 2, c * S:(c + 1) * S], w_alpha[0:16, c * P:(c + 1) * P], rz[0:16, 14, 1:],
                                      start=True, stop=True)
            mm.then_inc(sem("gla_logit"), 1)
            pe.wait_ge(sem("gla_scaled"), 1)
            for h in range(GLA_HEADS):
                o, c = 64 * (h % 2), h // 2
                for i, jt, n, col in PIECES:
                    k0 = GLA_AT[i] + jt * P
                    mm = nc.tensor.matmul(ps[0:n, 4 + h, col:col + CHUNK], gla_kd[o:o + 64, c, k0:k0 + n],
                                          gla_qd[o:o + 64, c, i * CHUNK:(i + 1) * CHUNK], start=True, stop=True)
                mm.then_inc(sem("gla_scores"), 1)
            pe.wait_ge(sem("mla_out"), MLA_HEADS)
            for h in range(GLA_HEADS):
                pe.wait_ge(sem("gla_masked"), h + 1)
                for i in range(CHUNKS):
                    mine = [x for x in PIECES if x[0] == i]
                    for m, (_, jt, n, col) in enumerate(mine):
                        out_at = (h % 2) * S + i * CHUNK
                        mm = nc.tensor.matmul(ps[:, h // 2, out_at:out_at + CHUNK], gla_v[0:n, jt, h * P:(h + 1) * P],
                                              gla_at[0:n, h, col:col + CHUNK], start=(m == 0), stop=(m == len(mine) - 1))
            mm.then_inc(sem("gla_out"), 1)
            pe.wait_ge(sem("gla_square"), 1)
            for h in range(GLA_HEADS):
                mm = nc.tensor.matmul(ps[:, 2 + h // 2, (h % 2) * S:(h % 2 + 1) * S], ones[:, 0:P], sq[:, h, :],
                                      start=True, stop=True)
            mm.then_inc(sem("gla_sum"), 1)

        def act_gla(act):
            act.wait_ge(sem("gla_logit"), 1)
            for c in range(2):
                ins = nc.scalar.activation(gla_tmp[:, 0, c, :], ps[:, 2, c * S:(c + 1) * S], ACT.Abs, bias=col2("gla_b_alpha", c))
            ins.then_inc(sem("gla_log"), 1)
            act.wait_ge(sem("gla_log"), 1)
            nc.scalar.activation(gla_tmp[:, 0, :, :], gla_tmp[:, 0, :, :], ACT.Exp, scale=-1.0).then_inc(sem("gla_log"), 1)
            act.wait_ge(sem("gla_log"), 2)
            nc.scalar.activation(gla_tmp[:, 0, :, :], gla_tmp[:, 0, :, :], ACT.Ln, bias=1.0).then_inc(sem("gla_log"), 1)
            act.wait_ge(sem("gla_summed"), 1)
            for i in range(CHUNKS):
                for c in range(2):
                    n = CHUNK * (i + 1)
                    nc.scalar.activation(gla_ek[:, c, GLA_AT[i]:GLA_AT[i] + n], gla_b[:, c, 1:n + 1], ACT.Exp,
                                         bias=gla_mid[:, 0, c, i:i + 1], scale=-1.0 / GLA_GATE)
                    ins = nc.scalar.activation(gla_qd[:, c, i * CHUNK:(i + 1) * CHUNK],
                                               gla_b[:, c, i * CHUNK + 1:(i + 1) * CHUNK + 1], ACT.Exp,
                                               bias=gla_mid[:, 1, c, i:i + 1], scale=1.0 / GLA_GATE)
            ins.then_inc(sem("gla_decay"), 1)
            act.wait_ge(sem("gla_out"), 1)
            nc.scalar.activation(sq[:, 0:4, :], bank2(0), ACT.Square).then_inc(sem("gla_square"), 1)
            act.wait_ge(sem("gla_sum"), 1)
            nc.scalar.activation(zT[:, 0:4, :], bank2(2), ACT.Sqrt, bias=cst("eps_rms", 1), scale=1.0 / P)\
                .then_inc(sem("gla_std"), 1)

        def dve_gla(dve, steps):
            dve.wait_ge(sem("gla_log"), 1)
            steps.link(nc.vector.memset(gla_b[:, :, 0:1], 0.0))
            for c in range(2):
                ins = nc.vector.tensor_scalar(gla_tmp[:, 1, c, :], ps[:, 2, c * S:(c + 1) * S], col2("gla_b_alpha", c), 0.0,
                                              ALU.add, ALU.min)
            steps.link(ins)
            dve.wait_ge(sem("gla_log"), 3)
            steps.link(nc.vector.tensor_tensor(gla_tmp[:, 1, :, :], gla_tmp[:, 1, :, :], gla_tmp[:, 0, :, :], ALU.subtract))
            for c in range(2):
                ins = nc.vector.tensor_tensor_scan(gla_b[:, c, 1:], ones[:, :], gla_tmp[:, 1, c, :], 0.0, ALU.mult, ALU.add)
            steps.link(ins)
            mid = gla_b[:, :, 1:].rearrange("p c (n t) -> p c n t", t=CHUNK)[:, :, :, CHUNK // 2 - 1]
            nc.vector.tensor_scalar(gla_mid[:, 0, :, :], mid, 1.0 / GLA_GATE, None, ALU.mult)
            nc.vector.tensor_scalar(gla_mid[:, 1, :, :], mid, -1.0 / GLA_GATE, None, ALU.mult).then_inc(sem("gla_summed"), 1)
            dve.wait_ge(sem("gla_decay"), 1)
            for i in range(CHUNKS):
                n, at = CHUNK * (i + 1), GLA_AT[i]
                nc.vector.tensor_tensor(gla_kd[:, :, at:at + n], gla_ek[:, :, at:at + n], gla_k[:, :, 0:n], ALU.mult)
            nc.vector.scalar_tensor_tensor(gla_qd[:, :, :], gla_q[:, :, :], 64 ** -0.5, gla_qd[:, :, :], ALU.mult, ALU.mult)\
                .then_inc(sem("gla_scaled"), 1)
            for h in range(GLA_HEADS):
                dve.wait_ge(sem("gla_scores"), h + 1)
                nc.vector.tensor_tensor(gla_at[:, h, 0:256], ps[:, 4 + h, 0:256], cst("gla_full", 256), ALU.mult)
                nc.vector.tensor_tensor(gla_at[0:64, h, 256:384], ps[0:64, 4 + h, 256:384], cst("gla_half", P, 64), ALU.mult)\
                    .then_inc(sem("gla_masked"), 1)
            dve.wait_ge(sem("gla_std"), 1)
            steps.link(nc.vector.reciprocal(zT[:, 0:4, :], zT[:, 0:4, :]))
            for b in range(2):
                ins = nc.vector.scalar_tensor_tensor(o_gla[:, 2 * b:2 * b + 2, :],
                                                     ps[:, b, :].rearrange("p (c t) -> p c t", c=2), col2("gla_norm"),
                                                     zT[:, 2 * b:2 * b + 2, :], ALU.mult, ALU.mult)
            steps.link(ins)
            nc.vector.tensor_tensor(o_gla, o_gla, gla_g[:, :, :], ALU.mult).then_inc(sem("gla_done"), 1)

        POWERS = 5
        W = CHUNK

        HEADS = [(t, slice(64 * half, 64 * half + 64)) for t in range(4) for half in range(2)]

        def pe_halves(pe, src, bank):
            for t in range(4):
                mm = nc.tensor.matmul(ps[:, bank + t // 2, (t % 2) * S:(t % 2 + 1) * S], cst("halves", P), src(t), start=True,
                                      stop=True)
            return mm

        def four(bank):
            return ps[:, bank, 0:4 * W].rearrange("p (t c) -> p t c", t=4)

        def pe_rwkv(pe):
            pe.wait_ge(sem("rw_tanh"), 1)
            for t in range(4):
                nc.tensor.matmul(ps[:, 4 + t // 2, (t % 2) * S:(t % 2 + 1) * S], w_lora[0:64, t * P:(t + 1) * P],
                                 rz[0:64, 12, 1:], start=True, stop=True)
            for t in range(4):
                mm = nc.tensor.matmul(ps[:, 6 + t // 2, (t % 2) * S:(t % 2 + 1) * S], w_lora[64:P, t * P:(t + 1) * P],
                                      rz[64:P, 12, 1:], start=True, stop=True)
            mm.then_inc(sem("rw_logits"), 1)
            pe.wait_ge(sem("rw_square"), 1)
            pe.wait_ge(sem("gla_done"), 1)
            pe_halves(pe, lambda t: sq[:, t, :], 0).then_inc(sem("rw_norm"), 1)
            pe.wait_ge(sem("rw_scaled"), 1)
            pe.wait_ge(sem("rw_sigmoid"), 8)
            for n in range(CHUNKS):
                at = slice(n * W, (n + 1) * W)
                pe.wait_ge(sem("rw_chunk_in"), n + 1)
                if n:
                    pe.wait_ge(sem("rw_y_taken"), n)
                    pe.wait_ge(sem("rw_state"), n + 1)
                for t, o in HEADS:
                    for b, src in enumerate((rz[o, 8 + t, 1 + n * W:1 + (n + 1) * W], rw_c[o, 2, t, :], rw_c[o, 3, t, :])):
                        col = (b % 2) * 4 * W + t * W
                        mm = nc.tensor.matmul(ps[o, b // 2, col:col + W], src, const[o, CONST["ident"] + o.start:
                                              CONST["ident"] + o.stop], start=True, stop=True)
                mm.then_inc(sem("rw_turned"), 1)
                for t, o in HEADS:
                    for bank, keys in ((4, rw_bh), (6, rw_kh)):
                        nc.tensor.matmul(ps[o, bank, 2 * W * t:2 * W * (t + 1)].rearrange("p (a c) -> p a c", a=2),
                                         keys[o, t, at], rw_pr[o, t, :, at], start=True, stop=True)
                    mm = nc.tensor.matmul(ps[o, 3, t * W:(t + 1) * W], rw_pr[o, t, 0, at], rw_bh[o, t, at], start=True,
                                          stop=True)
                mm.then_inc(sem("rw_grams"), 1)
                pe.wait_ge(sem("rw_grams_taken"), n + 1)

                def power(i, t, o):
                    return (rw_pow[o, 2 * (i % 2), t, :],
                            rw_pow[o, 2 * (i % 2) + 1, t, :] if i else rw_g[o, 0, t, 0:W])

                pe.wait_ge(sem("rw_tok"), 2 * (n + 1))
                for i in range(1, POWERS + 1):
                    if i > 1:
                        pe.wait_ge(sem("rw_pow_a"), POWERS * n + i - 1)
                        pe.wait_ge(sem("rw_pow_b"), (POWERS - 1) * n + i - 1)
                    for t, o in HEADS:
                        a, b = power(i - 1, t, o)
                        mm = nc.tensor.matmul(ps[o, 0, t * W:(t + 1) * W], b, a, start=True, stop=True)
                        if i < POWERS:
                            mm = nc.tensor.matmul(ps[o, 1, t * W:(t + 1) * W], a, b, start=True, stop=True)
                    mm.then_inc(sem("rw_pow"), 1)
                    pe.wait_ge(sem("rw_pow_a"), POWERS * n + i)
                    if i > 1:
                        pe.wait_ge(sem("rw_inv"), POWERS * n + i - 1)
                    for t, o in HEADS:
                        mm = nc.tensor.matmul(ps[o, 2, t * W:(t + 1) * W], power(i, t, o)[0], rw_t[o, (i - 1) % 2, t, :],
                                              start=True, stop=True)
                    mm.then_inc(sem("rw_inv_mm"), 1)
                for t, o in HEADS:
                    x = ps[o, 3, t * W:(t + 1) * W]
                    nc.tensor.matmul(x, rw_c[o, 0, t, :], rw_st[o, t, :], start=True, stop=False)
                    mm = nc.tensor.matmul(x, rw_g[o, 1, t, 0:W], rw_tok[o, 0, t, :], start=False, stop=True)
                mm.then_inc(sem("rw_x"), 1)
                pe.wait_ge(sem("rw_x_taken"), n + 1)
                pe.wait_ge(sem("rw_inv"), POWERS * (n + 1))
                for t, o in HEADS:
                    mm = nc.tensor.matmul(ps[o, 0, t * W:(t + 1) * W], rw_t[o, POWERS % 2, t, :], rw_x[o, t, :], start=True,
                                          stop=True)
                mm.then_inc(sem("rw_u"), 1)
                pe.wait_ge(sem("rw_u_taken"), n + 1)
                for t, o in HEADS:
                    y, state = ps[o, 4, t * W:(t + 1) * W], ps[o, 5, t * W:(t + 1) * W]
                    nc.tensor.matmul(y, rw_st[o, t, :], rw_c[o, 1, t, :], start=True, stop=False)
                    nc.tensor.matmul(y, rw_u[o, t, :], rw_g[o, 0, t, W:2 * W], start=False, stop=False)
                    nc.tensor.matmul(y, rw_tok[o, 0, t, :], rw_g[o, 1, t, W:2 * W], start=False, stop=True)
                    nc.tensor.matmul(state, rw_tok[o, 2, t, :], rw_u[o, t, :], start=True, stop=False)
                    mm = nc.tensor.matmul(state, rw_tok[o, 1, t, :], rw_tok[o, 0, t, :], start=False, stop=True)
                mm.then_inc(sem("rw_y"), 1)
            pe.wait_ge(sem("rw_y_taken"), CHUNKS)
            pe_halves(pe, lambda t: rw_kk[:, t, :], 0).then_inc(sem("gn_mean"), 1)
            pe.wait_ge(sem("rw_bonus"), 1)
            pe.wait_ge(sem("rw_state"), CHUNKS + 1)
            pe_halves(pe, lambda t: rw_bh[:, t, :], 4).then_inc(sem("rw_bonus_sum"), 1)
            for t in range(4):
                o = ps[:, 6 + t // 2, (t % 2) * S:(t % 2 + 1) * S]
                nc.tensor.matmul(o, w_rgate[:, 0, t * P:(t + 1) * P], rz[:, 13, 1:], start=True, stop=False)
                mm = nc.tensor.matmul(o, w_rgate[32:64, 1, t * P:(t + 1) * P], rz[32:64, 14, 1:], start=False, stop=True)
            mm.then_inc(sem("rw_gate"), 1)
            pe.wait_ge(sem("gn_square"), 1)
            pe_halves(pe, lambda t: sq[:, t, :], 2).then_inc(sem("gn_var"), 1)

        def act_rwkv(act):
            act.wait_ge(sem("rw_mixed"), 15)
            nc.scalar.activation(rz[0:64, 12, 1:], rz[0:64, 12, 1:], ACT.Tanh).then_inc(sem("rw_tanh"), 1)
            nc.scalar.activation(rz[:, 13, 1:], rz[:, 13, 1:], ACT.Sigmoid).then_inc(sem("rw_gate_in"), 1)
            nc.scalar.activation(rz[32:64, 14, 1:], rz[32:64, 14, 1:], ACT.Sigmoid).then_inc(sem("rw_gate_in"), 1)
            act.wait_ge(sem("rw_logits"), 1)
            for t in range(4):
                nc.scalar.activation(rw_tmp[:, t, :], ps[:, 4 + t // 2, (t % 2) * S:(t % 2 + 1) * S], ACT.Sigmoid,
                                     bias=col2("rwkv_w0", t)).then_inc(sem("rw_sigmoid"), 1)
            for t in range(4):
                nc.scalar.activation(rw_a[:, t, :], ps[:, 6 + t // 2, (t % 2) * S:(t % 2 + 1) * S], ACT.Sigmoid,
                                     bias=col2("rwkv_a0", t)).then_inc(sem("rw_sigmoid"), 1)
            act.wait_ge(sem("rw_kk_raw"), 4)
            nc.scalar.activation(sq[:, 0:4, :], rw_kk[:, :, :], ACT.Square).then_inc(sem("rw_square"), 1)
            act.wait_ge(sem("rw_norm"), 1)
            nc.scalar.activation(zT[:, 0:4, :], bank2(0), ACT.Sqrt, bias=cst("eps_0", 1)).then_inc(sem("rw_norm_root"), 1)
            act.wait_ge(sem("rw_logs"), 1)
            nc.scalar.activation(rw_pr[:, :, 1, :], rw_bh[:, :, :], ACT.Exp, scale=-DECAY_SCALE)
            nc.scalar.activation(rw_kh[:, :, :], rw_bh[:, :, :], ACT.Exp, scale=DECAY_SCALE)
            nc.scalar.activation(rw_edge[:, 0:2], rw_edge[:, 0:2], ACT.Exp, scale=-DECAY_SCALE)
            nc.scalar.activation(rw_pr[:, :, 0, :], rw_pr[:, :, 0, :], ACT.Exp, scale=-DECAY_SCALE)\
                .then_inc(sem("rw_decay"), 1)
            for n in range(CHUNKS):
                act.wait_ge(sem("rw_turned"), n + 1)
                nc.scalar.activation(rw_tok[:, 0:2], ps[:, 0, :].rearrange("p (b t c) -> p b t c", b=2, t=4), ACT.Copy)\
                    .then_inc(sem("rw_tok"), 1)
                nc.scalar.activation(rw_tok[:, 2], four(1), ACT.Copy).then_inc(sem("rw_tok"), 1)
                for i in range(1, POWERS + 1):
                    act.wait_ge(sem("rw_pow"), POWERS * n + i)
                    nc.scalar.activation(rw_pow[:, 2 * (i % 2)], four(0), ACT.Copy).then_inc(sem("rw_pow_a"), 1)
                act.wait_ge(sem("rw_x"), n + 1)
                nc.scalar.activation(rw_x, four(3), ACT.Copy).then_inc(sem("rw_x_taken"), 1)
                act.wait_ge(sem("rw_y"), n + 1)
                nc.scalar.activation(rw_kk[:, :, n * W:(n + 1) * W], four(4), ACT.Copy).then_inc(sem("rw_y_taken"), 1)
            act.wait_ge(sem("gn_centred"), 1)
            nc.scalar.activation(sq[:, 0:4, :], rw_kk[:, :, :], ACT.Square).then_inc(sem("gn_square"), 1)
            act.wait_ge(sem("gn_var"), 1)
            nc.scalar.activation(zT[:, 4:8, :], bank2(2), ACT.Sqrt, bias=cst("eps_gn", 1), scale=1.0 / 64)\
                .then_inc(sem("gn_std"), 1)

        def dve_rwkv(dve, steps):
            r, k, v = (rz[:, 4 * i:4 * i + 4, 1:] for i in range(3))
            dve.wait_ge(sem("gla_out"), 1)
            diff = view(0, 15, S, of=work)
            steps.link(nc.vector.tensor_tensor(diff, rz[:, :, 0:S], rz[:, :, 1:], ALU.subtract))
            for t in range(15):
                lo, n = (0, P) if t < 14 else (32, 32)
                nc.vector.scalar_tensor_tensor(rz[lo:lo + n, t, 1:], diff[lo:lo + n, t, :], col2("rwkv_mu", t, n, lo),
                                               rz[lo:lo + n, t, 1:], ALU.mult, ALU.add).then_inc(sem("rw_mixed"), 1)
            dve.wait_ge(sem("rw_mixed"), 15)
            for t in range(4):
                nc.vector.tensor_scalar(rw_kk[:, t, :], k[:, t, :], col2("rwkv_k_k", t), None, ALU.mult)\
                    .then_inc(sem("rw_kk_raw"), 1)
            steps.link(nc.vector.memset(rw_L[:, :, 0:1], 0.0))
            steps.link(nc.vector.memset(rw_st[:, :, :], 0.0))
            dve.wait_ge(sem("rw_sigmoid"), 8)
            for t in range(4):
                ins = nc.vector.tensor_tensor_scan(rw_L[:, t, 1:], ones[:, :], rw_tmp[:, t, :], 0.0, ALU.mult, ALU.add)
            steps.link(ins)
            inc = rw_L[:, :, 1:].rearrange("p c (n t) -> p c n t", t=W)
            exc = rw_L[:, :, 0:S].rearrange("p c (n t) -> p c n t", t=W)
            mid = inc[:, :, :, W // 2 - 1:W // 2]
            nc.vector.tensor_tensor(rw_bh[:, :, :].rearrange("p c (n t) -> p c n t", t=W), inc,
                                    mid.broadcast_to([P, 4, CHUNKS, W]), ALU.subtract)
            nc.vector.tensor_tensor(rw_pr[:, :, 0, :].rearrange("p c (n t) -> p c n t", t=W), exc,
                                    mid.broadcast_to([P, 4, CHUNKS, W]), ALU.subtract)
            nc.vector.tensor_tensor(rw_edge[:, 0], mid[:, :, :, 0], exc[:, :, :, 0], ALU.subtract)
            nc.vector.tensor_tensor(rw_edge[:, 1], inc[:, :, :, W - 1], mid[:, :, :, 0], ALU.subtract)\
                .then_inc(sem("rw_logs"), 1)
            dve.wait_ge(sem("rw_norm_root"), 1)
            steps.link(nc.vector.tensor_scalar(zT[:, 0:4, :], zT[:, 0:4, :], 1e-12, None, ALU.max))
            steps.link(nc.vector.reciprocal(zT[:, 0:4, :], zT[:, 0:4, :]))
            steps.link(nc.vector.tensor_tensor(rw_kk[:, :, :], rw_kk[:, :, :], zT[:, 0:4, :], ALU.mult))
            for t in range(4):
                ins = nc.vector.tensor_scalar(zT[:, t, :], rw_a[:, t, :], -1.0, col2("rwkv_k_a", t), ALU.add, ALU.mult)
            steps.link(ins)
            nc.vector.scalar_tensor_tensor(k, zT[:, 0:4, :], 1.0, k, ALU.add, ALU.mult)
            steps.link(nc.vector.scalar_tensor_tensor(rw_a[:, :, :], rw_kk[:, :, :], -1.0, rw_a[:, :, :], ALU.mult, ALU.mult))
            dve.wait_ge(sem("rw_decay"), 1)
            nc.vector.tensor_tensor(rw_pr[:, :, 0, :], rw_pr[:, :, 0, :], rw_kk[:, :, :], ALU.mult)
            nc.vector.tensor_tensor(rw_pr[:, :, 1, :], rw_pr[:, :, 1, :], r, ALU.mult)
            nc.vector.tensor_tensor(rw_edge[:, 2], rw_edge[:, 0], rw_edge[:, 1], ALU.mult)
            steps.link(nc.vector.tensor_tensor(rw_bh[:, :, :], rw_kh[:, :, :], rw_a[:, :, :], ALU.mult))
            steps.link(nc.vector.tensor_tensor(rw_kh[:, :, :], rw_kh[:, :, :], k, ALU.mult))
            nc.vector.tensor_copy(rw_tmp[:, 0, 0:1], rw_st[:, 0, 0:1]).then_inc(sem("rw_scaled"), 1)
            dve.sem_inc(sem("rw_state"), 1)

            def edge(e, n):
                return rw_edge[:, e, :, n:n + 1].broadcast_to([P, 4, W])

            for n in range(CHUNKS):
                at = slice(n * W, (n + 1) * W)
                if n:
                    dve.wait_ge(sem("rw_y"), n)
                nc.vector.tensor_tensor(rw_c[:, 0], rw_pr[:, :, 0, at], edge(0, n), ALU.mult)
                nc.vector.tensor_tensor(rw_c[:, 1], rw_pr[:, :, 1, at], edge(0, n), ALU.mult)
                nc.vector.tensor_tensor(rw_c[:, 2], rw_kh[:, :, at], edge(1, n), ALU.mult)
                nc.vector.tensor_tensor(rw_c[:, 3], rw_bh[:, :, at], edge(1, n), ALU.mult).then_inc(sem("rw_chunk_in"), 1)
                dve.wait_ge(sem("rw_grams"), n + 1)
                def blocks(name, w):
                    return cst(name, w).rearrange("p (o c) -> p o c", o=1).broadcast_to([P, 4, w])

                for b in range(2):
                    ins = nc.vector.tensor_tensor(rw_g[:, b], ps[:, 4 + 2 * b, :].rearrange("p (h c) -> p h c", h=4),
                                                  blocks("strict", 2 * W), ALU.mult)
                steps.link(ins)
                nc.vector.tensor_tensor(rw_t[:, 0], rw_g[:, 0, :, 0:W], blocks("eye2", W), ALU.add)
                nc.vector.tensor_tensor(rw_pow[:, 0], four(3), blocks("lower", W), ALU.mult)\
                    .then_inc(sem("rw_grams_taken"), 1)
                for i in range(1, POWERS + 1):
                    if i < POWERS:
                        dve.wait_ge(sem("rw_pow"), POWERS * n + i)
                        nc.vector.tensor_copy(rw_pow[:, 2 * (i % 2) + 1], four(1)).then_inc(sem("rw_pow_b"), 1)
                    dve.wait_ge(sem("rw_inv_mm"), POWERS * n + i)
                    if i > 1:
                        dve.wait_ge(sem("rw_inv"), POWERS * n + i - 1)
                    nc.vector.tensor_tensor(rw_t[:, i % 2], four(2), rw_t[:, (i - 1) % 2], ALU.add)\
                        .then_inc(sem("rw_inv"), 1)
                dve.wait_ge(sem("rw_u"), n + 1)
                nc.vector.tensor_copy(rw_u, four(0)).then_inc(sem("rw_u_taken"), 1)
                dve.wait_ge(sem("rw_y"), n + 1)
                steps.link(nc.vector.tensor_tensor(rw_st[:, :, :], rw_st[:, :, :], edge(2, n), ALU.mult))
                nc.vector.tensor_tensor(rw_st[:, :, :], rw_st[:, :, :], four(5), ALU.add).then_inc(sem("rw_state"), 1)
                dve.wait_ge(sem("rw_state"), n + 2)
            for t in range(4):
                ins = nc.vector.scalar_tensor_tensor(rw_bh[:, t, :], r[:, t, :], col2("rwkv_r_k", t), k[:, t, :], ALU.mult,
                                                     ALU.mult)
            ins.then_inc(sem("rw_bonus"), 1)
            dve.wait_ge(sem("gn_mean"), 1)
            steps.link(nc.vector.tensor_scalar(zT[:, 0:4, :], bank2(0), 1.0 / 64, None, ALU.mult))
            nc.vector.tensor_tensor(rw_kk[:, :, :], rw_kk[:, :, :], zT[:, 0:4, :], ALU.subtract).then_inc(sem("gn_centred"), 1)
            dve.wait_ge(sem("gn_std"), 1)
            steps.link(nc.vector.reciprocal(zT[:, 0:4, :], zT[:, 4:8, :]))
            steps.link(nc.vector.tensor_tensor(rw_kk[:, :, :], rw_kk[:, :, :], zT[:, 0:4, :], ALU.mult))
            for t in range(4):
                nc.vector.tensor_scalar(rw_kk[:, t, :], rw_kk[:, t, :], col2("rwkv_ln_w", t), col2("rwkv_ln_b", t), ALU.mult,
                                        ALU.add)
            dve.wait_ge(sem("rw_bonus_sum"), 1)
            steps.link(nc.vector.tensor_tensor(zT[:, 0:4, :], v, bank2(4), ALU.mult))
            steps.link(nc.vector.tensor_tensor(rw_kk[:, :, :], rw_kk[:, :, :], zT[:, 0:4, :], ALU.add))
            dve.wait_ge(sem("rw_gate"), 1)
            nc.vector.tensor_tensor(o_rwkv, rw_kk[:, :, :], bank2(6), ALU.mult).then_inc(sem("rw_done"), 1)

        def layer_end(eng, n):
            eng.drain().then_inc(arrived, 1)
            if eng is not nc.sync:
                eng.wait_ge(cleared, n)
                return
            eng.wait_ge(arrived, 5 * n)
            eng.sem_inc(all_arrived, 1)
            ids = sorted(s.num for k, s in sems.items() if k not in WHOLE)
            assert ids == list(range(ids[0], ids[-1] + 1))
            eng.sem_clear(range(ids[0], ids[-1] + 1))
            eng.drain().then_inc(cleared, 1)

        @block.tensor
        def _(pe):
            pe.wait_ge(loaded, 48)
            pe.wait_ge(ones_set, 1)
            with pe.Fori(0, LAYERS) as l:
                pe.sem_inc(sem("hidden_used"), AHEAD)
                pe_ffn(pe, 0, ffn1_at, xT)
                pe_ln(pe, 0)
                pe.wait_ge(sem("x_ready"), KD)
                groups = [features(xT)] * 8 + [tokens(xT)] * 2
                pe_linear(pe, 0, win_at, groups)
                pe.wait_ge(sem("pooled"), 1)
                pe.wait_ge(sem("pool_w_here"), 64)
                for c in range(2):
                    mm = nc.tensor.matmul(ps[:, 2, c * S:(c + 1) * S], pool_w[:, c, :], pooled[:, c, :],
                                          start=True, stop=True)
                mm.then_inc(sem("pool_ready"), 1)
                pe.wait_ge(sem("linear_taken"), 10)

                def scores(h, t):
                    o = 64 * (h % 2)
                    return [(na_q[o:o + 64, h // 2, t * P:(t + 1) * P], na_k[o:o + 64, h // 2, :])]

                def values(h):
                    o = 64 * (h % 2)
                    return [(ps[o:o + 64, h % 2, 0:S], lambda kt: na_v[:, kt, h * 64:(h + 1) * 64])]

                pe_attention(pe, "na", NA_HEADS, scores, values)
                pe.wait_ge(sem("pool_out"), 2)
                pe.wait_ge(sem("conv_out"), 1)
                pe.wait_ge(sem("na_out"), NA_HEADS)
                pe_linear(pe, 10, wout_at, [features(mix1)] * 4)
                pe_ln(pe, 1)
                pe.wait_ge(sem("x_ready"), 2 * KD)
                pe_ffn(pe, 1, ffn2_at, xT)
                pe_ln(pe, 2)
                layer_end(pe, l + 1)
            with pe.Fori(0, LAYERS) as l:
                pe.sem_inc(sem("hidden_used"), AHEAD)
                pe_rms(pe, 0)
                pe.wait_ge(sem("h_ready"), KD)
                pe_ffn(pe, 0, f1_at, hT)
                pe_rms(pe, 1)
                pe_rms(pe, 2)
                pe.wait_ge(sem("h_ready"), 2 * KD)
                pe_linear(pe, Q_IN, win2_at, [features(hT)] * 5 + [tokens(hT)] * 2 + [features(hT)] * 21)
                pe_mla(pe)
                pe_gla(pe)
                pe_rwkv(pe)
                pe.wait_ge(sem("mla_out"), MLA_HEADS)
                pe.wait_ge(sem("gla_done"), 1)
                pe.wait_ge(sem("rw_done"), 1)
                pe.wait_ge(sem("linear_taken"), MIX_SLOTS)

                def branch(b):
                    def group(bank, s):
                        for c in range(2):
                            for k in range(4):
                                yield (ps[:, bank, c * S:(c + 1) * S], slot(s)[:, k, c * P:(c + 1) * P],
                                       branch_in[:, b, k, :], k == 0, k == 3)
                    return group

                pe_linear(pe, Q_BRANCH, branch_at, [branch(b) for i in range(4) for b in range(3)])
                pe_rms(pe, 3)
                pe.wait_ge(sem("merged"), 4)
                pe_linear(pe, Q_OUT, wout2_at, [features(hT)] * 4)
                pe.wait_ge(sem("mem_ready"), KD)
                pe.wait_ge(sem("linear_taken"), Q_KV)
                pe_linear(pe, Q_KV, wkv_at, [features(mem_n)] * 4 + [tokens(mem_n)] * 4)
                pe_rms(pe, 4)
                pe_rms(pe, 5)
                pe.wait_ge(sem("h_ready"), 3 * KD)
                pe_linear(pe, Q_Q, wq_at, [features(hT)] * 4)
                pe.wait_ge(sem("linear_taken"), Q_O)

                def mem_scores(h, t):
                    return [(mem_q[:, 2 * h + c, t * P:(t + 1) * P], mem_k[:, 2 * h + c, :]) for c in range(2)]

                def mem_values(h):
                    return [(ps[:, h % 2, c * S:(c + 1) * S],
                             lambda kt, c=c: mem_v[:, kt, (2 * h + c) * P:(2 * h + c + 1) * P]) for c in range(2)]

                pe_attention(pe, "mem", MEM_HEADS, mem_scores, mem_values)
                pe.wait_ge(sem("mem_out"), MEM_HEADS)
                pe_linear(pe, Q_O, wo_at, [features(mem_o)] * 4)
                pe_rms(pe, 6)
                pe_rms(pe, 7)
                pe.wait_ge(sem("h_ready"), 4 * KD)
                pe_ffn(pe, 1, f2_at, hT)
                pe_rms(pe, 8)
                layer_end(pe, l + 1 + LAYERS)

        @block.scalar
        def _(act):
            act.wait_ge(loaded, 48)
            with act.Fori(0, LAYERS) as l:
                act_ffn(act, 0)
                act_take_y(act, 0, 0.5)
                act_ln(act, 0)
                act.wait_ge(sem("pool_pads"), 1)
                dests = [pool_in[:, :, POOL_PAD:POOL_PAD + S], gate_b[:, :, :], gate_c[:, :, :], conv_h[:, :, :],
                         na_q[:, 0:2, :], na_q[:, 2:4, :], na_k[:, 0:2, :], na_k[:, 2:4, :],
                         na_v[:, :, 0:S], na_v[:, :, S:2 * S]]
                act_linear(act, 0, dests)
                act.wait_ge(sem("pool_ready"), 1)
                for c in range(2):
                    nc.scalar.activation(mix1[:, c, :], ps[:, 2, c * S:(c + 1) * S], ACT.Copy,
                                         scale=vec1[:, V1["pool_scale"] + c:V1["pool_scale"] + c + 1])\
                        .then_inc(sem("pool_out"), 1)

                def outs(h):
                    o = 64 * (h % 2)
                    return mix1[o:o + 64, 4 + h // 2, :], ps[o:o + 64, h % 2, 0:S]

                act_attention(act, "na", NA_HEADS, outs)
                act_linear(act, 10, [yT[:, 2 * i:2 * i + 2, :] for i in range(4)])
                act_ln(act, 1)
                act_ffn(act, 1)
                act_take_y(act, 1, 0.5)
                act_ln(act, 2)
                layer_end(act, l + 1)
            act.wait_ge(sem("angle_ready"), 1)
            nc.scalar.activation(sin, sq[:, 2, :], ACT.Sin).then_inc(sem("rope_sin"), 1)
            nc.scalar.activation(sq[:, 3, :], sq[:, 2, :], ACT.Abs).then_inc(sem("rope_sin"), 1)
            act.wait_ge(sem("angle_ready"), 2)
            nc.scalar.activation(cos, sq[:, 4, :], ACT.Sin).then_inc(sem("rope_sin"), 1)
            with act.Fori(0, LAYERS) as l:
                act_rms(act, 0, xT[:, :, :], lambda: act.wait_ge(rope_set, 1))
                act_rms_std(act, 0)
                act_ffn(act, 0)
                act_take_y(act, 0, 1.0)
                act_rms(act, 1, yT[:, :, :], lambda: act.wait_ge(sem("y_taken"), 4))
                act_rms_std(act, 1)
                act_rms(act, 2, xT[:, :, :], lambda: act.wait_ge(sem("x_ready"), 1))
                act_rms_std(act, 2)
                act.wait_ge(sem("rz_cleared"), 1)
                for q in range(MIX_SLOTS):
                    act.wait_ge(sem("linear_ready"), q + 1)
                    two = ps[:, 4 + q % 4, :].rearrange("p (c t) -> p c t", c=2)
                    if q == 1:
                        nc.scalar.activation(c_kv[:, 0, :], two[:, 0, :], ACT.Copy).then_inc(sem("narrow_taken"), 1)
                        nc.scalar.activation(rz[:, 14, 1:], two[:, 1, :], ACT.Copy).then_inc(sem("linear_taken"), 1)
                    elif 5 <= q < 7:
                        c = (q - 5) * S
                        nc.scalar.activation(gla_v[:, :, c:c + S], two, ACT.Copy).then_inc(sem("linear_taken"), 1)
                    elif 7 <= q < 9:
                        c = 2 * (q - 7)
                        nc.scalar.activation(gla_g[:, c:c + 2, :], two, ACT.Silu).then_inc(sem("linear_taken"), 1)
                    elif 9 <= q < 16:
                        c = 2 * (q - 9)
                        nc.scalar.activation(rz[:, c:c + 2, 1:], two, ACT.Copy).then_inc(sem("linear_taken"), 1)
                    elif q >= 16:
                        c = 2 * (q - 16)
                        nc.scalar.activation(gates[:, c:c + 2, :], two, ACT.Sigmoid).then_inc(sem("linear_taken"), 1)
                    else:
                        dst = {0: c_q, 2: k_rope, 3: gla_q, 4: gla_k}[q]
                        nc.scalar.activation(dst[:, :, :], two, ACT.Copy).then_inc(sem("linear_taken"), 1)
                act_mla(act)
                act_gla(act)
                act_rwkv(act)
                act.wait_ge(sem("mem_here"), 16)
                act_rms(act, 3, mem_n[:, :, :], lambda: act.wait_ge(sem("rw_done"), 1))
                act_rms_std(act, 3)
                act_linear(act, Q_OUT, [yT[:, 2 * i:2 * i + 2, :] for i in range(4)])
                act_linear(act, Q_KV, [mem_k[:, 2 * i:2 * i + 2, :] for i in range(4)] +
                           [mem_v[:, :, i * S:(i + 1) * S] for i in range(4)])
                act_rms(act, 4, yT[:, :, :], lambda: act.wait_ge(sem("linear_taken"), Q_KV))
                act_rms_std(act, 4)
                act_rms(act, 5, xT[:, :, :], lambda: act.wait_ge(sem("x_ready"), 2))
                act_rms_std(act, 5)
                act_linear(act, Q_Q, [mem_q[:, 2 * i:2 * i + 2, :] for i in range(4)])

                def outs(h):
                    return mem_o[:, 2 * h:2 * h + 2, :], ps[:, h % 2, :].rearrange("p (c t) -> p c t", c=2)

                act_attention(act, "mem", MEM_HEADS, outs)
                act_linear(act, Q_O, [yT[:, 2 * i:2 * i + 2, :] for i in range(4)])
                act_rms(act, 6, yT[:, :, :], lambda: act.wait_ge(sem("linear_taken"), Q_O + 4))
                act_rms_std(act, 6)
                act_rms(act, 7, xT[:, :, :], lambda: act.wait_ge(sem("x_ready"), 3))
                act_rms_std(act, 7)
                act_ffn(act, 1)
                act_take_y(act, 1, 1.0)
                act_rms(act, 8, yT[:, :, :], lambda: act.wait_ge(sem("y_taken"), 8))
                act_rms_std(act, 8)
                layer_end(act, l + 1 + LAYERS)

        @block.vector
        def _(dve):
            dve.wait_ge(loaded, 48)
            nc.vector.memset(ones[:, :], 1.0).then_inc(ones_set, 1)
            dve.wait_ge(ones_set, 1)
            with dve.Fori(0, LAYERS) as l:
                steps = Steps(dve, "vector_step")
                dve.sem_inc(sem("hidden_ready"), AHEAD)
                nc.vector.memset(pool_in[:, :, :], 0.0).then_inc(sem("pool_pads"), 1)
                steps.link(nc.vector.memset(conv_z[:, :, :], 0.0))
                dve.wait_ge(sem("vec_here"), 16)
                dve_ffn(dve, 0)
                dve_ln(dve, steps, 0, lambda: dve.wait_ge(sem("y_taken"), 4))
                dve.wait_ge(sem("linear_taken"), 1)
                n = S + 2 * POOL_PAD
                steps.link(nc.vector.tensor_tensor(sum2[:, :, 0:n - 1], pool_in[:, :, 0:n - 1], pool_in[:, :, 1:n], ALU.add))
                steps.link(nc.vector.tensor_tensor(sum4[:, :, 0:n - 3], sum2[:, :, 0:n - 3], sum2[:, :, 2:n - 1], ALU.add))
                steps.link(nc.vector.tensor_tensor(sum8[:, :, 0:n - 7], sum4[:, 1:2, 0:n - 7], sum4[:, 1:2, 4:n - 3], ALU.add))
                steps.link(nc.vector.tensor_tensor(sum16[:, :, 0:n - 15], sum8[:, :, 0:n - 15], sum8[:, :, 8:n - 7], ALU.add))
                cnt = cst("pool_cnt", 2 * S).rearrange("p (c t) -> p c t", c=2)
                for g, (w, sums) in enumerate(zip(POOL_W, (sum2[:, 0], sum4[:, 0], sum8[:, 0], sum16[:, 0]))):
                    o = 64 * (g % 2)
                    lo = POOL_PAD - w // 2
                    ins = nc.vector.tensor_tensor(pooled[o:o + 64, g // 2, :], sums[o:o + 64, lo:lo + S],
                                                  cnt[o:o + 64, g // 2, :], ALU.mult)
                steps.link(ins)
                nc.vector.tensor_tensor(pooled[:, :, :], pooled[:, :, :], pool_in[:, :, POOL_PAD:POOL_PAD + S],
                                        ALU.subtract).then_inc(sem("pooled"), 1)
                dve.wait_ge(sem("linear_taken"), 4)
                steps.link(nc.vector.tensor_tensor(conv_z[:, :, 1:S + 1], gate_c[:, :, :], conv_h[:, :, :], ALU.mult))
                for tap in (1, 0, 2):
                    for c in range(2):
                        w = vec1[:, V1["conv_w"] + 2 * tap + c:V1["conv_w"] + 2 * tap + c + 1]
                        z = conv_z[:, c, tap:tap + S]
                        if tap == 1:
                            ins = nc.vector.tensor_scalar(conv_y[:, c, :], z, w, None, ALU.mult)
                        else:
                            ins = nc.vector.scalar_tensor_tensor(conv_y[:, c, :], z, w, conv_y[:, c, :], ALU.mult, ALU.add)
                    steps.link(ins)
                nc.vector.tensor_tensor(mix1[:, 2:4, :], gate_b[:, :, :], conv_y[:, :, :], ALU.mult)\
                    .then_inc(sem("conv_out"), 1)
                dve.wait_ge(bias_here, 16 * LAYERS * 2 * NA_HEADS)
                strips = na_bias.rearrange("p h (e k) -> p (h e) k", k=GRID)
                raw = na_raw[:, bass.ds(l, 1), :, :].rearrange("p o e k -> p (o e) k")
                mask = cst("na_mask", GRID).rearrange("p (o k) -> p o k", o=1).broadcast_to([P, NA_HEADS * STRIPS, GRID])
                steps.link(nc.vector.tensor_tensor(strips[:, :, ::-1], raw, mask, ALU.min))
                dve_attention(dve, steps, "na", NA_HEADS, 64 ** -0.5,
                              lambda h, t: na_bias[:, h, (2 - 2 * t) * GRID:(6 - 2 * t) * GRID])
                dve_ln(dve, steps, 1, lambda: dve.wait_ge(sem("linear_taken"), 14))
                dve_ffn(dve, 1)
                dve_ln(dve, steps, 2, lambda: dve.wait_ge(sem("y_taken"), 8))
                layer_end(dve, l + 1)
            steps = Steps(dve, "rope_step")
            steps.link(nc.vector.tensor_scalar(sq[:, 0, :], pos_i[:, :], cst("inv_freq", 1), None, ALU.mult))
            steps.link(nc.vector.tensor_scalar(sq[:, 1, :], sq[:, 0, :], 1.0 / (2 * PI), ROUND, ALU.mult, ALU.add))
            steps.link(nc.vector.tensor_scalar(sq[:, 1, :], sq[:, 1, :], ROUND, None, ALU.subtract))
            for part in (TURN1, TURN2, TURN3):
                steps.link(nc.vector.scalar_tensor_tensor(sq[:, 0, :], sq[:, 1, :], -part, sq[:, 0, :], ALU.mult, ALU.add))
            nc.vector.tensor_scalar(sq[:, 2, :], sq[:, 0, :], 3.1415925, -3.1415925, ALU.min, ALU.max)\
                .then_inc(sem("angle_ready"), 1)
            dve.wait_ge(sem("rope_sin"), 2)
            nc.vector.tensor_scalar(sq[:, 4, :], sq[:, 3, :], -1.0, PI / 2, ALU.mult, ALU.add)\
                .then_inc(sem("angle_ready"), 1)
            dve.wait_ge(sem("rope_sin"), 3)
            nc.vector.tensor_scalar(sin, sin, cst("rope_sign", 1), None, ALU.mult).then_inc(rope_set, 1)
            dve.wait_ge(rope_set, 1)
            with dve.Fori(0, LAYERS) as l:
                steps = Steps(dve, "mix_step")
                dve.sem_inc(sem("hidden_ready"), AHEAD)
                nc.vector.memset(rz[:, :, 0:1], 0.0).then_inc(sem("rz_cleared"), 1)
                dve.wait_ge(sem("small_here"), 8 * 16)
                dve_rms(dve, steps, 0, xT, lambda k: col2("norm_g", k), hT, "h_ready")
                dve_ffn(dve, 0)
                dve_residual(dve, steps, 1, lambda k: col2("norm_g", KD + k), 0.5)
                dve_rms(dve, steps, 2, xT, lambda k: col2("norm_g", 2 * KD + k), hT, "h_ready")
                dve_mla(dve, steps)
                dve_gla(dve, steps)
                dve_rwkv(dve, steps)
                for i in range(4):
                    for b in range(3):
                        q = Q_BRANCH + 3 * i + b
                        dve.wait_ge(sem("linear_ready"), q + 1)
                        two = ps[:, 4 + q % 4, :].rearrange("p (c t) -> p c t", c=2)
                        g = gates[:, b * KD + 2 * i:b * KD + 2 * i + 2, :]
                        dst = hT[:, 2 * i:2 * i + 2, :]
                        if b == 0:
                            nc.vector.tensor_tensor(dst, g, two, ALU.mult).then_inc(sem("linear_taken"), 1)
                            continue
                        nc.vector.tensor_tensor(zT[:, 0:2, :], g, two, ALU.mult).then_inc(sem("linear_taken"), 1)
                        dve.wait_ge(sem("linear_taken"), q + 1)
                        ins = nc.vector.tensor_tensor(dst, dst, zT[:, 0:2, :], ALU.add)
                        if b == 2:
                            ins.then_inc(sem("merged"), 1)
                            dve.wait_ge(sem("merged"), i + 1)
                        else:
                            steps.link(ins)
                dve_rms(dve, steps, 3, mem_n, lambda k: col2("mem_norm", k), mem_n, "mem_ready")
                dve_residual(dve, steps, 4, lambda k: col2("norm_g", 3 * KD + k), 1.0)
                dve_rms(dve, steps, 5, xT, lambda k: col2("norm_g", 4 * KD + k), hT, "h_ready")
                dve_attention(dve, steps, "mem", MEM_HEADS, 256 ** -0.5, lambda h, t: None)
                dve_residual(dve, steps, 6, lambda k: col2("norm_g", 5 * KD + k), 1.0)
                dve_rms(dve, steps, 7, xT, lambda k: col2("norm_g", 6 * KD + k), hT, "h_ready")
                dve_ffn(dve, 1)
                dve_residual(dve, steps, 8, lambda k: col2("norm_g", 7 * KD + k), 0.5)
                layer_end(dve, l + 1 + LAYERS)

        @block.gpsimd
        def _(pool):
            pool.memset(pool_w[:, :, :], 0.0).then_inc(sem_pw, 1)
            with pool.Fori(0, LAYERS) as l:
                layer_end(pool, l + 1)
            with pool.Fori(0, LAYERS) as l:
                layer_end(pool, l + 1 + LAYERS)

        @block.sync
        def _(sp):
            sp.dma_start(const[:, :], a["const"]).then_inc(loaded, 16)
            sp.dma_start(xT[:, :, :], a["xT"]).then_inc(loaded, 16)
            pos = a["positions"]
            sp.dma_start(pos_i[:, :], bass.AP(tensor=pos.tensor, offset=pos.offset, ap=[[0, P], [1, S]])).then_inc(loaded, 16)
            g1 = a["ffn1_w_gate"].rearrange("l (k p) f -> l p k f", p=P)
            u1 = a["ffn1_w_up"].rearrange("l (k p) f -> l p k f", p=P)
            d1 = a["ffn1_w_down"].rearrange("l (j p) d -> l p j d", p=P)
            g2 = a["ffn2_w_gate"].rearrange("l (k p) f -> l p k f", p=P)
            u2 = a["ffn2_w_up"].rearrange("l (k p) f -> l p k f", p=P)
            d2 = a["ffn2_w_down"].rearrange("l (j p) d -> l p j d", p=P)
            w_in = a["w_in"].rearrange("l (k p) f -> l p k f", p=P)
            w_out = a["w_out"].rearrange("l (k p) f -> l p k f", p=P)

            def ffn(sp, places, l, g, u, d):
                rows = d.rearrange("l p j d -> l p j d")
                sp_ffn(sp, places, lambda c: g[l][:, :, bass.ds(c, 2 * P)], lambda c: u[l][:, :, bass.ds(c, 2 * P)],
                       lambda c: d_rows(d, l, c))

            def d_rows(d, l, c):
                if isinstance(c, int):
                    return d[l][:, c // P:c // P + 2, :]
                return d[l][:, bass.ds(c // P, 2), :]

            for layer in range(LAYERS):
                for half in range(2):
                    for h in range(NA_HEADS):
                        row = a["rpb"][layer, h]
                        src = bass.AP(tensor=row.tensor, offset=row.offset + (5 - half) * RPB_C + 15 - (GRID - 1),
                                      ap=[[1, GRID], [RPB_C, STRIPS], [1, GRID]])
                        sp.dma_start(na_raw[64 * half:64 * half + 64, layer, h * STRIPS:(h + 1) * STRIPS, :],
                                     src).then_inc(bias_here, 16)
            with sp.Fori(0, LAYERS) as l:
                sp.dma_start(vec1[:, :], a["vec1"][l]).then_inc(sem("vec_here"), 16)
                sp.wait_ge(sem_pw, 1)
                for g in range(4):
                    o = 64 * (g % 2)
                    sp.dma_start(pool_w[o:o + 64, g // 2, o:o + 64], a["pool_w"][l][g]).then_inc(sem("pool_w_here"), 16)
                ffn(sp, ffn1_at, l, g1, u1, d1)
                sp_linear(sp, win_at, [(w_in[l][:, :, i * S:(i + 1) * S], slot) for i in range(10)])
                sp_linear(sp, wout_at, [(w_out[l][:, :, i * S:(i + 1) * S], slot) for i in range(4)])
                ffn(sp, ffn2_at, l, g2, u2, d2)
                layer_end(sp, l + 1)
            f_in = a["w_ffn_in_2"].rearrange("l n (k p) f -> l n p k f", p=P)
            f_out = a["w_ffn_out_2"].rearrange("l n (j p) d -> l n p j d", p=P)
            mix_in = a["w_mix"].rearrange("l (k p) f -> l p k f", p=P)
            w_branch = a["w_branch_2"].rearrange("l (b k p) f -> l b p k f", p=P, k=4)
            w_out2 = a["w_out_2"].rearrange("l (k p) f -> l p k f", p=P)
            wkv = a["mem_wkv_2"].rearrange("l (k p) f -> l p k f", p=P)
            wq = a["mem_wq_2"].rearrange("l (k p) f -> l p k f", p=P)
            wo = a["mem_wo_2"].rearrange("l (k p) f -> l p k f", p=P)

            def ffn2(places, l, n):
                sp_ffn(sp, places, lambda c: f_in[l, n][:, :, bass.ds(c, 2 * P)],
                       lambda c: f_in[l, n][:, :, bass.ds(c + F, 2 * P)], lambda c: rows2(l, n, c))

            def rows2(l, n, c):
                j = c // P
                return f_out[l, n][:, j:j + 2, :] if isinstance(c, int) else f_out[l, n][:, bass.ds(j, 2), :]

            with sp.Fori(0, LAYERS) as l:
                for dst, src in ((vec2, a["vec2"][l]), (w_uq, a["w_uq"][l].rearrange("(k p) c -> p k c", p=P)),
                                 (w_ukv, a["w_ukv"][l]), (w_alpha[0:16, :], a["gla_w_alpha_2"][l]),
                                 (w_lora[0:64, :], a["rwkv_w_decay_2"][l]), (w_lora[64:P, :], a["rwkv_w_iclr_2"][l]),
                                 (w_rgate[:, 0, :], a["rwkv_w_gate_2"][l][0:P, :]),
                                 (w_rgate[32:64, 1, :], a["rwkv_w_gate_2"][l][P:P + 32, :])):
                    sp.dma_start(dst, src).then_inc(sem("small_here"), 16)
                ffn2(f1_at, l, 0)
                sp_linear(sp, win2_at, [(mix_in[l][:, :, i * S:(i + 1) * S], slot) for i in range(MIX_SLOTS)])
                sp_linear(sp, branch_at, [(w_branch[l, b][:, :, i * S:(i + 1) * S], lambda s: slot(s)[:, 0:4, :])
                                          for i in range(4) for b in range(3)])
                sp.wait_ge(sem("rw_done"), 1)
                sp.dma_start(mem_n, a["memT"]).then_inc(sem("mem_here"), 16)
                for w, at, n in ((w_out2, wout2_at, 4), (wkv, wkv_at, 8), (wq, wq_at, 4), (wo, wo_at, 4)):
                    sp_linear(sp, at, [(w[l][:, :, i * S:(i + 1) * S], slot) for i in range(n)])
                ffn2(f2_at, l, 1)
                layer_end(sp, l + 1 + LAYERS)
            sp.dma_start(out, xT[:, :, :]).then_inc(stored, 16)
            sp.wait_ge(stored, 16)


def host_arrays(i):
    L = LAYERS
    arr = {"const": constants()}

    def fm(x):
        return np.ascontiguousarray(np.asarray(x)[0].T.reshape(KD, P, S).transpose(1, 0, 2))

    def cols(v):
        v = np.asarray(v)
        v = v.reshape(L, -1, P)
        return v.transpose(0, 2, 1)

    arr["xT"] = fm(i["x"])
    arr["memT"] = fm(i["mem_2"])
    arr["positions"] = np.ascontiguousarray(np.asarray(i["positions_2"]).reshape(S))
    w = np.asarray(i["w_in_2"])
    rope = w[:, :, 384:416]
    swapped = np.concatenate([rope[:, :, 16:], rope[:, :, :16]], axis=2)
    narrow = np.zeros((L, D, P), w.dtype)
    narrow[:, :, 0:16] = w[:, :, 1952:1968]
    narrow[:, :, 32:64] = w[:, :, 3760:3792]
    arr["w_mix"] = np.concatenate([w[:, :, 0:384], narrow] + [rope] * 4 + [swapped] * 4 + [w[:, :, 416:1952],
                                  w[:, :, 1968:3760], w[:, :, 3792:]], axis=2)
    w = np.asarray(i["mla_w_uq_2"]).reshape(L, 256, MLA_HEADS, 96)
    parts = [w[..., :64], w[..., 64:], np.concatenate([w[..., 80:], w[..., 64:80]], axis=3)]
    arr["w_uq"] = np.concatenate([p.reshape(L, 256, -1) for p in parts], axis=2)
    w = np.asarray(i["mla_w_ukv_2"]).reshape(L, P, MLA_HEADS, 2, 64)
    arr["w_ukv"] = np.ascontiguousarray(w.transpose(0, 1, 3, 2, 4).reshape(L, P, -1))
    mu = np.asarray(i["rwkv_mu_2"])
    last = np.zeros((L, P), mu.dtype)
    last[:, 32:64] = mu[:, 1792:]
    arr["vec2"] = np.ascontiguousarray(np.concatenate(
        [cols(i["norm_g_2"]), cols(i["mem_norm_2"]), cols(i["mla_q_norm_2"]), cols(i["mla_kv_norm_2"]),
         cols(i["gla_b_alpha_2"]), cols(i["gla_norm_2"]), cols(mu[:, :1792]), cols(last)] +
        [cols(i["rwkv_" + n + "_2"]) for n in ("w0", "a0", "k_k", "k_a", "r_k", "ln_w", "ln_b")], axis=2))
    arr["vec1"] = np.ascontiguousarray(np.concatenate([cols(i["ln_g"]), cols(i["ln_b"]), cols(i["pool_scale"]),
                                                       cols(i["conv_w"])], axis=2))
    arr["rpb"] = np.ascontiguousarray(np.asarray(i["rpb"])[..., ::-1])
    for n in ("ffn1_w_gate", "ffn1_w_up", "ffn1_w_down", "ffn2_w_gate", "ffn2_w_up", "ffn2_w_down", "w_in", "pool_w",
              "w_out", "w_ffn_in_2", "w_ffn_out_2", "gla_w_alpha_2", "rwkv_w_decay_2", "rwkv_w_iclr_2",
              "rwkv_w_gate_2", "w_branch_2", "w_out_2", "mem_wq_2", "mem_wkv_2", "mem_wo_2"):
        arr[n] = np.ascontiguousarray(i[n])
    return arr


def kernel(**inputs):
    import concourse.bacc as bacc
    from concourse.bass_utils import run_bass_kernel_spmd

    nc = bacc.Bacc("TRN2", target_bir_lowering=False, num_devices=1)
    arrays = host_arrays(inputs)
    aps = {n: nc.dram_tensor(f"in_{n}", v.shape, mybir.dt.from_np(v.dtype), kind="ExternalInput").ap()
           for n, v in arrays.items()}
    out = nc.dram_tensor("out_xT", (P, KD, S), F32, kind="ExternalOutput").ap()
    build(nc, aps, out)
    r = run_bass_kernel_spmd(nc, [{f"in_{n}": v for n, v in arrays.items()}], core_ids=[0])
    y = r.results[0]["out_xT"]
    return np.ascontiguousarray(y.transpose(1, 0, 2).reshape(D, S).T)[None]
```

```python
from contextlib import ExitStack

import concourse.bass as bass
import numpy as np
from concourse import mybir

F32 = mybir.dt.float32
F32R = mybir.dt.float32r
I32 = mybir.dt.int32
ACT = mybir.ActivationFunctionType
ALU = mybir.AluOpType
AX = mybir.AxisListType

P = 128
D = 1024
S = 256
LAYERS = 2
KD = D // P
F = 2816
TILES = F // P
ALPHA = (2.0 * LAYERS) ** 0.25
LN_EPS = 1e-5
RMS_EPS = 1e-6
NEG = -1e30

RAW, SPLIT = 6, 3
PIECE = 1024
FFN_PIECES = 3 * TILES
HALF = S // P

GRID = 64
NA_HEADS = 8
NA_COLS = 16
RPB_R, RPB_C = 15, 31
STRIPS = 6
POOL_PAD = 8
POOL_W = (2, 4, 8, 16)

V1 = {"ln_g": 0, "ln_b": 24, "pool_scale": 48, "conv_w": 50}
V1_N = 56


DECAY_SCALE = float(np.exp(-0.5))
GLA_GATE = 16.0
CHUNK = 64
CHUNKS = S // CHUNK
MIX_SLOTS, FIRST_SLOTS = 28, 3
FILL_GLA, FILL_RWKV, FILL_GATES = 3, 9, 16
Q_IN, Q_BRANCH, Q_OUT, Q_KV, Q_Q, Q_O = 0, 3, 7, 11, 19, 23
MLA_HEADS, MEM_HEADS, GLA_HEADS, RWKV_HEADS = 8, 4, 4, 8
PI = float(np.pi)
ROUND = 1.5 * 2.0 ** 23
TURN1 = 6.28125
TURN2 = float(np.float32(np.floor((2 * np.pi - TURN1) * 2.0 ** 21) / 2.0 ** 21))
TURN3 = float(np.float32(2 * np.pi - TURN1 - TURN2))
V2, V2_N = {}, 0
for _name, _width in (("norm_g", 64), ("mem_norm", 8), ("mla_q_norm", 2), ("mla_kv_norm", 1), ("gla_b_alpha", 2),
                      ("gla_norm", 1), ("rwkv_mu", 15), ("rwkv_w0", 4), ("rwkv_a0", 4), ("rwkv_k_k", 4),
                      ("rwkv_k_a", 4), ("rwkv_r_k", 4), ("rwkv_ln_w", 4), ("rwkv_ln_b", 4)):
    V2[_name] = V2_N
    V2_N += _width


def const_layout():
    at, n = {}, 0
    for name, width in (("ident", P), ("na_mask", GRID), ("pool_cnt", 2 * S), ("causal", 2 * S), ("eps_ln", 1), ("eps_ln4", 1),
                        ("eps_rms", 1), ("eps_gn", 1), ("eps_0", 1), ("inv_freq", 1),
                        ("rope_sign", 1), ("halves", P), ("gla_full", 256), ("gla_half", P), ("strict", P),
                        ("lower", CHUNK), ("eye2", CHUNK)):
        at[name] = n
        n += width
    return at, n


CONST, CONST_N = const_layout()


def constants():
    c = np.zeros((P, CONST_N), np.float32)

    def put(name, a):
        a = np.asarray(a, np.float32)
        c[:a.shape[0], CONST[name]:CONST[name] + a.shape[1]] = a

    put("ident", np.eye(P))
    col = np.arange(GRID)
    start = np.clip(col - NA_COLS // 2, 0, GRID - NA_COLS)
    ok = (col[None] >= start[:, None]) & (col[None] < start[:, None] + NA_COLS)
    put("na_mask", np.tile(np.where(ok, -NEG, NEG), (2, 1))[:, ::-1])
    t = np.arange(S)
    cnt = np.zeros((P, 2, S))
    for g, w in enumerate(POOL_W):
        n = np.clip(t - w // 2 + w, 0, S) - np.clip(t - w // 2, 0, S)
        cnt[64 * (g % 2):64 * (g % 2) + 64, g // 2] = 1.0 / n
    put("pool_cnt", cnt.reshape(P, -1))
    q = np.arange(P)[:, None, None] + P * np.arange(2)[None, :, None]
    put("causal", np.where(np.arange(S)[None, None] <= q, 0.0, NEG).reshape(P, -1))
    put("eps_ln", np.full((P, 1), LN_EPS))
    put("eps_ln4", np.full((P, 1), 4 * LN_EPS))
    put("eps_rms", np.full((P, 1), RMS_EPS))
    put("eps_gn", np.full((P, 1), 64e-5))
    freq = np.float32(10000.0) ** (-np.arange(0, 32, 2, dtype=np.float32) / np.float32(32))
    put("inv_freq", np.tile(freq.astype(np.float32), 8)[:, None])
    put("rope_sign", np.tile(np.repeat([-1.0, 1.0], 16), 4)[:, None])
    put("halves", np.kron(np.eye(2), np.ones((64, 64))))
    j, i = np.arange(P)[:, None], np.arange(CHUNK)[None]
    late = (j <= i + 64).astype(np.float32)
    put("gla_full", np.concatenate([late, np.ones((P, 2 * CHUNK)), late], axis=1))
    put("gla_half", np.tile(j[:64] <= i, (1, 2)))
    j = j % 64
    put("strict", np.concatenate([j < i, j <= i], axis=1))
    put("lower", j > i)
    put("eye2", j == i)
    return c


def build(nc, a, out, stop=None):
    ctx = ExitStack()
    with ctx:
        def sb(name, shape, dt=F32):
            return ctx.enter_context(nc.sbuf_tensor(name, shape, dt))

        sems = {}

        def sem(name):
            if name not in sems:
                sems[name] = ctx.enter_context(nc.semaphore(name))
            return sems[name]

        WHOLE = ("arrived", "all_arrived", "cleared", "loaded", "stored", "positions_here", "pool_w_cleared", "rope_set", "angle_ready",
                 "rope_sin", "rope_step", "ones_set")
        arrived, all_arrived, cleared, loaded, stored, positions_here, sem_pw, rope_set, _, _, _, ones_set = [sem(n) for n in WHOLE]

        ps = ctx.enter_context(nc.psum_tensor("ps", [P, 8, 512], F32))
        raw = sb("raw", [P, RAW, PIECE])
        w_hi, w_lo = (sb(n, [P, SPLIT, PIECE], F32R) for n in ("w_hi", "w_lo"))
        in_hi, in_lo = (sb(n, [P, KD, S], F32R) for n in ("in_hi", "in_lo"))
        hid_hi, hid_lo = (sb(n, [P, 2, S], F32R) for n in ("hid_hi", "hid_lo"))
        const = sb("const", [P, CONST_N])
        ones = sb("ones", [P, S])
        xT = sb("xT", [P, KD, S])
        zT = sb("zT", [P, KD, S])
        yT = sb("yT", [P, KD, S])
        sq = sb("sq", [P, KD, S])
        std = sb("std", [P, S])
        rstd = sb("rstd", [P, S])
        work = sb("work", [P, 16 * S])
        silu = work[:, 0:2 * S].rearrange("p (a t) -> p a t", a=2)
        hid = work[:, 2 * S:4 * S].rearrange("p (a t) -> p a t", a=2)
        att_p = work[:, 4 * S:12 * S].rearrange("p (b c t) -> p b c t", b=4, c=2)
        att_pT = work[:, 12 * S:16 * S].rearrange("p (b c t) -> p b c t", b=2, c=2)
        vec1 = sb("vec1", [P, V1_N])
        att_max = sb("att_max", [P, 4, 2])
        att_sum = sb("att_sum", [P, 4, 2])
        att_rec = sb("att_rec", [P, 4, 2])
        pos_i = sb("pos_i", [P, S], I32)
        arena = sb("arena", [P, 23184])

        def view(lo, *shape, of=None):
            n = int(np.prod(shape))
            v = (arena if of is None else of)[:, lo:lo + n]
            names = "abcd"[:len(shape)]
            return v if len(shape) == 1 else v.rearrange(
                f"p ({' '.join(names)}) -> p {' '.join(names)}", **dict(zip(names[1:], shape[1:])))

        def cst(name, n, p=P):
            return const[0:p, CONST[name]:CONST[name] + n]

        ident = cst("ident", P)

        pool_in = view(0, 2, S + 2 * POOL_PAD)
        sum2 = view(544, 2, S + 2 * POOL_PAD)
        sum4 = view(1088, 2, S + 2 * POOL_PAD)
        sum8 = view(1632, 1, S + 2 * POOL_PAD)
        sum16 = view(1904, 1, S + 2 * POOL_PAD)
        pooled = view(2176, 2, S)
        gate_b = view(2688, 2, S)
        gate_c = view(3200, 2, S)
        conv_h = view(3712, 2, S)
        conv_z = view(4224, 2, S + 2)
        conv_y = view(4740, 2, S)
        na_q = view(5252, 4, S)
        na_k = view(6276, 4, S)
        na_v = view(7300, 2, 512)
        na_bias = view(8324, NA_HEADS, STRIPS * GRID)
        mix1 = view(11396, KD, S)
        pool_w = view(13444, 2, P)
        na_raw = view(16384, NA_HEADS * STRIPS, GRID)

        gates = view(0, 3 * KD, S)
        branch_in = view(6144, 3, 4, S)
        two_branches = branch_in[:, 0:2].rearrange("p b k t -> p (b k) t")
        o_mla, o_gla, o_rwkv = (branch_in[:, b] for b in range(3))
        w_uq = view(9216, 2, 1024)
        w_ukv = view(11264, 1024)
        w_alpha = view(12288, S)
        w_lora = view(12544, 512)
        w_rgate = view(13056, 2, 512)
        vec2 = view(14080, V2_N)
        cos = view(14208, S)
        sin = view(14464, S)
        c_q = view(14720, 2, S)
        c_kv = view(15232, 1, S)
        k_rope = view(15488, 2, S)
        gla_q = view(16000, 2, S)
        gla_k = view(16512, 2, S)
        gla_v = view(17024, 2, 512)
        gla_g = view(18048, 4, S)
        rz = view(19072, 15, S + 1)
        mla_qn = yT[:, 0:4, :]
        mla_qr = yT[:, 4:8, :]
        mla_kn = sq[:, 0:4, :]
        mla_v = sq[:, 4:8, :].rearrange("p (c k) t -> p c (k t)", c=2)
        gla_b = view(0, 2, S + 1, of=work)
        gla_ek = view(514, 2, 640, of=work)
        gla_kd = view(1794, 2, 640, of=work)
        gla_mid = view(3074, 2, 2, CHUNKS, of=work)
        gla_qd = view(3090, 2, S, of=work)
        gla_at = yT[:, :, :].rearrange("p k t -> p (k t)")[:, 0:4 * 384].rearrange("p (h c) -> p h c", h=4)
        gla_tmp = zT[:, 0:6, :].rearrange("p (a c) t -> p a c t", a=3)
        rw_pr = view(9216, 4, 2, S)
        rw_kh = view(11264, 4, S)
        rw_bh = view(14720, 4, S)
        rw_a = view(15744, 4, S)
        rw_kk = view(16768, 4, S)
        rw_L = view(17792, 4, S + 1)
        rw_edge = view(18820, 3, 4, CHUNKS)
        rw_c2 = (view(0, 4, 4, CHUNK, of=work), zT[:, 0:4, :].rearrange("p a (k t) -> p a k t", k=4))
        rw_g = view(1024, 2, 4, 2 * CHUNK, of=work)
        rw_tok = view(2048, 3, 4, CHUNK, of=work)
        rw_st = view(22928, 4, CHUNK)
        rw_pow = yT[:, 0:4, :].rearrange("p a (k t) -> p a k t", k=4)
        rw_t = yT[:, 4:6, :].rearrange("p a (k t) -> p a k t", k=4)
        rw_x = yT[:, 6, :].rearrange("p (k t) -> p k t", k=4)
        rw_u = yT[:, 7, :].rearrange("p (k t) -> p k t", k=4)
        rw_tmp = zT[:, 4:8, :]
        mem_n = view(14720, KD, S)
        mem_q = view(0, KD, S)
        mem_k = view(2048, KD, S)
        mem_v = view(4096, 2, D)
        mem_o = view(6144, KD, S)
        merged = gates[:, 0:KD, :]
        y_mla = yT[:, :, :]
        y_gla = view(0, KD, S, of=work)

        E1_FFN1, E1_IN, E1_OUT, E1_FFN2, E1_END = np.cumsum([0, FFN_PIECES, 20, 8, FFN_PIECES]).tolist()
        E_FFN1, E_IN, E_BRANCH, E_OUT, E_KV, E_Q, E_O, E_FFN2, E_END = \
            np.cumsum([0, FFN_PIECES, 2 * MIX_SLOTS, 12, 8, 16, 8, 8, FFN_PIECES]).tolist()
        E_FILL = E_IN + 2 * FIRST_SLOTS
        C1_FFN1, C1_IN, C1_OUT, C1_FFN2 = range(0, 16, 4)
        C_FFN1, C_IN, C_AB, C_RW, C_OUT, C_KV, C_Q, C_O, C_FFN2 = 0, 4, 8, 12, 14, 18, 22, 26, 30
        HERE = [sem(f"weights_here{s}") for s in range(RAW)]

        def mem_y(c):
            return two_tiles(4 + (Q_O + c) % 4)

        block = ctx.enter_context(nc.Block())

        def sp_load(sp, e, src, it=0):
            if e >= RAW:
                sp.wait_ge(sem("split_low"), e - RAW + 1 + it * RAW)
            k = src.shape[1]
            sp.dma_start(raw[:, e % RAW, :].rearrange("p (k c) -> p k c", k=k), src).then_inc(HERE[e % RAW], 16)

        def sp_ffn(sp, e0, w_gate, w_up, w_down):
            def tile(j, it=0):
                c = j * P + it * (2 * P)
                e = e0 + max(3 * j - 1, 0)
                sp_load(sp, e, w_gate(c), it)
                sp_load(sp, e + 1, w_up(c), it)
                if j:
                    sp_load(sp, e + 2, w_down((j - 1) * P + it * (2 * P)), it)

            tile(0)
            tile(1)
            tile(2)
            tile(3)
            with sp.Fori(0, TILES // 2 - 2) as it:
                tile(4, it)
                tile(5, it)
            sp_load(sp, e0 + FFN_PIECES - 1, w_down((TILES - 1) * P))

        def sp_linear(sp, e0, srcs):
            for i, src in enumerate(srcs):
                sp_load(sp, e0 + i, src)

        def three(o, left, right, first, last, **kw):
            (lh, ll), (rh, rl) = left, right
            nc.tensor.matmul(o, lh, rh, start=first, stop=False, **kw)
            nc.tensor.matmul(o, lh, rl, start=False, stop=False, **kw)
            return nc.tensor.matmul(o, ll, rh, start=False, stop=last, **kw)

        def piece(e, k=KD):
            return [w[:, e % SPLIT, :].rearrange("p (k c) -> p k c", k=k) for w in (w_hi, w_lo)]

        def at2(pair, *index):
            return [v[index] for v in pair]

        ALL = slice(None)
        given = (in_hi, in_lo)

        def pe_ffn(pe, n, e0, chunk):
            def gate_up(j, it=0):
                for i in range(2):
                    e = e0 + max(3 * j - 1, 0) + i
                    pe.wait_ge(sem("split_low"), e + 1 + it * RAW)
                    w = piece(e)
                    for k in range(KD):
                        if j == 0 and i == 0 and k % 2 == 0:
                            pe.wait_ge(sem("in_ready"), chunk + k // 2 + 1)
                        mm = three(ps[:, 4 + j % 2, i * S:(i + 1) * S], at2(w, ALL, k, ALL), at2(given, ALL, k, ALL),
                                   k == 0, k == KD - 1)
                    mm.then_inc(sem("piece_used"), 1)

            def down(j, it=0, last=False):
                e = e0 + (FFN_PIECES - 1 if last else 3 * j + 4)
                pe.wait_ge(sem("split_low"), e + 1 + it * RAW)
                pe.wait_ge(sem("hidden_ready"), n * TILES + j + 1 + it * 2)
                w = piece(e, 1)
                for i in range(KD):
                    mm = three(ps[:, i // 2, (i % 2) * S:(i % 2 + 1) * S], at2(w, ALL, 0, slice(i * P, (i + 1) * P)),
                               at2((hid_hi, hid_lo), ALL, j % 2, ALL), j == 0 and i % 2 == 0, last, skip_group_check=True)
                mm.then_inc(sem("piece_used"), 1)

            gate_up(0)
            gate_up(1)
            down(0)
            with pe.Fori(0, TILES // 2 - 1) as it:
                for j in (2, 3):
                    gate_up(j, it)
                    down(j - 1, it)
            down(TILES - 1, last=True)

        def pe_linear(pe, q0, e0, groups, chunk, chunks=4):
            e = e0
            for i, group in enumerate(groups):
                q = q0 + i
                if q >= 4:
                    pe.wait_ge(sem("linear_taken"), q - 3)
                for products in group(4 + q % 4, e):
                    pe.wait_ge(sem("split_low"), e + 1)
                    seen = 0
                    for k, o, left, right, first, last in products:
                        if e == e0 and k // 2 == seen:
                            seen += 1
                            pe.wait_ge(sem("in_ready"), chunk + seen)
                        mm = three(o, left, right, first, last, skip_group_check=True)
                    mm.then_inc(sem("piece_used"), 1)
                    e += 1

        def features(bank, e):
            return [[(k, ps[:, bank, c * S:(c + 1) * S], at2(piece(e + c), ALL, k, ALL), at2(given, ALL, k, ALL),
                      k == 0, k == KD - 1) for k in range(KD)] for c in range(2)]

        def tokens(bank, e):
            return [[(k, ps[:, bank, t * S:(t + 1) * S], at2(given, ALL, k, slice(t * P, (t + 1) * P)),
                      at2(piece(e + c, KD // 2), ALL, k - KD // 2 * c, ALL), k == 0 and t == 0, k == KD - 1)
                     for t in range(HALF) for k in range(KD // 2 * c, KD // 2 * (c + 1))] for c in range(2)]

        def branch(tile):
            def group(bank, e):
                return [[(tile + k, ps[:, bank, c * S:(c + 1) * S], at2(piece(e, 4), ALL, k, slice(c * P, (c + 1) * P)),
                          at2(given, ALL, tile + k, ALL), k == 0, k == 3) for c in range(2) for k in range(4)]]
            return group

        def pe_branches(pe):
            pe.wait_ge(sem("filling_taken"), MIX_SLOTS - FIRST_SLOTS)
            for i in range(8):
                e = E_BRANCH + i
                if i >= 2:
                    pe.wait_ge(sem("branch_taken"), i - 1)
                if i % 4 == 0:
                    pe.wait_ge(sem("in_ready"), C_AB + 2 + i // 2)
                pe.wait_ge(sem("split_low"), e + 1)
                for _, o, left, right, first, last in branch(i // 4 * 4)(2 + i % 2, e)[0]:
                    mm = three(o, left, right, first, last)
                mm.then_inc(sem("piece_used"), 1)

        class Filling:

            def __init__(self, pe):
                self.pe, self.quarter = pe, 0

            def __call__(self, pieces):
                end = min(self.quarter + int(4 * pieces), 4 * (E_BRANCH - E_FILL))
                for x in range(self.quarter, end):
                    i, part = divmod(x, 4)
                    e = E_FILL + i
                    q, c = divmod(e - E_IN, 2)
                    if part == 0:
                        if c == 0 and q >= FIRST_SLOTS + 2:
                            self.pe.wait_ge(sem("filling_taken"), q - FIRST_SLOTS - 1)
                        self.pe.wait_ge(sem("split_low"), e + 1)
                    layout = tokens if FILL_GLA + 2 <= q < FILL_GLA + 4 else features
                    for _, o, left, right, first, last in layout(2 + q % 2, e - c)[c][2 * part:2 * part + 2]:
                        mm = three(o, left, right, first, last, skip_group_check=True)
                    if part == 3:
                        mm.then_inc(sem("piece_used"), 1)
                self.quarter = end

            def until(self, slot):
                self(2 * (slot - FIRST_SLOTS) - self.quarter / 4)

        def pe_stat(pe, bank, src, tag, chunk):
            for k in range(KD):
                if k % 2 == 0:
                    pe.wait_ge(sem(tag), chunk + k // 2 + 1)
                mm = nc.tensor.matmul(ps[:, bank, 0:S], ones[:, 0:P], src[:, k, :], start=(k == 0), stop=(k == KD - 1))
            mm.then_inc(sem("stat_sum"), 1)

        def pe_ln(pe, n, bank):
            pe_stat(pe, bank, zT, "ln_in", 4 * n)
            pe_stat(pe, bank + 1, sq, "ln_square", 4 * n)

        def two_tiles(bank):
            return ps[:, bank, :].rearrange("p (c t) -> p c t", c=2)

        def pe_attention(pe, tag, heads, scores, values, fill=lambda n: None):
            for i in range(heads + 3):
                if i < heads:
                    if i >= 2:
                        pe.wait_ge(sem(tag + "_biased"), i - 1)
                    for t in range(HALF):
                        pieces = scores(i, t)
                        for m, (q, k) in enumerate(pieces):
                            mm = nc.tensor.matmul(ps[:, 4 + i % 2, t * S:(t + 1) * S], q, k,
                                                  start=(m == 0), stop=(m == len(pieces) - 1))
                    mm.then_inc(sem(tag + "_scores"), 1)
                fill(1)
                h = i - 2
                if 0 <= h < heads:
                    pe.wait_ge(sem(tag + "_probs"), h + 1)
                    if h >= 2:
                        pe.wait_ge(sem(tag + "_turned"), h - 1)
                    for t in range(HALF):
                        for kt in range(HALF):
                            mm = nc.tensor.transpose(ps[:, 6 + h % 2, kt * S + t * P:kt * S + (t + 1) * P],
                                                     att_p[:, h % 4, t, kt * P:(kt + 1) * P], ident)
                    mm.then_inc(sem(tag + "_transposed"), 1)
                h = i - 3
                if 0 <= h < heads:
                    pe.wait_ge(sem(tag + "_turned"), h + 1)
                    if h >= 2:
                        pe.wait_ge(sem(tag + "_out"), h - 1)
                    for o, v in values(h):
                        for kt in range(HALF):
                            mm = nc.tensor.matmul(o, v(kt), att_pT[:, h % 2, kt, :], start=(kt == 0),
                                                  stop=(kt == HALF - 1))
                    mm.then_inc(sem(tag + "_values"), 1)

        def act_split(act, e, it=0):
            act.wait_ge(HERE[e % RAW], 16 * (e // RAW + 1) + it * 16)
            if e >= SPLIT:
                act.wait_ge(sem("piece_used"), e - SPLIT + 1 + it * RAW)
            nc.scalar.activation(w_hi[:, e % SPLIT, :], raw[:, e % RAW, :], ACT.Copy).then_inc(sem("split_high"), 1)

        def act_in_split(act, n, src, ready, tile=0):
            for c in range(src.shape[1] // 2):
                ready(c)
                nc.scalar.activation(in_hi[:, tile + 2 * c:tile + 2 * c + 2, :], src[:, 2 * c:2 * c + 2, :], ACT.Copy)\
                    .then_inc(sem("in_high"), 1)

        def act_ffn(act, n, e0, end):
            def after(e, up=None, it=0):
                if up is not None:
                    act.wait_ge(sem("piece_used"), e0 + e + 1 + it * RAW)
                    nc.scalar.activation(silu[:, up % 2, :], ps[:, 4 + up % 2, 0:S], ACT.Silu).then_inc(sem("silu_ready"), 1)
                if e0 + e + SPLIT < end:
                    act_split(act, e0 + e + SPLIT, it)

            ffn_steps(act, after)

        def ffn_steps(eng, after):
            def tile(j, it=0):
                if j == 0:
                    after(0)
                    after(1, 0)
                    return
                after(3 * j - 1, None, it)
                after(3 * j, j, it)
                after(3 * j + 1, None, it)

            tile(0)
            tile(1)
            with eng.Fori(0, TILES // 2 - 2) as it:
                tile(2, it)
                tile(3, it)
            tile(TILES - 2)
            tile(TILES - 1)
            after(FFN_PIECES - 1)

        def act_linear(act, q0, e0, dests, square=False):
            for i, dst in enumerate(dests):
                e = e0 + 2 * i
                act_split(act, e + SPLIT)
                act.wait_ge(sem("piece_used"), e + 2)
                src = two_tiles(4 + (q0 + i) % 4)
                if square:
                    nc.scalar.activation(sq[:, 2 * i:2 * i + 2, :], src, ACT.Square).then_inc(sem("rms_square"), 1)
                nc.scalar.activation(dst, src, ACT.Copy).then_inc(sem("linear_taken"), 1)
                act_split(act, e + 1 + SPLIT)

        class Taking:

            def __init__(self, act):
                self.act, self.quarter = act, 0

            def __call__(self, pieces):
                end = min(self.quarter + int(4 * pieces), 4 * (E_BRANCH - E_FILL))
                for x in range(self.quarter // 8, end // 8):
                    q = FIRST_SLOTS + x
                    self.act.wait_ge(sem("piece_used"), E_FILL + 2 * x + 2)
                    dst, f = self.dest(q)
                    nc.scalar.activation(dst, ps[:, 2 + q % 2, :].rearrange("p (c t) -> p c t", c=2), f)\
                        .then_inc(sem("filling_taken"), 1)
                self.quarter = end

            def until(self, slot):
                self(2 * (slot - FIRST_SLOTS) - self.quarter / 4)

            def dest(self, q):
                if q < FILL_GLA + 2:
                    return (gla_q, gla_k)[q - FILL_GLA][:, :, :], ACT.Copy
                if q < FILL_GLA + 4:
                    c = (q - FILL_GLA - 2) * S
                    return gla_v[:, :, c:c + S], ACT.Copy
                for first, end, dst, f in ((FILL_GLA + 4, FILL_RWKV, gla_g, ACT.Copy),
                                           (FILL_RWKV, FILL_GATES, rz[:, :, 1:], ACT.Copy),
                                           (FILL_GATES, MIX_SLOTS, gates, ACT.Sigmoid)):
                    if first <= q < end:
                        return dst[:, 2 * (q - first):2 * (q - first) + 2, :], f

        def act_std(act, s, n, bank, eps):
            act.wait_ge(sem("stat_sum"), s + 1)
            nc.scalar.activation(std[:, :], ps[:, bank, 0:S], ACT.Sqrt, bias=cst(eps, 1), scale=1.0 / D)\
                .then_inc(sem("stat_std"), 1)

        def act_ln(act, n, bank, eps):
            for c in range(KD // 2):
                act.wait_ge(sem("ln_centred"), 4 * n + c + 1)
                nc.scalar.activation(sq[:, 2 * c:2 * c + 2, :], zT[:, 2 * c:2 * c + 2, :], ACT.Square)\
                    .then_inc(sem("ln_square"), 1)
            act_std(act, 2 * n + 1, n, bank + 1, eps)

        def act_attention(act, tag, heads, outs, take=lambda n: None):
            for i in range(heads + 3):
                if i < heads:
                    act.wait_ge(sem(tag + "_biased"), i + 1)
                    for t in range(HALF):
                        e = nc.scalar.activation(att_p[:, i % 4, t, :], att_p[:, i % 4, t, :], ACT.Exp,
                                                 bias=att_max[:, i % 4, t:t + 1], accum_out=att_sum[:, i % 4, t:t + 1])
                        e.then_inc(sem(tag + "_exp"), 1)
                h = i - 2
                if 0 <= h < heads:
                    act.wait_ge(sem(tag + "_transposed"), h + 1)
                    if h >= 2:
                        act.wait_ge(sem(tag + "_values"), h - 1)
                    nc.scalar.activation(att_pT[:, h % 2, :, :], ps[:, 6 + h % 2, :].rearrange("p (c t) -> p c t", c=2),
                                         ACT.Copy).then_inc(sem(tag + "_turned"), 1)
                h = i - 3
                if 0 <= h < heads:
                    act.wait_ge(sem(tag + "_values"), h + 1)
                    dst, src = outs(h)
                    nc.scalar.activation(dst, src, ACT.Copy).then_inc(sem(tag + "_out"), 1)
                take(1)

        class Steps:

            def __init__(self, eng, name):
                self.eng, self.sem, self.n = eng, sem(name), 0

            def link(self, ins):
                self.n += 1
                ins.then_inc(self.sem, 1)
                self.eng.wait_ge(self.sem, self.n)

        def low_part(eng, e, it=0):
            eng.wait_ge(sem("split_high"), e + 1 + it * RAW)
            eng.tensor_tensor(w_lo[:, e % SPLIT, :], raw[:, e % RAW, :],
                                                 w_hi[:, e % SPLIT, :].bitcast(F32), ALU.subtract)\
                .then_inc(sem("split_low"), 1)

        def pool_low(pool, e0, n):
            if e0:
                pool.wait_ge(sem("split_low"), e0)
            if n >= RAW:
                with pool.Fori(0, n // RAW) as it:
                    for e in range(e0, e0 + RAW):
                        low_part(pool, e, it)
            for e in range(e0 + n // RAW * RAW, e0 + n):
                low_part(pool, e)

        def pool_filling(pool):
            one = ones[:, 0:1].broadcast_to([P, PIECE])
            pool.wait_ge(sem("split_high"), E_FILL)
            for e in range(E_FILL, E_BRANCH + SPLIT):
                pool.wait_ge(HERE[e % RAW], 16 * (e // RAW + 1))
                pool.wait_ge(sem("piece_used"), e - SPLIT + 1)
                pool.tensor_tensor(w_hi[:, e % SPLIT, :], raw[:, e % RAW, :], one, ALU.mult).then_inc(sem("split_high"), 1)
                low_part(pool, e)

        def dve_in_split(dve, n, src, produce=None, tile=0):
            chunks = src.shape[1] // 2
            if produce is not None:
                produce(0)
            for c in range(chunks):
                if produce is not None and c + 1 < chunks:
                    produce(c + 1)
                dve.wait_ge(sem("in_high"), n + c + 1)
                lo, hi = tile + 2 * c, tile + 2 * c + 2
                nc.vector.tensor_tensor(in_lo[:, lo:hi, :], src[:, 2 * c:2 * c + 2, :], in_hi[:, lo:hi, :].bitcast(F32),
                                        ALU.subtract).then_inc(sem("in_ready"), 1)

        def dve_ffn(dve, n, e0):
            def after(e, up=None, it=0):
                if up is not None:
                    j, count = up % 2, n * TILES + up + 1 + it * 2
                    dve.wait_ge(sem("silu_ready"), count)
                    nc.vector.tensor_tensor(hid[:, j, :], silu[:, j, :], ps[:, 4 + j, S:2 * S], ALU.mult)\
                        .then_inc(sem("hidden_whole"), 1)
                    dve.wait_ge(sem("hidden_whole"), count)
                    nc.vector.tensor_copy(hid_hi[:, j, :], hid[:, j, :]).then_inc(sem("hidden_high"), 1)
                    dve.wait_ge(sem("hidden_high"), count)
                    nc.vector.tensor_tensor(hid_lo[:, j, :], hid[:, j, :], hid_hi[:, j, :].bitcast(F32), ALU.subtract)\
                        .then_inc(sem("hidden_ready"), 1)
                if e + SPLIT < FFN_PIECES:
                    low_part(dve, e0 + e + SPLIT, it)

            dve.wait_ge(sem("split_low"), e0 + SPLIT)
            ffn_steps(dve, after)

        def dve_inverse(dve, steps, n):
            dve.wait_ge(sem("stat_std"), n + 1)
            steps.link(nc.vector.reciprocal(rstd[:, :], std[:, :]))

        def over_two(v):
            return v.rearrange("p (o t) -> p o t", o=1).broadcast_to([P, 2, S])

        def dve_ln(dve, steps, n, bank, alpha, y, ready, chunk=None):
            pairs = [slice(2 * c, 2 * c + 2) for c in range(KD // 2)]
            for c, two in enumerate(pairs):
                ready(c)
                nc.vector.scalar_tensor_tensor(zT[:, two, :], xT[:, two, :], alpha, y(c), ALU.mult, ALU.add)\
                    .then_inc(sem("ln_in"), 1)
            dve.wait_ge(sem("stat_sum"), 2 * n + 1)
            dve.wait_ge(sem("ln_in"), 4 * n + 4)
            for two in pairs:
                nc.vector.scalar_tensor_tensor(zT[:, two, :], over_two(ps[:, bank, 0:S]), -1.0 / D, zT[:, two, :], ALU.mult,
                                               ALU.add)\
                    .then_inc(sem("ln_centred"), 1)
            dve_inverse(dve, steps, n)
            dve.wait_ge(sem("ln_centred"), 4 * n + 4)
            g, b = V1["ln_g"] + n * KD, V1["ln_b"] + n * KD

            def produce(c):
                steps.link(nc.vector.tensor_tensor(zT[:, pairs[c], :], zT[:, pairs[c], :], over_two(rstd[:, :]), ALU.mult))
                for k in (2 * c, 2 * c + 1):
                    ins = nc.vector.tensor_scalar(xT[:, k, :], zT[:, k, :], vec1[:, g + k:g + k + 1],
                                                  vec1[:, b + k:b + k + 1], ALU.mult, ALU.add)
                ins.then_inc(sem("x_ready"), 1)

            if chunk is not None:
                dve_in_split(dve, chunk, xT, produce)
            else:
                for c in range(KD // 2):
                    produce(c)

        def dve_attention(dve, steps, tag, heads, scale, bias):
            for i in range(heads + 1):
                if i < heads:
                    dve.wait_ge(sem(tag + "_scores"), i + 1)
                    if i >= 4:
                        dve.wait_ge(sem(tag + "_transposed"), i - 3)
                    for t in range(HALF):
                        s = ps[:, 4 + i % 2, t * S:(t + 1) * S]
                        b = bias(i, t)
                        if b is None:
                            ins = nc.vector.tensor_scalar(att_p[:, i % 4, t, :], s, scale, None, ALU.mult)
                        else:
                            ins = nc.vector.scalar_tensor_tensor(att_p[:, i % 4, t, :], s, scale, b, ALU.mult, ALU.add)
                    steps.link(ins)
                    nc.vector.tensor_reduce(att_max[:, i % 4, :], att_p[:, i % 4, :, :], AX.X, ALU.max,
                                            negate=True).then_inc(sem(tag + "_biased"), 1)
                h = i - 1
                if 0 <= h < heads:
                    dve.wait_ge(sem(tag + "_exp"), HALF * (h + 1))
                    steps.link(nc.vector.reciprocal(att_rec[:, h % 4, :], att_sum[:, h % 4, :]))
                    for t in range(HALF):
                        ins = nc.vector.tensor_scalar(att_p[:, h % 4, t, :], att_p[:, h % 4, t, :],
                                                      att_rec[:, h % 4, t:t + 1], None, ALU.mult)
                    ins.then_inc(sem(tag + "_probs"), 1)

        def col2(name, i=0, p=P, lo=0):
            return vec2[lo:lo + p, V2[name] + i:V2[name] + i + 1]

        def bank2(b, p=P, lo=0):
            return ps[lo:lo + p, b:b + 2, :].rearrange("p b (c t) -> p (b c) t", c=2)

        RMS_BANK = (0, 6, 7, 2, 0, 1, 0, 1, 6)

        def pe_rms(pe, n):
            pe_stat(pe, RMS_BANK[n], sq, "rms_square", 4 * n)

        def act_rms(act, n, src, ready):
            for c in range(KD // 2):
                ready(c)
                nc.scalar.activation(sq[:, 2 * c:2 * c + 2, :], src(c), ACT.Square).then_inc(sem("rms_square"), 1)

        def act_rms_std(act, n):
            act_std(act, n, n, RMS_BANK[n], "eps_rms")

        def dve_rms(dve, steps, n, src, gain, dst, chunk, tag="in_raw"):
            dve_inverse(dve, steps, n)

            def produce(c):
                for k in (2 * c, 2 * c + 1):
                    ins = nc.vector.scalar_tensor_tensor(dst[:, k, :], src[:, k, :], gain(k), rstd[:, :], ALU.mult,
                                                         ALU.mult)
                ins.then_inc(sem(tag), 1)

            dve_in_split(dve, chunk, dst, produce)

        def dve_residual(dve, steps, n, r, y, gain, scale):
            dve_inverse(dve, steps, n)
            for c in range(KD // 2 + 1):
                if c < KD // 2:
                    for j in range(2):
                        k = 2 * c + j
                        ins = nc.vector.scalar_tensor_tensor(zT[:, k, :], y(c)[:, j, :], gain(k), rstd[:, :],
                                                             ALU.mult, ALU.mult)
                    ins.then_inc(sem("residual_scaled"), 1)
                if c:
                    dve.wait_ge(sem("residual_scaled"), 4 * r + c)
                    two = slice(2 * c - 2, 2 * c)
                    nc.vector.scalar_tensor_tensor(xT[:, two, :], zT[:, two, :], scale, xT[:, two, :], ALU.mult, ALU.add)\
                        .then_inc(sem("x_ready"), 1)

        ROPE = 32

        def pe_mla(pe, fill):
            fill(1)
            pe.wait_ge(sem("mla_square"), 2)
            for i, tiles in enumerate(((0, 1), (2,))):
                for t in tiles:
                    mm = nc.tensor.matmul(ps[:, 0, i * S:(i + 1) * S], ones[:, 0:P], sq[:, t, :], start=(t == tiles[0]),
                                          stop=(t == tiles[-1]))
            mm.then_inc(sem("mla_sum"), 1)
            fill(2)
            pe.wait_ge(sem("mla_normed"), 3)
            pe.wait_ge(sem("small_here"), 7 * 16)
            pe.wait_ge(sem("linear_taken"), FIRST_SLOTS)
            for t in (4, 5, 6, 7, 0, 1, 2, 3):
                for k in range(2):
                    mm = nc.tensor.matmul(ps[:, (0, 1, 4, 5)[t // 2], (t % 2) * S:(t % 2 + 1) * S], w_uq[:, k, t * P:(t + 1) * P],
                                          c_q[:, k, :], start=(k == 0), stop=(k == 1))
            mm.then_inc(sem("mla_q_ready"), 1)
            for t in range(4):
                nc.tensor.matmul(ps[:, 6 + t // 2, (t % 2) * S:(t % 2 + 1) * S], w_ukv[:, t * P:(t + 1) * P], c_kv[:, 0, :],
                                 start=True, stop=True)
            pe.wait_ge(sem("mla_taken"), 1)
            for t in range(HALF):
                mm = nc.tensor.matmul(ps[:, 4 + t, :], c_kv[:, 0, t * P:(t + 1) * P], w_ukv[:, 512:1024], start=True,
                                      stop=True)
            mm.then_inc(sem("mla_kv_ready"), 1)
            fill(1)
            pe.wait_ge(sem("mla_taken"), 4)
            pe.wait_ge(sem("mla_rope"), 2)

            def scores(h, t):
                o, r = 64 * (h % 2), ROPE * (h % 4)
                return [(mla_qn[o:o + 64, h // 2, t * P:(t + 1) * P], mla_kn[o:o + 64, h // 2, :]),
                        (mla_qr[r:r + ROPE, h // 4, t * P:(t + 1) * P], k_rope[r:r + ROPE, 0, :])]

            def values(h):
                o = 64 * (h % 2)
                return [(ps[o:o + 64, h % 2, 0:S], lambda kt: mla_v[:, kt, h * 64:(h + 1) * 64])]

            pe_attention(pe, "mla", MLA_HEADS, scores, values, fill)

        def act_mla(act, take):
            act.wait_ge(sem("linear_taken"), 2)
            act.wait_ge(sem("narrow_taken"), 1)
            nc.scalar.activation(sq[:, 0:2, :], c_q[:, :, :], ACT.Square).then_inc(sem("mla_square"), 1)
            nc.scalar.activation(sq[:, 2:3, :], c_kv[:, :, :], ACT.Square).then_inc(sem("mla_square"), 1)
            act.wait_ge(sem("mla_sum"), 1)
            nc.scalar.activation(zT[:, 0, :], ps[:, 0, 0:S], ACT.Sqrt, bias=cst("eps_rms", 1), scale=1.0 / 256)\
                .then_inc(sem("mla_std"), 1)
            nc.scalar.activation(zT[:, 1, :], ps[:, 0, S:2 * S], ACT.Sqrt, bias=cst("eps_rms", 1), scale=1.0 / P)\
                .then_inc(sem("mla_std"), 1)
            take(3)
            act.wait_ge(sem("mla_q_ready"), 1)
            nc.scalar.activation(mla_qr[:, :, :], bank2(4), ACT.Copy).then_inc(sem("mla_taken"), 1)
            nc.scalar.activation(mla_qn[:, :, :], bank2(0), ACT.Copy).then_inc(sem("mla_taken"), 1)
            act.wait_ge(sem("mla_kv_ready"), 1)
            nc.scalar.activation(mla_kn[:, :, :], bank2(6), ACT.Copy).then_inc(sem("mla_taken"), 1)
            nc.scalar.activation(mla_v[:, :, :], ps[:, 4:6, :], ACT.Copy).then_inc(sem("mla_taken"), 1)
            take(1)

            def outs(h):
                o = 64 * (h % 2)
                return o_mla[o:o + 64, h // 2, :], ps[o:o + 64, h % 2, 0:S]

            act_attention(act, "mla", MLA_HEADS, outs, take)

        def dve_mla(dve, steps):
            dve.wait_ge(sem("mla_std"), 2)
            steps.link(nc.vector.reciprocal(zT[:, 2:4, :], zT[:, 0:2, :]))
            for k in range(2):
                nc.vector.scalar_tensor_tensor(c_q[:, k, :], c_q[:, k, :], col2("mla_q_norm", k), zT[:, 2, :], ALU.mult,
                                               ALU.mult).then_inc(sem("mla_normed"), 1)
            nc.vector.scalar_tensor_tensor(c_kv[:, 0, :], c_kv[:, 0, :], col2("mla_kv_norm"), zT[:, 3, :], ALU.mult,
                                           ALU.mult).then_inc(sem("mla_normed"), 1)
            cos1, sin1 = cos.rearrange("p (o t) -> p o t", o=1), sin.rearrange("p (o t) -> p o t", o=1)
            dve.wait_ge(sem("linear_taken"), 3)
            for buf, n, ready in ((k_rope, 1, None), (mla_qr, 2, sem("mla_taken"))):
                if ready is not None:
                    dve.wait_ge(ready, 1)
                nc.vector.tensor_tensor(buf[:, 0:n, :], buf[:, 0:n, :], cos1.broadcast_to([P, n, S]), ALU.mult)
                steps.link(nc.vector.tensor_tensor(buf[:, n:2 * n, :], buf[:, n:2 * n, :], sin1.broadcast_to([P, n, S]),
                                                   ALU.mult))
                nc.vector.tensor_tensor(buf[:, 0:n, :], buf[:, 0:n, :], buf[:, n:2 * n, :], ALU.add)\
                    .then_inc(sem("mla_rope"), 1)
            causal = cst("causal", 2 * S)
            dve_attention(dve, steps, "mla", MLA_HEADS, 96 ** -0.5, lambda h, t: causal[:, t * S:(t + 1) * S])

        GLA_AT = [CHUNK * i * (i + 1) // 2 for i in range(CHUNKS)]
        PIECES = [(1, 0, P, 0), (2, 0, P, 64), (3, 0, P, 128), (3, 1, P, 192), (0, 0, 64, 256), (2, 1, 64, 320)]

        def pe_gla(pe, fill):
            for c in range(2):
                mm = nc.tensor.matmul(ps[:, 6, c * S:(c + 1) * S], w_alpha[0:16, c * P:(c + 1) * P], rz[0:16, 14, 1:],
                                      start=True, stop=True)
            mm.then_inc(sem("gla_logit"), 1)
            fill(4)
            pe.wait_ge(sem("gla_scaled"), 1)
            for h in range(GLA_HEADS):
                o, c = 64 * (h % 2), h // 2
                for i, jt, n, col in PIECES:
                    k0 = GLA_AT[i] + jt * P
                    mm = nc.tensor.matmul(ps[0:n, 4 + h, col:col + CHUNK], gla_kd[o:o + 64, c, k0:k0 + n],
                                          gla_qd[o:o + 64, c, i * CHUNK:(i + 1) * CHUNK], start=True, stop=True)
                mm.then_inc(sem("gla_scores"), 1)
            pe.wait_ge(sem("mla_out"), MLA_HEADS)
            pe.wait_ge(sem("filling_taken"), FILL_GLA + 4 - FIRST_SLOTS)
            for h in range(GLA_HEADS):
                fill(1)
                pe.wait_ge(sem("gla_masked"), h + 1)
                for i in range(CHUNKS):
                    mine = [x for x in PIECES if x[0] == i]
                    for m, (_, jt, n, col) in enumerate(mine):
                        out_at = (h % 2) * S + i * CHUNK
                        mm = nc.tensor.matmul(ps[:, h // 2, out_at:out_at + CHUNK], gla_v[0:n, jt, h * P:(h + 1) * P],
                                              gla_at[0:n, h, col:col + CHUNK], start=(m == 0), stop=(m == len(mine) - 1))
            mm.then_inc(sem("gla_out"), 1)
            fill(1)
            pe.wait_ge(sem("gla_square"), 1)
            for h in range(GLA_HEADS):
                mm = nc.tensor.matmul(ps[:, 4 + h // 2, (h % 2) * S:(h % 2 + 1) * S], ones[:, 0:P], sq[:, h, :],
                                      start=True, stop=True)
            mm.then_inc(sem("gla_sum"), 1)

        def act_gla(act, take):
            act.wait_ge(sem("gla_logit"), 1)
            for c in range(2):
                ins = nc.scalar.activation(gla_tmp[:, 0, c, :], ps[:, 6, c * S:(c + 1) * S], ACT.Abs, bias=col2("gla_b_alpha", c))
            ins.then_inc(sem("gla_log"), 1)
            act.wait_ge(sem("gla_log"), 1)
            nc.scalar.activation(gla_tmp[:, 0, :, :], gla_tmp[:, 0, :, :], ACT.Exp, scale=-1.0).then_inc(sem("gla_log"), 1)
            act.wait_ge(sem("gla_log"), 2)
            nc.scalar.activation(gla_tmp[:, 0, :, :], gla_tmp[:, 0, :, :], ACT.Ln, bias=1.0).then_inc(sem("gla_log"), 1)
            take(4)
            act.wait_ge(sem("gla_summed"), 1)
            for i in range(CHUNKS):
                for c in range(2):
                    n = CHUNK * (i + 1)
                    nc.scalar.activation(gla_ek[:, c, GLA_AT[i]:GLA_AT[i] + n], gla_b[:, c, 1:n + 1], ACT.Exp,
                                         bias=gla_mid[:, 0, c, i:i + 1], scale=-1.0 / GLA_GATE)
                    ins = nc.scalar.activation(gla_qd[:, c, i * CHUNK:(i + 1) * CHUNK],
                                               gla_b[:, c, i * CHUNK + 1:(i + 1) * CHUNK + 1], ACT.Exp,
                                               bias=gla_mid[:, 1, c, i:i + 1], scale=1.0 / GLA_GATE)
            ins.then_inc(sem("gla_decay"), 1)
            take(4)
            act.wait_ge(sem("filling_taken"), FILL_RWKV - FIRST_SLOTS)
            nc.scalar.activation(gla_g[:, :, :], gla_g[:, :, :], ACT.Silu).then_inc(sem("gla_gate"), 1)
            act.wait_ge(sem("gla_out"), 1)
            nc.scalar.activation(sq[:, 0:4, :], bank2(0), ACT.Square).then_inc(sem("gla_square"), 1)
            take(1)
            act.wait_ge(sem("gla_sum"), 1)
            nc.scalar.activation(zT[:, 0:4, :], bank2(4), ACT.Sqrt, bias=cst("eps_rms", 1), scale=1.0 / P)\
                .then_inc(sem("gla_std"), 1)

        def dve_gla(dve, steps):
            dve.wait_ge(sem("gla_log"), 1)
            steps.link(nc.vector.memset(gla_b[:, :, 0:1], 0.0))
            for c in range(2):
                ins = nc.vector.tensor_scalar(gla_tmp[:, 1, c, :], ps[:, 6, c * S:(c + 1) * S], col2("gla_b_alpha", c), 0.0,
                                              ALU.add, ALU.min)
            steps.link(ins)
            dve.wait_ge(sem("gla_log"), 3)
            steps.link(nc.vector.tensor_tensor(gla_tmp[:, 1, :, :], gla_tmp[:, 1, :, :], gla_tmp[:, 0, :, :], ALU.subtract))
            for c in range(2):
                ins = nc.vector.tensor_tensor_scan(gla_b[:, c, 1:], ones[:, :], gla_tmp[:, 1, c, :], 0.0, ALU.mult, ALU.add)
            steps.link(ins)
            mid = gla_b[:, :, 1:].rearrange("p c (n t) -> p c n t", t=CHUNK)[:, :, :, CHUNK // 2 - 1]
            nc.vector.tensor_scalar(gla_mid[:, 0, :, :], mid, 1.0 / GLA_GATE, None, ALU.mult)
            nc.vector.tensor_scalar(gla_mid[:, 1, :, :], mid, -1.0 / GLA_GATE, None, ALU.mult).then_inc(sem("gla_summed"), 1)
            dve.wait_ge(sem("gla_decay"), 1)
            dve.wait_ge(sem("filling_taken"), FILL_GLA + 2 - FIRST_SLOTS)
            for i in range(CHUNKS):
                n, at = CHUNK * (i + 1), GLA_AT[i]
                nc.vector.tensor_tensor(gla_kd[:, :, at:at + n], gla_ek[:, :, at:at + n], gla_k[:, :, 0:n], ALU.mult)
            nc.vector.scalar_tensor_tensor(gla_qd[:, :, :], gla_q[:, :, :], 64 ** -0.5, gla_qd[:, :, :], ALU.mult, ALU.mult)\
                .then_inc(sem("gla_scaled"), 1)
            for h in range(GLA_HEADS):
                dve.wait_ge(sem("gla_scores"), h + 1)
                nc.vector.tensor_tensor(gla_at[:, h, 0:256], ps[:, 4 + h, 0:256], cst("gla_full", 256), ALU.mult)
                nc.vector.tensor_tensor(gla_at[0:64, h, 256:384], ps[0:64, 4 + h, 256:384], cst("gla_half", P, 64), ALU.mult)\
                    .then_inc(sem("gla_masked"), 1)
        def dve_gla_end(dve, steps):
            dve.wait_ge(sem("gla_std"), 1)
            steps.link(nc.vector.reciprocal(zT[:, 0:4, :], zT[:, 0:4, :]))
            for b in range(2):
                ins = nc.vector.scalar_tensor_tensor(o_gla[:, 2 * b:2 * b + 2, :],
                                                     ps[:, b, :].rearrange("p (c t) -> p c t", c=2), col2("gla_norm"),
                                                     zT[:, 2 * b:2 * b + 2, :], ALU.mult, ALU.mult)
            steps.link(ins)
            dve.wait_ge(sem("gla_gate"), 1)
            nc.vector.tensor_tensor(o_gla, o_gla, gla_g[:, :, :], ALU.mult).then_inc(sem("gla_done"), 1)

        POWERS = 5
        W = CHUNK

        HEADS = [(t, slice(64 * half, 64 * half + 64)) for t in range(4) for half in range(2)]

        def pe_halves(pe, src, bank):
            for t in range(4):
                mm = nc.tensor.matmul(ps[:, bank + t // 2, (t % 2) * S:(t % 2 + 1) * S], cst("halves", P), src(t), start=True,
                                      stop=True)
            return mm

        def four(bank):
            return ps[:, bank, 0:4 * W].rearrange("p (t c) -> p t c", t=4)

        def pe_rwkv(pe, fill):
            fill.until(FILL_GATES)
            fill(5)
            pe.wait_ge(sem("rw_tanh"), 1)
            for t in range(4):
                nc.tensor.matmul(ps[:, 4 + t // 2, (t % 2) * S:(t % 2 + 1) * S], w_lora[0:64, t * P:(t + 1) * P],
                                 rz[0:64, 12, 1:], start=True, stop=True)
            for t in range(4):
                mm = nc.tensor.matmul(ps[:, 6 + t // 2, (t % 2) * S:(t % 2 + 1) * S], w_lora[64:P, t * P:(t + 1) * P],
                                      rz[64:P, 12, 1:], start=True, stop=True)
            mm.then_inc(sem("rw_logits"), 1)
            fill(1)
            pe.wait_ge(sem("rw_square"), 1)
            pe.wait_ge(sem("gla_done"), 1)
            pe_halves(pe, lambda t: sq[:, t, :], 0).then_inc(sem("rw_norm"), 1)
            fill(7)
            pe.wait_ge(sem("rw_scaled"), 1)
            pe.wait_ge(sem("rw_sigmoid"), 8)
            for n in range(CHUNKS):
                at = slice(n * W, (n + 1) * W)
                pe.wait_ge(sem("rw_chunk_in"), n + 1)
                rw_c = rw_c2[n % 2]
                for t, o in HEADS:
                    for b, src in enumerate((rz[o, 8 + t, 1 + n * W:1 + (n + 1) * W], rw_c[o, 2, t, :], rw_c[o, 3, t, :])):
                        col = (b % 2) * 4 * W + t * W
                        mm = nc.tensor.matmul(ps[o, b // 2, col:col + W], src, const[o, CONST["ident"] + o.start:
                                              CONST["ident"] + o.stop], start=True, stop=True)
                mm.then_inc(sem("rw_turned"), 1)
                if n:
                    pe.wait_ge(sem("rw_y_taken"), n)
                for t, o in HEADS:
                    for bank, keys in ((4, rw_bh), (6, rw_kh)):
                        nc.tensor.matmul(ps[o, bank, 2 * W * t:2 * W * (t + 1)].rearrange("p (a c) -> p a c", a=2),
                                         keys[o, t, at], rw_pr[o, t, :, at], start=True, stop=True)
                    mm = nc.tensor.matmul(ps[o, 7, t * W:(t + 1) * W], rw_pr[o, t, 0, at], rw_bh[o, t, at], start=True,
                                          stop=True)
                mm.then_inc(sem("rw_grams"), 1)
                fill(1)
                pe.wait_ge(sem("rw_grams_taken"), n + 1)

                def power(i, t, o):
                    return (rw_pow[o, 2 * (i % 2), t, :],
                            rw_pow[o, 2 * (i % 2) + 1, t, :] if i else rw_g[o, 0, t, 0:W])

                pe.wait_ge(sem("rw_tok"), 2 * (n + 1))
                pe.wait_ge(sem("rw_state"), n + 1)
                for t, o in HEADS:
                    x = ps[o, 7, t * W:(t + 1) * W]
                    nc.tensor.matmul(x, rw_c[o, 0, t, :], rw_st[o, t, :], start=True, stop=False)
                    mm = nc.tensor.matmul(x, rw_g[o, 1, t, 0:W], rw_tok[o, 0, t, :], start=False, stop=True)
                mm.then_inc(sem("rw_x"), 1)
                for i in range(1, POWERS + 1):
                    if i > 1:
                        pe.wait_ge(sem("rw_pow_a"), POWERS * n + i - 1)
                        pe.wait_ge(sem("rw_pow_b"), (POWERS - 1) * n + i - 1)
                    for t, o in HEADS:
                        a, b = power(i - 1, t, o)
                        mm = nc.tensor.matmul(ps[o, 0, t * W:(t + 1) * W], b, a, start=True, stop=True)
                        if i < POWERS:
                            mm = nc.tensor.matmul(ps[o, 1, t * W:(t + 1) * W], a, b, start=True, stop=True)
                    mm.then_inc(sem("rw_pow"), 1)
                    fill(0.25)
                    pe.wait_ge(sem("rw_pow_a"), POWERS * n + i)
                    if i > 1:
                        pe.wait_ge(sem("rw_inv"), POWERS * n + i - 1)
                    for t, o in HEADS:
                        mm = nc.tensor.matmul(ps[o, 5, t * W:(t + 1) * W], power(i, t, o)[0], rw_t[o, (i - 1) % 2, t, :],
                                              start=True, stop=True)
                    mm.then_inc(sem("rw_inv_mm"), 1)
                pe.wait_ge(sem("rw_x_taken"), n + 1)
                pe.wait_ge(sem("rw_inv"), POWERS * (n + 1))
                for t, o in HEADS:
                    mm = nc.tensor.matmul(ps[o, 0, t * W:(t + 1) * W], rw_t[o, POWERS % 2, t, :], rw_x[o, t, :], start=True,
                                          stop=True)
                mm.then_inc(sem("rw_u"), 1)
                for t, o in HEADS:
                    y, state = ps[o, 4, t * W:(t + 1) * W], ps[o, 5, t * W:(t + 1) * W]
                    nc.tensor.matmul(y, rw_st[o, t, :], rw_c[o, 1, t, :], start=(t == 0), stop=False, skip_group_check=True)
                    nc.tensor.matmul(y, rw_tok[o, 0, t, :], rw_g[o, 1, t, W:2 * W], start=False, stop=False,
                                     skip_group_check=True)
                    nc.tensor.matmul(state, rw_tok[o, 1, t, :], rw_tok[o, 0, t, :], start=(t == 0), stop=False,
                                     skip_group_check=True)
                pe.wait_ge(sem("rw_u_taken"), n + 1)
                for t, o in HEADS:
                    y, state = ps[o, 4, t * W:(t + 1) * W], ps[o, 5, t * W:(t + 1) * W]
                    nc.tensor.matmul(y, rw_u[o, t, :], rw_g[o, 0, t, W:2 * W], start=False, stop=True, skip_group_check=True)
                    mm = nc.tensor.matmul(state, rw_tok[o, 2, t, :], rw_u[o, t, :], start=False, stop=True,
                                          skip_group_check=True)
                mm.then_inc(sem("rw_y"), 1)
            fill.until(MIX_SLOTS)
            pe.wait_ge(sem("rw_y_taken"), CHUNKS)
            pe_halves(pe, lambda t: rw_kk[:, t, :], 0).then_inc(sem("gn_mean"), 1)
            pe.wait_ge(sem("rw_bonus"), 1)
            pe.wait_ge(sem("rw_state"), CHUNKS + 1)
            pe_halves(pe, lambda t: rw_bh[:, t, :], 4).then_inc(sem("rw_bonus_sum"), 1)
            for t in range(4):
                o = ps[:, 6 + t // 2, (t % 2) * S:(t % 2 + 1) * S]
                nc.tensor.matmul(o, w_rgate[:, 0, t * P:(t + 1) * P], rz[:, 13, 1:], start=True, stop=False)
                mm = nc.tensor.matmul(o, w_rgate[32:64, 1, t * P:(t + 1) * P], rz[32:64, 14, 1:], start=False, stop=True)
            mm.then_inc(sem("rw_gate"), 1)
            pe.wait_ge(sem("gn_square"), 1)
            pe_halves(pe, lambda t: sq[:, t, :], 0).then_inc(sem("gn_var"), 1)
            pe_branches(pe)

        def act_rwkv(act, take):
            take.until(FILL_GATES)
            act.wait_ge(sem("rw_mixed"), 15)
            nc.scalar.activation(rz[0:64, 12, 1:], rz[0:64, 12, 1:], ACT.Tanh).then_inc(sem("rw_tanh"), 1)
            nc.scalar.activation(rz[:, 13, 1:], rz[:, 13, 1:], ACT.Sigmoid).then_inc(sem("rw_gate_in"), 1)
            nc.scalar.activation(rz[32:64, 14, 1:], rz[32:64, 14, 1:], ACT.Sigmoid).then_inc(sem("rw_gate_in"), 1)
            take(5)
            act.wait_ge(sem("rw_logits"), 1)
            for t in range(4):
                nc.scalar.activation(rw_tmp[:, t, :], ps[:, 4 + t // 2, (t % 2) * S:(t % 2 + 1) * S], ACT.Sigmoid,
                                     bias=col2("rwkv_w0", t)).then_inc(sem("rw_sigmoid"), 1)
            for t in range(4):
                nc.scalar.activation(rw_a[:, t, :], ps[:, 6 + t // 2, (t % 2) * S:(t % 2 + 1) * S], ACT.Sigmoid,
                                     bias=col2("rwkv_a0", t)).then_inc(sem("rw_sigmoid"), 1)
            take(1)
            act.wait_ge(sem("rw_kk_raw"), 4)
            nc.scalar.activation(sq[:, 0:4, :], rw_kk[:, :, :], ACT.Square).then_inc(sem("rw_square"), 1)
            act.wait_ge(sem("rw_norm"), 1)
            nc.scalar.activation(zT[:, 0:4, :], bank2(0), ACT.Sqrt, bias=cst("eps_0", 1)).then_inc(sem("rw_norm_root"), 1)
            act.wait_ge(sem("rw_logs"), 1)
            nc.scalar.activation(rw_pr[:, :, 1, :], rw_bh[:, :, :], ACT.Exp, scale=-DECAY_SCALE)
            nc.scalar.activation(rw_kh[:, :, :], rw_bh[:, :, :], ACT.Exp, scale=DECAY_SCALE)
            nc.scalar.activation(rw_edge[:, 0:2], rw_edge[:, 0:2], ACT.Exp, scale=-DECAY_SCALE)
            nc.scalar.activation(rw_pr[:, :, 0, :], rw_pr[:, :, 0, :], ACT.Exp, scale=-DECAY_SCALE)\
                .then_inc(sem("rw_decay"), 1)
            take(7)
            for n in range(CHUNKS):
                act.wait_ge(sem("rw_turned"), n + 1)
                nc.scalar.activation(rw_tok[:, 0:2], ps[:, 0, :].rearrange("p (b t c) -> p b t c", b=2, t=4), ACT.Copy)\
                    .then_inc(sem("rw_tok"), 1)
                nc.scalar.activation(rw_tok[:, 2], four(1), ACT.Copy).then_inc(sem("rw_tok"), 1)
                take(1)
                act.wait_ge(sem("rw_x"), n + 1)
                nc.scalar.activation(rw_x, four(7), ACT.Copy).then_inc(sem("rw_x_taken"), 1)
                for i in range(1, POWERS + 1):
                    act.wait_ge(sem("rw_pow"), POWERS * n + i)
                    nc.scalar.activation(rw_pow[:, 2 * (i % 2)], four(0), ACT.Copy).then_inc(sem("rw_pow_a"), 1)
                    take(0.25)
                act.wait_ge(sem("rw_y"), n + 1)
                nc.scalar.activation(rw_kk[:, :, n * W:(n + 1) * W], four(4), ACT.Copy).then_inc(sem("rw_y_taken"), 1)
            take.until(MIX_SLOTS)

            def heads_done(c):
                act.wait_ge(*((sem("mla_out"), MLA_HEADS) if c < 2 else (sem("gla_done"), 1)))
                act.wait_ge(sem("piece_used"), E_BRANCH)

            act_in_split(act, C_AB, two_branches, heads_done)
            act.wait_ge(sem("gn_centred"), 1)
            nc.scalar.activation(sq[:, 0:4, :], rw_kk[:, :, :], ACT.Square).then_inc(sem("gn_square"), 1)
            act.wait_ge(sem("gn_var"), 1)
            nc.scalar.activation(zT[:, 4:8, :], bank2(0), ACT.Sqrt, bias=cst("eps_gn", 1), scale=1.0 / 64)\
                .then_inc(sem("gn_std"), 1)
            act.wait_ge(sem("split_high"), E_BRANCH + SPLIT)
            for i in range(8):
                act_split(act, E_BRANCH + i + SPLIT)
                act.wait_ge(sem("piece_used"), E_BRANCH + i + 1)
                dst = (y_mla, y_gla)[i // 4][:, 2 * (i % 4):2 * (i % 4) + 2, :]
                nc.scalar.activation(dst, two_tiles(2 + i % 2), ACT.Copy).then_inc(sem("branch_taken"), 1)

        def dve_rwkv(dve, steps):
            r, k, v = (rz[:, 4 * i:4 * i + 4, 1:] for i in range(3))
            dve.wait_ge(sem("filling_taken"), FILL_GATES - FIRST_SLOTS)
            dve.wait_ge(sem("gla_out"), 1)
            diff = view(0, 15, S, of=work)
            steps.link(nc.vector.tensor_tensor(diff, rz[:, :, 0:S], rz[:, :, 1:], ALU.subtract))
            for t in range(15):
                lo, n = (0, P) if t < 14 else (32, 32)
                nc.vector.scalar_tensor_tensor(rz[lo:lo + n, t, 1:], diff[lo:lo + n, t, :], col2("rwkv_mu", t, n, lo),
                                               rz[lo:lo + n, t, 1:], ALU.mult, ALU.add).then_inc(sem("rw_mixed"), 1)
            dve.wait_ge(sem("rw_mixed"), 15)
            for t in range(4):
                nc.vector.tensor_scalar(rw_kk[:, t, :], k[:, t, :], col2("rwkv_k_k", t), None, ALU.mult)\
                    .then_inc(sem("rw_kk_raw"), 1)
            dve_gla_end(dve, steps)
            dve.wait_ge(sem("gla_done"), 1)
            steps.link(nc.vector.memset(rw_L[:, :, 0:1], 0.0))
            steps.link(nc.vector.memset(rw_st[:, :, :], 0.0))
            dve.wait_ge(sem("rw_sigmoid"), 8)
            for t in range(4):
                ins = nc.vector.tensor_tensor_scan(rw_L[:, t, 1:], ones[:, :], rw_tmp[:, t, :], 0.0, ALU.mult, ALU.add)
            steps.link(ins)
            inc = rw_L[:, :, 1:].rearrange("p c (n t) -> p c n t", t=W)
            exc = rw_L[:, :, 0:S].rearrange("p c (n t) -> p c n t", t=W)
            mid = inc[:, :, :, W // 2 - 1:W // 2]
            nc.vector.tensor_tensor(rw_bh[:, :, :].rearrange("p c (n t) -> p c n t", t=W), inc,
                                    mid.broadcast_to([P, 4, CHUNKS, W]), ALU.subtract)
            nc.vector.tensor_tensor(rw_pr[:, :, 0, :].rearrange("p c (n t) -> p c n t", t=W), exc,
                                    mid.broadcast_to([P, 4, CHUNKS, W]), ALU.subtract)
            nc.vector.tensor_tensor(rw_edge[:, 0], mid[:, :, :, 0], exc[:, :, :, 0], ALU.subtract)
            nc.vector.tensor_tensor(rw_edge[:, 1], inc[:, :, :, W - 1], mid[:, :, :, 0], ALU.subtract)\
                .then_inc(sem("rw_logs"), 1)
            dve.wait_ge(sem("rw_norm_root"), 1)
            steps.link(nc.vector.tensor_scalar(zT[:, 0:4, :], zT[:, 0:4, :], 1e-12, None, ALU.max))
            steps.link(nc.vector.reciprocal(zT[:, 0:4, :], zT[:, 0:4, :]))
            steps.link(nc.vector.tensor_tensor(rw_kk[:, :, :], rw_kk[:, :, :], zT[:, 0:4, :], ALU.mult))
            for t in range(4):
                ins = nc.vector.tensor_scalar(zT[:, t, :], rw_a[:, t, :], -1.0, col2("rwkv_k_a", t), ALU.add, ALU.mult)
            steps.link(ins)
            nc.vector.scalar_tensor_tensor(k, zT[:, 0:4, :], 1.0, k, ALU.add, ALU.mult)
            steps.link(nc.vector.scalar_tensor_tensor(rw_a[:, :, :], rw_kk[:, :, :], -1.0, rw_a[:, :, :], ALU.mult, ALU.mult))
            dve.wait_ge(sem("rw_decay"), 1)
            nc.vector.tensor_tensor(rw_pr[:, :, 0, :], rw_pr[:, :, 0, :], rw_kk[:, :, :], ALU.mult)
            nc.vector.tensor_tensor(rw_pr[:, :, 1, :], rw_pr[:, :, 1, :], r, ALU.mult)
            nc.vector.tensor_tensor(rw_edge[:, 2], rw_edge[:, 0], rw_edge[:, 1], ALU.mult)
            steps.link(nc.vector.tensor_tensor(rw_bh[:, :, :], rw_kh[:, :, :], rw_a[:, :, :], ALU.mult))
            steps.link(nc.vector.tensor_tensor(rw_kh[:, :, :], rw_kh[:, :, :], k, ALU.mult))
            nc.vector.tensor_copy(rw_tmp[:, 0, 0:1], rw_st[:, 0, 0:1]).then_inc(sem("rw_scaled"), 1)
            dve.sem_inc(sem("rw_state"), 1)

            def edge(e, n):
                return rw_edge[:, e, :, n:n + 1].broadcast_to([P, 4, W])

            def chunk_in(n):
                at, rw_c = slice(n * W, (n + 1) * W), rw_c2[n % 2]
                nc.vector.tensor_tensor(rw_c[:, 0], rw_pr[:, :, 0, at], edge(0, n), ALU.mult)
                nc.vector.tensor_tensor(rw_c[:, 1], rw_pr[:, :, 1, at], edge(0, n), ALU.mult)
                nc.vector.tensor_tensor(rw_c[:, 2], rw_kh[:, :, at], edge(1, n), ALU.mult)
                nc.vector.tensor_tensor(rw_c[:, 3], rw_bh[:, :, at], edge(1, n), ALU.mult).then_inc(sem("rw_chunk_in"), 1)

            chunk_in(0)
            for n in range(CHUNKS):
                dve.wait_ge(sem("rw_grams"), n + 1)
                def blocks(name, w):
                    return cst(name, w).rearrange("p (o c) -> p o c", o=1).broadcast_to([P, 4, w])

                for b in range(2):
                    ins = nc.vector.tensor_tensor(rw_g[:, b], ps[:, 4 + 2 * b, :].rearrange("p (h c) -> p h c", h=4),
                                                  blocks("strict", 2 * W), ALU.mult)
                steps.link(ins)
                nc.vector.tensor_tensor(rw_t[:, 0], rw_g[:, 0, :, 0:W], blocks("eye2", W), ALU.add)
                nc.vector.tensor_tensor(rw_pow[:, 0], four(7), blocks("lower", W), ALU.mult)\
                    .then_inc(sem("rw_grams_taken"), 1)
                for i in range(1, POWERS + 1):
                    if i < POWERS:
                        dve.wait_ge(sem("rw_pow"), POWERS * n + i)
                        nc.vector.tensor_copy(rw_pow[:, 2 * (i % 2) + 1], four(1)).then_inc(sem("rw_pow_b"), 1)
                    dve.wait_ge(sem("rw_inv_mm"), POWERS * n + i)
                    if i > 1:
                        dve.wait_ge(sem("rw_inv"), POWERS * n + i - 1)
                    nc.vector.tensor_tensor(rw_t[:, i % 2], four(5), rw_t[:, (i - 1) % 2], ALU.add)\
                        .then_inc(sem("rw_inv"), 1)
                    if i == 1 and n + 1 < CHUNKS:
                        chunk_in(n + 1)
                dve.wait_ge(sem("rw_u"), n + 1)
                nc.vector.tensor_copy(rw_u, four(0)).then_inc(sem("rw_u_taken"), 1)
                dve.wait_ge(sem("rw_y"), n + 1)
                steps.link(nc.vector.tensor_tensor(rw_st[:, :, :], rw_st[:, :, :], edge(2, n), ALU.mult))
                nc.vector.tensor_tensor(rw_st[:, :, :], rw_st[:, :, :], four(5), ALU.add).then_inc(sem("rw_state"), 1)
                dve.wait_ge(sem("rw_state"), n + 2)
            for t in range(4):
                ins = nc.vector.scalar_tensor_tensor(rw_bh[:, t, :], r[:, t, :], col2("rwkv_r_k", t), k[:, t, :], ALU.mult,
                                                     ALU.mult)
            ins.then_inc(sem("rw_bonus"), 1)
            dve.wait_ge(sem("gn_mean"), 1)
            steps.link(nc.vector.tensor_scalar(zT[:, 0:4, :], bank2(0), 1.0 / 64, None, ALU.mult))
            nc.vector.tensor_tensor(rw_kk[:, :, :], rw_kk[:, :, :], zT[:, 0:4, :], ALU.subtract).then_inc(sem("gn_centred"), 1)
            dve_in_split(dve, C_AB, two_branches)
            dve.wait_ge(sem("gn_std"), 1)
            steps.link(nc.vector.reciprocal(zT[:, 0:4, :], zT[:, 4:8, :]))
            steps.link(nc.vector.tensor_tensor(rw_kk[:, :, :], rw_kk[:, :, :], zT[:, 0:4, :], ALU.mult))
            for t in range(4):
                nc.vector.tensor_scalar(rw_kk[:, t, :], rw_kk[:, t, :], col2("rwkv_ln_w", t), col2("rwkv_ln_b", t), ALU.mult,
                                        ALU.add)
            dve.wait_ge(sem("rw_bonus_sum"), 1)
            steps.link(nc.vector.tensor_tensor(zT[:, 0:4, :], v, bank2(4), ALU.mult))
            steps.link(nc.vector.tensor_tensor(rw_kk[:, :, :], rw_kk[:, :, :], zT[:, 0:4, :], ALU.add))
            dve.wait_ge(sem("rw_gate"), 1)
            nc.vector.tensor_tensor(o_rwkv, rw_kk[:, :, :], bank2(6), ALU.mult).then_inc(sem("rw_done"), 1)

        def layer_end(eng, n):
            eng.drain().then_inc(arrived, 1)
            if eng is not nc.sync:
                eng.wait_ge(cleared, n)
                return
            eng.wait_ge(arrived, 5 * n)
            eng.sem_inc(all_arrived, 1)
            ids = sorted(s.num for k, s in sems.items() if k not in WHOLE)
            assert ids == list(range(ids[0], ids[-1] + 1))
            eng.sem_clear(range(ids[0], ids[-1] + 1))
            eng.drain().then_inc(cleared, 1)

        @block.tensor
        def _(pe):
            pe.wait_ge(loaded, 32)
            pe.wait_ge(ones_set, 1)
            with pe.Fori(0, LAYERS) as l:
                pe_ffn(pe, 0, E1_FFN1, C1_FFN1)
                pe_ln(pe, 0, 6)
                pe_linear(pe, 0, E1_IN, [features] * 8 + [tokens] * 2, C1_IN)
                pe.wait_ge(sem("pooled"), 1)
                pe.wait_ge(sem("pool_w_here"), 64)
                for c in range(2):
                    mm = nc.tensor.matmul(ps[:, 2, c * S:(c + 1) * S], pool_w[:, c, :], pooled[:, c, :],
                                          start=True, stop=True)
                mm.then_inc(sem("pool_ready"), 1)
                pe.wait_ge(sem("linear_taken"), 10)

                def scores(h, t):
                    o = 64 * (h % 2)
                    return [(na_q[o:o + 64, h // 2, t * P:(t + 1) * P], na_k[o:o + 64, h // 2, :])]

                def values(h):
                    o = 64 * (h % 2)
                    return [(ps[o:o + 64, h % 2, 0:S], lambda kt: na_v[:, kt, h * 64:(h + 1) * 64])]

                pe_attention(pe, "na", NA_HEADS, scores, values)
                pe_linear(pe, 10, E1_OUT, [features] * 4, C1_OUT)
                pe_ln(pe, 1, 0)
                pe_ffn(pe, 1, E1_FFN2, C1_FFN2)
                pe_ln(pe, 2, 6)
                layer_end(pe, l + 1)
            with pe.Fori(0, LAYERS) as l:
                pe_rms(pe, 0)
                pe_ffn(pe, 0, E_FFN1, C_FFN1)
                pe_rms(pe, 1)
                pe_rms(pe, 2)
                pe_linear(pe, Q_IN, E_IN, [features] * FIRST_SLOTS, C_IN)
                fill = Filling(pe)
                pe_mla(pe, fill)
                pe_gla(pe, fill)
                pe_rwkv(pe, fill)
                pe.wait_ge(sem("mla_out"), MLA_HEADS)
                pe.wait_ge(sem("gla_done"), 1)
                pe.wait_ge(sem("rw_done"), 1)

                pe_linear(pe, Q_BRANCH, E_BRANCH + 8, [branch(0)] * 4, C_RW)
                pe_rms(pe, 3)
                pe_linear(pe, Q_OUT, E_OUT, [features] * 2, C_OUT)
                pe_linear(pe, Q_OUT + 2, E_OUT + 4, [features] * 2, C_OUT)
                pe_rms(pe, 4)
                pe.wait_ge(sem("linear_taken"), Q_KV)
                pe_linear(pe, Q_KV, E_KV, [features] * 2, C_KV)
                pe_linear(pe, Q_KV + 2, E_KV + 4, [features] * 2 + [tokens], C_KV)
                pe_rms(pe, 5)
                pe_linear(pe, Q_KV + 5, E_KV + 10, [tokens] * 2, C_KV)
                pe_linear(pe, Q_KV + 7, E_KV + 14, [tokens], C_KV)
                pe_linear(pe, Q_Q, E_Q, [features] * 4, C_Q)
                pe.wait_ge(sem("linear_taken"), Q_O)

                def mem_scores(h, t):
                    return [(mem_q[:, 2 * h + c, t * P:(t + 1) * P], mem_k[:, 2 * h + c, :]) for c in range(2)]

                def mem_values(h):
                    return [(ps[:, h % 2, c * S:(c + 1) * S],
                             lambda kt, c=c: mem_v[:, kt, (2 * h + c) * P:(2 * h + c + 1) * P]) for c in range(2)]

                pe_attention(pe, "mem", MEM_HEADS, mem_scores, mem_values)
                pe_linear(pe, Q_O, E_O, [features] * 4, C_O)
                pe_rms(pe, 6)
                pe_rms(pe, 7)
                pe_ffn(pe, 1, E_FFN2, C_FFN2)
                pe_rms(pe, 8)
                layer_end(pe, l + 1 + LAYERS)

        @block.scalar
        def _(act):
            act.wait_ge(loaded, 32)
            with act.Fori(0, LAYERS) as l:
                act_in_split(act, C1_FFN1, xT, lambda c: None)
                for e in range(SPLIT):
                    act_split(act, e)
                act_ffn(act, 0, E1_FFN1, E1_END)
                act_ln(act, 0, 6, "eps_ln4")
                act_in_split(act, C1_IN, xT, lambda c: act.wait_ge(sem("x_ready"), c + 1))
                act.wait_ge(sem("pool_pads"), 1)
                dests = [pool_in[:, :, POOL_PAD:POOL_PAD + S], gate_b[:, :, :], gate_c[:, :, :], conv_h[:, :, :],
                         na_q[:, 0:2, :], na_q[:, 2:4, :], na_k[:, 0:2, :], na_k[:, 2:4, :],
                         na_v[:, :, 0:S], na_v[:, :, S:2 * S]]
                act_linear(act, 0, E1_IN, dests)
                act.wait_ge(sem("pool_ready"), 1)
                for c in range(2):
                    nc.scalar.activation(mix1[:, c, :], ps[:, 2, c * S:(c + 1) * S], ACT.Copy,
                                         scale=vec1[:, V1["pool_scale"] + c:V1["pool_scale"] + c + 1])\
                        .then_inc(sem("pool_out"), 1)

                def outs(h):
                    o = 64 * (h % 2)
                    return mix1[o:o + 64, 4 + h // 2, :], ps[o:o + 64, h % 2, 0:S]

                act_attention(act, "na", NA_HEADS, outs)

                def mixed(c):
                    act.wait_ge(*((sem("pool_out"), 2), (sem("conv_out"), 1), (sem("na_out"), 6),
                                  (sem("na_out"), NA_HEADS))[c])

                act_in_split(act, C1_OUT, mix1, mixed)
                for e in range(E1_OUT, E1_FFN2):
                    act_split(act, e + SPLIT)
                act_ln(act, 1, 0, "eps_ln")
                act_in_split(act, C1_FFN2, xT, lambda c: act.wait_ge(sem("x_ready"), KD // 2 + c + 1))
                act_ffn(act, 1, E1_FFN2, E1_END)
                act_ln(act, 2, 6, "eps_ln4")
                layer_end(act, l + 1)
            act.wait_ge(sem("angle_ready"), 1)
            nc.scalar.activation(sin, sq[:, 2, :], ACT.Sin).then_inc(sem("rope_sin"), 1)
            nc.scalar.activation(sq[:, 3, :], sq[:, 2, :], ACT.Abs).then_inc(sem("rope_sin"), 1)
            act.wait_ge(sem("angle_ready"), 2)
            nc.scalar.activation(cos, sq[:, 4, :], ACT.Sin).then_inc(sem("rope_sin"), 1)
            with act.Fori(0, LAYERS) as l:
                x_pair = lambda c: xT[:, 2 * c:2 * c + 2, :]
                act_rms(act, 0, x_pair, lambda c: act.wait_ge(rope_set, 1))
                act_rms_std(act, 0)
                for e in range(SPLIT):
                    act_split(act, e)
                in_raw = lambda n: lambda c: act.wait_ge(sem("in_raw"), 4 * n + c + 1)
                act_in_split(act, C_FFN1, zT, in_raw(0))
                act_ffn(act, 0, E_FFN1, E_END)
                act_rms(act, 1, two_tiles, lambda c: act.wait_ge(sem("piece_used"), E_IN))
                act_rms_std(act, 1)
                act_rms(act, 2, x_pair, lambda c: act.wait_ge(sem("x_ready"), c + 1))
                act_rms_std(act, 2)
                act_in_split(act, C_IN, zT, in_raw(1))
                for e in range(E_IN + SPLIT, E_FILL):
                    act_split(act, e)
                act.wait_ge(sem("rz_cleared"), 1)
                for q, dst in enumerate((c_q, None, k_rope)):
                    act.wait_ge(sem("piece_used"), E_IN + 2 * q + 2)
                    two = ps[:, 4 + q, :].rearrange("p (c t) -> p c t", c=2)
                    if q == 1:
                        nc.scalar.activation(c_kv[:, 0, :], two[:, 0, :], ACT.Copy).then_inc(sem("narrow_taken"), 1)
                        nc.scalar.activation(rz[:, 14, 1:], two[:, 1, :], ACT.Copy).then_inc(sem("linear_taken"), 1)
                    else:
                        nc.scalar.activation(dst[:, :, :], two, ACT.Copy).then_inc(sem("linear_taken"), 1)
                take = Taking(act)
                act_mla(act, take)
                act_gla(act, take)
                act_rwkv(act, take)

                def rwkv_done(c):
                    act.wait_ge(sem("rw_done"), 1)
                    act.wait_ge(sem("piece_used"), E_BRANCH + 4)

                act_in_split(act, C_RW, o_rwkv, rwkv_done)
                for e in range(E_BRANCH + 8, E_OUT):
                    act_split(act, e + SPLIT)
                act_rms(act, 3, lambda c: mem_n[:, 2 * c:2 * c + 2, :], lambda c: act.wait_ge(sem("mem_here"), 16))
                act_rms_std(act, 3)
                act_in_split(act, C_OUT, merged, lambda c: act.wait_ge(sem("merged"), c + 1))
                act_linear(act, Q_OUT, E_OUT, [yT[:, 2 * i:2 * i + 2, :] for i in range(4)], square=True)

                def mem_normed(c):
                    act.wait_ge(sem("mem_ready"), c + 1)
                    act.wait_ge(sem("piece_used"), E_KV)

                act_in_split(act, C_KV, mem_n, mem_normed)
                act_rms_std(act, 4)
                mem_kv = [mem_k[:, 2 * i:2 * i + 2, :] for i in range(4)] + [mem_v[:, :, i * S:(i + 1) * S] for i in range(4)]
                act_linear(act, Q_KV, E_KV, mem_kv[:4])
                act_rms(act, 5, x_pair, lambda c: act.wait_ge(sem("x_ready"), 4 + c + 1))
                act_linear(act, Q_KV + 4, E_KV + 8, mem_kv[4:5])
                act_rms_std(act, 5)
                act_linear(act, Q_KV + 5, E_KV + 10, mem_kv[5:])
                act_in_split(act, C_Q, zT, in_raw(2))
                act_linear(act, Q_Q, E_Q, [mem_q[:, 2 * i:2 * i + 2, :] for i in range(4)])

                def outs(h):
                    return mem_o[:, 2 * h:2 * h + 2, :], ps[:, h % 2, :].rearrange("p (c t) -> p c t", c=2)

                act_attention(act, "mem", MEM_HEADS, outs)
                act_in_split(act, C_O, mem_o, lambda c: act.wait_ge(sem("mem_out"), c + 1))
                def out_ready(c):
                    act_split(act, E_O + 2 * c + SPLIT)
                    act.wait_ge(sem("piece_used"), E_O + 2 * c + 2)
                    act_split(act, E_O + 2 * c + 1 + SPLIT)

                act_rms(act, 6, mem_y, out_ready)
                act_rms_std(act, 6)
                act_rms(act, 7, x_pair, lambda c: act.wait_ge(sem("x_ready"), 8 + c + 1))
                act_rms_std(act, 7)
                act_in_split(act, C_FFN2, zT, in_raw(3))
                act_ffn(act, 1, E_FFN2, E_END)
                act_rms(act, 8, two_tiles, lambda c: act.wait_ge(sem("piece_used"), E_END))
                act_rms_std(act, 8)
                layer_end(act, l + 1 + LAYERS)

        @block.vector
        def _(dve):
            nc.vector.memset(ones[:, :], 1.0).then_inc(ones_set, 1)
            dve.wait_ge(ones_set, 1)
            dve.wait_ge(loaded, 32)
            with dve.Fori(0, LAYERS) as l:
                steps = Steps(dve, "vector_step")
                dve_in_split(dve, C1_FFN1, xT)
                nc.vector.memset(pool_in[:, :, :], 0.0).then_inc(sem("pool_pads"), 1)
                steps.link(nc.vector.memset(conv_z[:, :, :], 0.0))
                dve_ffn(dve, 0, E1_FFN1)
                dve.wait_ge(sem("vec_here"), 16)
                dve_ln(dve, steps, 0, 6, 2 * ALPHA, two_tiles, lambda c: dve.wait_ge(sem("piece_used"), E1_IN), C1_IN)
                dve.wait_ge(sem("linear_taken"), 1)
                n = S + 2 * POOL_PAD
                steps.link(nc.vector.tensor_tensor(sum2[:, :, 0:n - 1], pool_in[:, :, 0:n - 1], pool_in[:, :, 1:n], ALU.add))
                steps.link(nc.vector.tensor_tensor(sum4[:, :, 0:n - 3], sum2[:, :, 0:n - 3], sum2[:, :, 2:n - 1], ALU.add))
                steps.link(nc.vector.tensor_tensor(sum8[:, :, 0:n - 7], sum4[:, 1:2, 0:n - 7], sum4[:, 1:2, 4:n - 3], ALU.add))
                steps.link(nc.vector.tensor_tensor(sum16[:, :, 0:n - 15], sum8[:, :, 0:n - 15], sum8[:, :, 8:n - 7], ALU.add))
                cnt = cst("pool_cnt", 2 * S).rearrange("p (c t) -> p c t", c=2)
                for g, (w, sums) in enumerate(zip(POOL_W, (sum2[:, 0], sum4[:, 0], sum8[:, 0], sum16[:, 0]))):
                    o = 64 * (g % 2)
                    lo = POOL_PAD - w // 2
                    ins = nc.vector.tensor_tensor(pooled[o:o + 64, g // 2, :], sums[o:o + 64, lo:lo + S],
                                                  cnt[o:o + 64, g // 2, :], ALU.mult)
                steps.link(ins)
                nc.vector.tensor_tensor(pooled[:, :, :], pooled[:, :, :], pool_in[:, :, POOL_PAD:POOL_PAD + S],
                                        ALU.subtract).then_inc(sem("pooled"), 1)
                dve.wait_ge(sem("linear_taken"), 4)
                steps.link(nc.vector.tensor_tensor(conv_z[:, :, 1:S + 1], gate_c[:, :, :], conv_h[:, :, :], ALU.mult))
                for tap in (1, 0, 2):
                    for c in range(2):
                        w = vec1[:, V1["conv_w"] + 2 * tap + c:V1["conv_w"] + 2 * tap + c + 1]
                        z = conv_z[:, c, tap:tap + S]
                        if tap == 1:
                            ins = nc.vector.tensor_scalar(conv_y[:, c, :], z, w, None, ALU.mult)
                        else:
                            ins = nc.vector.scalar_tensor_tensor(conv_y[:, c, :], z, w, conv_y[:, c, :], ALU.mult, ALU.add)
                    steps.link(ins)
                nc.vector.tensor_tensor(mix1[:, 2:4, :], gate_b[:, :, :], conv_y[:, :, :], ALU.mult)\
                    .then_inc(sem("conv_out"), 1)
                dve.wait_ge(sem("bias_here"), 16 * 2 * NA_HEADS)
                strips = na_bias.rearrange("p h (e k) -> p (h e) k", k=GRID)
                mask = cst("na_mask", GRID).rearrange("p (o k) -> p o k", o=1).broadcast_to([P, NA_HEADS * STRIPS, GRID])
                steps.link(nc.vector.tensor_tensor(strips[:, :, ::-1], na_raw, mask, ALU.min))
                dve_attention(dve, steps, "na", NA_HEADS, 64 ** -0.5,
                              lambda h, t: na_bias[:, h, (2 - 2 * t) * GRID:(6 - 2 * t) * GRID])
                dve_in_split(dve, C1_OUT, mix1)
                dve_ln(dve, steps, 1, 0, ALPHA, lambda c: two_tiles(4 + (10 + c) % 4),
                       lambda c: dve.wait_ge(sem("piece_used"), E1_OUT + 2 * c + 2), C1_FFN2)
                dve_ffn(dve, 1, E1_FFN2)
                dve_ln(dve, steps, 2, 6, 2 * ALPHA, two_tiles, lambda c: dve.wait_ge(sem("piece_used"), E1_END))
                layer_end(dve, l + 1)
            steps = Steps(dve, "rope_step")
            dve.wait_ge(positions_here, 16)
            steps.link(nc.vector.tensor_scalar(sq[:, 0, :], pos_i[:, :], cst("inv_freq", 1), None, ALU.mult))
            steps.link(nc.vector.tensor_scalar(sq[:, 1, :], sq[:, 0, :], 1.0 / (2 * PI), ROUND, ALU.mult, ALU.add))
            steps.link(nc.vector.tensor_scalar(sq[:, 1, :], sq[:, 1, :], ROUND, None, ALU.subtract))
            for part in (TURN1, TURN2, TURN3):
                steps.link(nc.vector.scalar_tensor_tensor(sq[:, 0, :], sq[:, 1, :], -part, sq[:, 0, :], ALU.mult, ALU.add))
            nc.vector.tensor_scalar(sq[:, 2, :], sq[:, 0, :], 3.1415925, -3.1415925, ALU.min, ALU.max)\
                .then_inc(sem("angle_ready"), 1)
            dve.wait_ge(sem("rope_sin"), 2)
            nc.vector.tensor_scalar(sq[:, 4, :], sq[:, 3, :], -1.0, PI / 2, ALU.mult, ALU.add)\
                .then_inc(sem("angle_ready"), 1)
            dve.wait_ge(sem("rope_sin"), 3)
            nc.vector.tensor_scalar(sin, sin, cst("rope_sign", 1), None, ALU.mult).then_inc(rope_set, 1)
            dve.wait_ge(rope_set, 1)
            with dve.Fori(0, LAYERS) as l:
                steps = Steps(dve, "mix_step")
                nc.vector.memset(rz[:, :, 0:1], 0.0).then_inc(sem("rz_cleared"), 1)
                dve.wait_ge(sem("gains_here"), 16)
                dve_rms(dve, steps, 0, xT, lambda k: col2("norm_g", k), zT, C_FFN1)
                dve_ffn(dve, 0, E_FFN1)
                dve_residual(dve, steps, 1, 0, two_tiles, lambda k: col2("norm_g", KD + k), 0.5)
                dve_rms(dve, steps, 2, xT, lambda k: col2("norm_g", 2 * KD + k), zT, C_IN)
                dve_mla(dve, steps)
                dve_gla(dve, steps)
                dve_rwkv(dve, steps)
                dve_in_split(dve, C_RW, o_rwkv)
                dve.wait_ge(sem("filling_taken"), MIX_SLOTS - FIRST_SLOTS)
                gates_b = [gates[:, b * KD:(b + 1) * KD, :] for b in range(3)]
                for b, y in enumerate((y_mla, y_gla)):
                    dve.wait_ge(sem("branch_taken"), 4 * b + 4)
                    steps.link(nc.vector.tensor_tensor(gates_b[b], gates_b[b], y, ALU.mult))
                steps.link(nc.vector.tensor_tensor(merged, merged, gates_b[1], ALU.add))
                for i in range(4):
                    q = Q_BRANCH + i
                    two = slice(2 * i, 2 * i + 2)
                    dve.wait_ge(sem("piece_used"), E_BRANCH + 8 + i + 1)
                    nc.vector.tensor_tensor(gates_b[2][:, two, :], gates_b[2][:, two, :], two_tiles(4 + q % 4), ALU.mult)\
                        .then_inc(sem("linear_taken"), 1)
                    dve.wait_ge(sem("linear_taken"), q + 1)
                    nc.vector.tensor_tensor(merged[:, two, :], merged[:, two, :], gates_b[2][:, two, :], ALU.add)\
                        .then_inc(sem("merged"), 1)
                dve_in_split(dve, C_OUT, merged)
                dve_rms(dve, steps, 3, mem_n, lambda k: col2("mem_norm", k), mem_n, C_KV, "mem_ready")
                dve_residual(dve, steps, 4, 1, lambda c: yT[:, 2 * c:2 * c + 2, :], lambda k: col2("norm_g", 3 * KD + k), 1.0)
                dve_rms(dve, steps, 5, xT, lambda k: col2("norm_g", 4 * KD + k), zT, C_Q)
                dve_attention(dve, steps, "mem", MEM_HEADS, 256 ** -0.5, lambda h, t: None)
                dve_in_split(dve, C_O, mem_o)
                dve_residual(dve, steps, 6, 2, mem_y, lambda k: col2("norm_g", 5 * KD + k), 1.0)
                dve_rms(dve, steps, 7, xT, lambda k: col2("norm_g", 6 * KD + k), zT, C_FFN2)
                dve_ffn(dve, 1, E_FFN2)
                dve_residual(dve, steps, 8, 3, two_tiles, lambda k: col2("norm_g", 7 * KD + k), 0.5)
                layer_end(dve, l + 1 + LAYERS)

        @block.gpsimd
        def _(pool):
            pool.memset(pool_w[:, :, :], 0.0).then_inc(sem_pw, 1)
            with pool.Fori(0, LAYERS) as l:
                pool_low(pool, 0, SPLIT)
                pool_low(pool, E1_IN, E1_FFN2 + SPLIT - E1_IN)
                layer_end(pool, l + 1)
            with pool.Fori(0, LAYERS) as l:
                pool_low(pool, 0, SPLIT)
                pool_low(pool, E_IN, E_FILL - E_IN)
                pool_filling(pool)
                pool_low(pool, E_BRANCH + SPLIT, E_FFN2 - E_BRANCH)
                layer_end(pool, l + 1 + LAYERS)

        @block.sync
        def _(sp):
            sp.dma_start(xT[:, :, :], a["xT"]).then_inc(loaded, 16)
            sp.dma_start(const[:, :], a["const"]).then_inc(loaded, 16)
            pos = a["positions"]
            sp.dma_start(pos_i[:, :], bass.AP(tensor=pos.tensor, offset=pos.offset, ap=[[0, P], [1, S]])).then_inc(positions_here, 16)
            g1 = a["ffn1_w_gate"].rearrange("l (k p) f -> l p k f", p=P)
            u1 = a["ffn1_w_up"].rearrange("l (k p) f -> l p k f", p=P)
            d1 = a["ffn1_w_down"].rearrange("l (j p) d -> l p j d", p=P)
            g2 = a["ffn2_w_gate"].rearrange("l (k p) f -> l p k f", p=P)
            u2 = a["ffn2_w_up"].rearrange("l (k p) f -> l p k f", p=P)
            d2 = a["ffn2_w_down"].rearrange("l (j p) d -> l p j d", p=P)
            w_in = a["w_in"].rearrange("l (k p) f -> l p k f", p=P)
            w_out = a["w_out"].rearrange("l (k p) f -> l p k f", p=P)

            def ffn(e0, l, g, u, d):
                sp_ffn(sp, e0, lambda c: g[l][:, :, bass.ds(c, P)], lambda c: u[l][:, :, bass.ds(c, P)],
                       lambda c: d_rows(d[l], c))

            def d_rows(d, c):
                return d[:, c // P:c // P + 1, :] if isinstance(c, int) else d[:, bass.ds(c // P, 1), :]

            def columns(w, n, token_slots=()):
                for i in range(n):
                    c = i * S
                    for h in range(2):
                        yield (w[:, h * KD // 2:(h + 1) * KD // 2, c:c + S] if i in token_slots else
                               w[:, :, c + h * P:c + (h + 1) * P])

            with sp.Fori(0, LAYERS) as l:
                ffn(E1_FFN1, l, g1, u1, d1)
                sp.dma_start(vec1[:, :], a["vec1"][l]).then_inc(sem("vec_here"), 16)
                sp.wait_ge(sem_pw, 1)
                for g in range(4):
                    o = 64 * (g % 2)
                    sp.dma_start(pool_w[o:o + 64, g // 2, o:o + 64], a["pool_w"][l][g]).then_inc(sem("pool_w_here"), 16)
                for half in range(2):
                    for h in range(NA_HEADS):
                        row = a["rpb"][l][h]
                        src = bass.AP(tensor=row.tensor, offset=row.offset + (5 - half) * RPB_C + 15 - (GRID - 1),
                                      ap=[[1, GRID], [RPB_C, STRIPS], [1, GRID]])
                        sp.dma_start(na_raw[64 * half:64 * half + 64, h * STRIPS:(h + 1) * STRIPS, :],
                                     src).then_inc(sem("bias_here"), 16)
                sp_linear(sp, E1_IN, columns(w_in[l], 10, (8, 9)))
                sp_linear(sp, E1_OUT, columns(w_out[l], 4))
                ffn(E1_FFN2, l, g2, u2, d2)
                layer_end(sp, l + 1)
            f_in = a["w_ffn_in_2"].rearrange("l n (k p) f -> l n p k f", p=P)
            f_out = a["w_ffn_out_2"].rearrange("l n (j p) d -> l n p j d", p=P)
            mix_in = a["w_mix"].rearrange("l (k p) f -> l p k f", p=P)
            w_branch = a["w_branch_2"].rearrange("l (b k p) f -> l b p k f", p=P, k=4)
            w_out2 = a["w_out_2"].rearrange("l (k p) f -> l p k f", p=P)
            wkv = a["mem_wkv_2"].rearrange("l (k p) f -> l p k f", p=P)
            wq = a["mem_wq_2"].rearrange("l (k p) f -> l p k f", p=P)
            wo = a["mem_wo_2"].rearrange("l (k p) f -> l p k f", p=P)

            def ffn2(e0, l, n):
                sp_ffn(sp, e0, lambda c: f_in[l, n][:, :, bass.ds(c, P)], lambda c: f_in[l, n][:, :, bass.ds(c + F, P)],
                       lambda c: d_rows(f_out[l, n], c))

            with sp.Fori(0, LAYERS) as l:
                sp.dma_start(vec2, a["vec2"][l]).then_inc(sem("gains_here"), 16)
                ffn2(E_FFN1, l, 0)
                for dst, src in ((w_uq, a["w_uq"][l].rearrange("(k p) c -> p k c", p=P)),
                                 (w_ukv, a["w_ukv"][l]), (w_alpha[0:16, :], a["gla_w_alpha_2"][l]),
                                 (w_lora[0:64, :], a["rwkv_w_decay_2"][l]), (w_lora[64:P, :], a["rwkv_w_iclr_2"][l]),
                                 (w_rgate[:, 0, :], a["rwkv_w_gate_2"][l][0:P, :]),
                                 (w_rgate[32:64, 1, :], a["rwkv_w_gate_2"][l][P:P + 32, :])):
                    sp.dma_start(dst, src).then_inc(sem("small_here"), 16)
                sp_linear(sp, E_IN, columns(mix_in[l], MIX_SLOTS, (FILL_GLA + 2, FILL_GLA + 3)))
                sp_linear(sp, E_BRANCH, [w_branch[l, b][:, :, i * S:(i + 1) * S] for b in range(3) for i in range(4)])
                sp.wait_ge(sem("rw_done"), 1)
                sp.dma_start(mem_n, a["memT"]).then_inc(sem("mem_here"), 16)
                for w, e0, n, token_slots in ((w_out2, E_OUT, 4, ()), (wkv, E_KV, 8, range(4, 8)), (wq, E_Q, 4, ()), (wo, E_O, 4, ())):
                    sp_linear(sp, e0, columns(w[l], n, token_slots))
                ffn2(E_FFN2, l, 1)
                layer_end(sp, l + 1 + LAYERS)
            sp.dma_start(out, xT[:, :, :]).then_inc(stored, 16)
            sp.wait_ge(stored, 16)


def host_arrays(i):
    L = LAYERS
    arr = {"const": constants()}

    def fm(x):
        return np.ascontiguousarray(np.asarray(x)[0].T.reshape(KD, P, S).transpose(1, 0, 2))

    def cols(v):
        v = np.asarray(v)
        v = v.reshape(L, -1, P)
        return v.transpose(0, 2, 1)

    arr["xT"] = fm(i["x"])
    arr["memT"] = fm(i["mem_2"])
    arr["positions"] = np.ascontiguousarray(np.asarray(i["positions_2"]).reshape(S))
    w = np.asarray(i["w_in_2"])
    rope = w[:, :, 384:416]
    swapped = np.concatenate([rope[:, :, 16:], rope[:, :, :16]], axis=2)
    narrow = np.zeros((L, D, P), w.dtype)
    narrow[:, :, 0:16] = w[:, :, 1952:1968]
    narrow[:, :, 32:64] = w[:, :, 3760:3792]
    arr["w_mix"] = np.concatenate([w[:, :, 0:384], narrow] + [rope] * 4 + [swapped] * 4 + [w[:, :, 416:1952],
                                  w[:, :, 1968:3760], w[:, :, 3792:]], axis=2)
    w = np.asarray(i["mla_w_uq_2"]).reshape(L, 256, MLA_HEADS, 96)
    parts = [w[..., :64], w[..., 64:], np.concatenate([w[..., 80:], w[..., 64:80]], axis=3)]
    arr["w_uq"] = np.concatenate([p.reshape(L, 256, -1) for p in parts], axis=2)
    w = np.asarray(i["mla_w_ukv_2"]).reshape(L, P, MLA_HEADS, 2, 64)
    arr["w_ukv"] = np.ascontiguousarray(w.transpose(0, 1, 3, 2, 4).reshape(L, P, -1))
    mu = np.asarray(i["rwkv_mu_2"])
    last = np.zeros((L, P), mu.dtype)
    last[:, 32:64] = mu[:, 1792:]
    arr["vec2"] = np.ascontiguousarray(np.concatenate(
        [cols(i["norm_g_2"]), cols(i["mem_norm_2"]), cols(i["mla_q_norm_2"]), cols(i["mla_kv_norm_2"]),
         cols(i["gla_b_alpha_2"]), cols(i["gla_norm_2"]), cols(mu[:, :1792]), cols(last)] +
        [cols(i["rwkv_" + n + "_2"]) for n in ("w0", "a0", "k_k", "k_a", "r_k", "ln_w", "ln_b")], axis=2))
    arr["vec1"] = np.ascontiguousarray(np.concatenate([cols(i["ln_g"]), cols(i["ln_b"]), cols(i["pool_scale"]),
                                                       cols(i["conv_w"])], axis=2))
    arr["rpb"] = np.ascontiguousarray(np.asarray(i["rpb"])[..., ::-1])
    for n in ("ffn1_w_gate", "ffn1_w_up", "ffn1_w_down", "ffn2_w_gate", "ffn2_w_up", "ffn2_w_down", "w_in", "pool_w",
              "w_out", "w_ffn_in_2", "w_ffn_out_2", "gla_w_alpha_2", "rwkv_w_decay_2", "rwkv_w_iclr_2",
              "rwkv_w_gate_2", "w_branch_2", "w_out_2", "mem_wq_2", "mem_wkv_2", "mem_wo_2"):
        arr[n] = np.ascontiguousarray(i[n])
    return arr


def kernel(**inputs):
    import concourse.bacc as bacc
    from concourse.bass_utils import run_bass_kernel_spmd

    nc = bacc.Bacc("TRN2", target_bir_lowering=False, num_devices=1, dynamic_dma_scratch_size=1024)
    arrays = host_arrays(inputs)
    aps = {n: nc.dram_tensor(f"in_{n}", v.shape, mybir.dt.from_np(v.dtype), kind="ExternalInput").ap()
           for n, v in arrays.items()}
    out = nc.dram_tensor("out_xT", (P, KD, S), F32, kind="ExternalOutput").ap()
    build(nc, aps, out)
    r = run_bass_kernel_spmd(nc, [{f"in_{n}": v for n, v in arrays.items()}], core_ids=[0])
    y = r.results[0]["out_xT"]
    return np.ascontiguousarray(y.transpose(1, 0, 2).reshape(D, S).T)[None]
```

```python
from contextlib import ExitStack

import concourse.bass as bass
import numpy as np
from concourse import mybir

F32 = mybir.dt.float32
F32R = mybir.dt.float32r
I32 = mybir.dt.int32
ACT = mybir.ActivationFunctionType
ALU = mybir.AluOpType
AX = mybir.AxisListType

P = 128
D = 1024
S = 256
LAYERS = 2
KD = D // P
F = 2816
TILES = F // P
ALPHA = (2.0 * LAYERS) ** 0.25
LN_EPS = 1e-5
RMS_EPS = 1e-6
NEG = -1e30

RAW, SPLIT = 6, 3
TOGETHER = 2
PIECE = 1024
FFN_PIECES = 3 * TILES
HALF = S // P

GRID = 64
NA_HEADS = 8
NA_COLS = 16
RPB_R, RPB_C = 15, 31
STRIPS = 6
POOL_PAD = 8
POOL_W = (2, 4, 8, 16)

V1 = {"ln_g": 0, "ln_b": 24, "pool_scale": 48, "conv_w": 50}
V1_N = 56


DECAY_SCALE = float(np.exp(-0.5))
GLA_GATE = 16.0
CHUNK = 64
CHUNKS = S // CHUNK
MIX_SLOTS, FIRST_SLOTS = 28, 3
FILL_GLA, FILL_RWKV, FILL_GATES = 3, 9, 16
Q_IN, Q_BRANCH, Q_OUT, Q_KV, Q_Q, Q_O = 0, 3, 7, 11, 19, 23
MLA_HEADS, MEM_HEADS, GLA_HEADS, RWKV_HEADS = 8, 4, 4, 8
PI = float(np.pi)
ROUND = 1.5 * 2.0 ** 23
TURN1 = 6.28125
TURN2 = float(np.float32(np.floor((2 * np.pi - TURN1) * 2.0 ** 21) / 2.0 ** 21))
TURN3 = float(np.float32(2 * np.pi - TURN1 - TURN2))
V2, V2_N = {}, 0
for _name, _width in (("norm_g", 64), ("mem_norm", 8), ("mla_q_norm", 2), ("mla_kv_norm", 1), ("gla_b_alpha", 2),
                      ("gla_norm", 1), ("rwkv_mu", 15), ("rwkv_w0", 4), ("rwkv_a0", 4), ("rwkv_k_k", 4),
                      ("rwkv_k_a", 4), ("rwkv_r_k", 4), ("rwkv_ln_w", 4), ("rwkv_ln_b", 4)):
    V2[_name] = V2_N
    V2_N += _width


def const_layout():
    at, n = {}, 0
    for name, width in (("ident", P), ("na_mask", GRID), ("pool_cnt", 2 * S), ("causal", 2 * S), ("eps_ln", 1), ("eps_ln4", 1),
                        ("eps_rms", 1), ("eps_gn", 1), ("eps_0", 1), ("inv_freq", 1),
                        ("rope_sign", 1), ("halves", P), ("gla_full", 256), ("gla_half", P), ("strict", P),
                        ("lower", CHUNK), ("eye2", CHUNK)):
        at[name] = n
        n += width
    return at, n


CONST, CONST_N = const_layout()


def constants():
    c = np.zeros((P, CONST_N), np.float32)

    def put(name, a):
        a = np.asarray(a, np.float32)
        c[:a.shape[0], CONST[name]:CONST[name] + a.shape[1]] = a

    put("ident", np.eye(P))
    col = np.arange(GRID)
    start = np.clip(col - NA_COLS // 2, 0, GRID - NA_COLS)
    ok = (col[None] >= start[:, None]) & (col[None] < start[:, None] + NA_COLS)
    put("na_mask", np.tile(np.where(ok, -NEG, NEG), (2, 1))[:, ::-1])
    t = np.arange(S)
    cnt = np.zeros((P, 2, S))
    for g, w in enumerate(POOL_W):
        n = np.clip(t - w // 2 + w, 0, S) - np.clip(t - w // 2, 0, S)
        cnt[64 * (g % 2):64 * (g % 2) + 64, g // 2] = 1.0 / n
    put("pool_cnt", cnt.reshape(P, -1))
    q = np.arange(P)[:, None, None] + P * np.arange(2)[None, :, None]
    put("causal", np.where(np.arange(S)[None, None] <= q, 0.0, NEG).reshape(P, -1))
    put("eps_ln", np.full((P, 1), LN_EPS))
    put("eps_ln4", np.full((P, 1), 4 * LN_EPS))
    put("eps_rms", np.full((P, 1), RMS_EPS))
    put("eps_gn", np.full((P, 1), 64e-5))
    freq = np.float32(10000.0) ** (-np.arange(0, 32, 2, dtype=np.float32) / np.float32(32))
    put("inv_freq", np.tile(freq.astype(np.float32), 8)[:, None])
    put("rope_sign", np.tile(np.repeat([-1.0, 1.0], 16), 4)[:, None])
    put("halves", np.kron(np.eye(2), np.ones((64, 64))))
    j, i = np.arange(P)[:, None], np.arange(CHUNK)[None]
    late = (j <= i + 64).astype(np.float32)
    put("gla_full", np.concatenate([late, np.ones((P, 2 * CHUNK)), late], axis=1))
    put("gla_half", np.tile(j[:64] <= i, (1, 2)))
    j = j % 64
    put("strict", np.concatenate([j < i, j <= i], axis=1))
    put("lower", j > i)
    put("eye2", j == i)
    return c


def build(nc, a, out, stop=None):
    ctx = ExitStack()
    with ctx:
        def sb(name, shape, dt=F32):
            return ctx.enter_context(nc.sbuf_tensor(name, shape, dt))

        sems = {}

        def sem(name):
            if name not in sems:
                sems[name] = ctx.enter_context(nc.semaphore(name))
            return sems[name]

        WHOLE = ("arrived", "all_arrived", "cleared", "x_here", "rope_here", "const_here", "first_gains_here", "first_here0",
                 "first_here1", "first_here2", "first_rest_here", "first_high", "first_low", "stored", "positions_here",
                 "pool_w_cleared", "rope_set", "angle_ready", "rope_sin", "rope_step", "ones_set")
        (arrived, all_arrived, cleared, x_here, rope_here, const_here, first_gains_here, first_here0,
         first_here1, first_here2, first_rest_here, first_high, first_low, stored, positions_here,
         sem_pw, rope_set, _, _, _, ones_set) = [sem(n) for n in WHOLE]

        ps = ctx.enter_context(nc.psum_tensor("ps", [P, 8, 512], F32))
        raw = sb("raw", [P, RAW, PIECE])
        w_hi, w_lo = (sb(n, [P, SPLIT, PIECE], F32R) for n in ("w_hi", "w_lo"))
        in_hi, in_lo = (sb(n, [P, KD, S], F32R) for n in ("in_hi", "in_lo"))
        hid_hi, hid_lo = (sb(n, [P, 2, S], F32R) for n in ("hid_hi", "hid_lo"))
        const = sb("const", [P, CONST_N])
        ones = sb("ones", [P, S])
        xT = sb("xT", [P, KD, S])
        zT = sb("zT", [P, KD, S])
        yT = sb("yT", [P, KD, S])
        sq = sb("sq", [P, KD, S])
        std = sb("std", [P, S])
        rstd = sb("rstd", [P, S])
        work = sb("work", [P, 16 * S])
        silu = work[:, 0:2 * S].rearrange("p (a t) -> p a t", a=2)
        hid = work[:, 2 * S:4 * S].rearrange("p (a t) -> p a t", a=2)
        gate_up = work[:, 4 * S:8 * S].rearrange("p (j a t) -> p j a t", j=2, a=2)
        att_p = work[:, 4 * S:12 * S].rearrange("p (b c t) -> p b c t", b=4, c=2)
        att_pT = work[:, 12 * S:16 * S].rearrange("p (b c t) -> p b c t", b=2, c=2)
        first_gains = sb("first_gains", [P, LAYERS, KD])
        first_gain = sb("first_gain", [P, KD])
        spare = sb("spare", [P, 1])
        vec1 = sb("vec1", [P, V1_N])
        att_max = sb("att_max", [P, 4, 2])
        att_sum = sb("att_sum", [P, 4, 2])
        att_rec = sb("att_rec", [P, 4, 2])
        pos_i = sb("pos_i", [P, S], I32)
        arena = sb("arena", [P, 23184])

        def view(lo, *shape, of=None):
            n = int(np.prod(shape))
            v = (arena if of is None else of)[:, lo:lo + n]
            names = "abcd"[:len(shape)]
            return v if len(shape) == 1 else v.rearrange(
                f"p ({' '.join(names)}) -> p {' '.join(names)}", **dict(zip(names[1:], shape[1:])))

        def cst(name, n, p=P):
            return const[0:p, CONST[name]:CONST[name] + n]

        ident = cst("ident", P)

        pool_in = view(0, 2, S + 2 * POOL_PAD)
        sum2 = view(544, 2, S + 2 * POOL_PAD)
        sum4 = view(1088, 2, S + 2 * POOL_PAD)
        sum8 = view(1632, 1, S + 2 * POOL_PAD)
        sum16 = view(1904, 1, S + 2 * POOL_PAD)
        pooled = view(2176, 2, S)
        gate_b = view(2688, 2, S)
        gate_c = view(3200, 2, S)
        conv_h = view(3712, 2, S)
        conv_z = view(4224, 2, S + 2)
        conv_y = view(4740, 2, S)
        na_q = view(5252, 4, S)
        na_k = view(6276, 4, S)
        na_v = view(7300, 2, 512)
        na_bias = view(8324, NA_HEADS, STRIPS * GRID)
        mix1 = view(11396, KD, S)
        pool_w = view(13444, 2, P)
        na_raw = view(16384, NA_HEADS * STRIPS, GRID)

        gates = view(0, 3 * KD, S)
        branch_in = view(6144, 3, 4, S)
        two_branches = branch_in[:, 0:2].rearrange("p b k t -> p (b k) t")
        o_mla, o_gla, o_rwkv = (branch_in[:, b] for b in range(3))
        w_uq = view(9216, 2, 1024)
        w_ukv = view(11264, 1024)
        w_alpha = view(12288, S)
        w_lora = view(12544, 512)
        w_rgate = view(13056, 2, 512)
        vec2 = view(14080, V2_N)
        cos = view(14208, S)
        sin = view(14464, S)
        c_q = view(14720, 2, S)
        c_kv = view(15232, 1, S)
        k_rope = view(15488, 2, S)
        gla_q = view(16000, 2, S)
        gla_k = view(16512, 2, S)
        gla_v = view(17024, 2, 512)
        gla_g = view(18048, 4, S)
        rz = view(19072, 15, S + 1)
        mla_qn = yT[:, 0:4, :]
        mla_qr = yT[:, 4:8, :]
        mla_kn = sq[:, 0:4, :]
        mla_v = sq[:, 4:8, :].rearrange("p (c k) t -> p c (k t)", c=2)
        gla_b = view(0, 2, S + 1, of=work)
        gla_ek = view(514, 2, 640, of=work)
        gla_kd = view(1794, 2, 640, of=work)
        gla_mid = view(3074, 2, 2, CHUNKS, of=work)
        gla_qd = view(3090, 2, S, of=work)
        gla_at = yT[:, :, :].rearrange("p k t -> p (k t)")[:, 0:4 * 384].rearrange("p (h c) -> p h c", h=4)
        gla_tmp = zT[:, 0:6, :].rearrange("p (a c) t -> p a c t", a=3)
        rw_pr = view(9216, 4, 2, S)
        rw_kh = view(11264, 4, S)
        rw_bh = view(14720, 4, S)
        rw_a = view(15744, 4, S)
        rw_kk = view(16768, 4, S)
        rw_L = view(17792, 4, S + 1)
        rw_edge = view(18820, 3, 4, CHUNKS)
        rw_c2 = (view(0, 4, 4, CHUNK, of=work), zT[:, 0:4, :].rearrange("p a (k t) -> p a k t", k=4))
        rw_g = view(1024, 2, 4, 2 * CHUNK, of=work)
        rw_tok = view(2048, 3, 4, CHUNK, of=work)
        rw_st = view(22928, 4, CHUNK)
        rw_pow = yT[:, 0:4, :].rearrange("p a (k t) -> p a k t", k=4)
        rw_t = yT[:, 4:6, :].rearrange("p a (k t) -> p a k t", k=4)
        rw_x = yT[:, 6, :].rearrange("p (k t) -> p k t", k=4)
        rw_u = yT[:, 7, :].rearrange("p (k t) -> p k t", k=4)
        rw_tmp = zT[:, 4:8, :]
        mem_n = view(14720, KD, S)
        mem_q = view(0, KD, S)
        mem_k = view(2048, KD, S)
        mem_v = view(4096, 2, D)
        mem_o = view(6144, KD, S)
        merged = gates[:, 0:KD, :]
        y_mla = yT[:, :, :]
        y_gla = view(0, KD, S, of=work)

        E1_FFN1, E1_IN, E1_OUT, E1_FFN2, E1_END = np.cumsum([0, FFN_PIECES, 20, 8, FFN_PIECES]).tolist()
        E_FFN1, E_IN, E_BRANCH, E_OUT, E_KV, E_Q, E_O, E_FFN2, E_END = \
            np.cumsum([0, FFN_PIECES, 2 * MIX_SLOTS, 12, 8, 16, 8, 8, FFN_PIECES]).tolist()
        E_FILL = E_IN + 2 * FIRST_SLOTS
        C1_FFN1, C1_IN, C1_OUT, C1_FFN2 = range(0, 16, 4)
        C_FFN1, C_IN, C_AB, C_RW, C_OUT, C_KV, C_Q, C_O, C_FFN2 = 0, 4, 8, 12, 14, 18, 22, 26, 30
        HERE = [sem(f"weights_here{s}") for s in range(RAW)]
        FIRST_HERE = [first_here0, first_here1, first_here2] + [first_rest_here] * (RAW - SPLIT)

        def mem_y(c):
            return two_tiles(4 + (Q_O + c) % 4)

        block = ctx.enter_context(nc.Block())

        def sp_load(sp, e, src, it=0):
            if e < RAW:
                return
            sp.wait_ge(sem("split_low"), e - RAW + 1 + it * RAW)
            sp.dma_start(raw_slot(e, src), src).then_inc(HERE[e % RAW], 16)

        def raw_slot(e, src):
            return raw[:, e % RAW, :].rearrange("p (k c) -> p k c", k=src.shape[1])

        def sp_first(sp, w_gate, w_up, w_down, before=None):
            for e, src in enumerate((w_gate(0), w_up(0), w_gate(P), w_up(P), w_down(0), w_gate(2 * P))):
                if before is not None:
                    sp.wait_ge(sem("split_low"), before - (before - 1 - e) % RAW)
                sp.dma_start(raw_slot(e, src), src).then_inc(FIRST_HERE[e], 16)
                if e == 0 and before is None:
                    sp.dma_start(xT[:, :, :], a["xT"]).then_inc(x_here, 16)

        def sp_ffn(sp, e0, w_gate, w_up, w_down):
            def tile(j, it=0):
                c = j * P + it * (2 * P)
                e = e0 + max(3 * j - 1, 0)
                sp_load(sp, e, w_gate(c), it)
                sp_load(sp, e + 1, w_up(c), it)
                if j:
                    sp_load(sp, e + 2, w_down((j - 1) * P + it * (2 * P)), it)

            tile(0)
            tile(1)
            tile(2)
            tile(3)
            with sp.Fori(0, TILES // 2 - 2) as it:
                tile(4, it)
                tile(5, it)
            sp_load(sp, e0 + FFN_PIECES - 1, w_down((TILES - 1) * P))

        def sp_linear(sp, e0, srcs):
            for i, src in enumerate(srcs):
                sp_load(sp, e0 + i, src)

        def three(o, left, right, first, last, **kw):
            (lh, ll), (rh, rl) = left, right
            nc.tensor.matmul(o, lh, rh, start=first, stop=False, **kw)
            nc.tensor.matmul(o, lh, rl, start=False, stop=False, **kw)
            return nc.tensor.matmul(o, ll, rh, start=False, stop=last, **kw)

        def piece(e, k=KD):
            return [w[:, e % SPLIT, :].rearrange("p (k c) -> p k c", k=k) for w in (w_hi, w_lo)]

        def at2(pair, *index):
            return [v[index] for v in pair]

        ALL = slice(None)
        given = (in_hi, in_lo)

        FFN_BANK = (7, 4)

        def pe_ffn(pe, n, e0, chunk, first=lambda: None):
            def begin():
                for c in range(KD // 2):
                    pe.wait_ge(sem("in_ready"), chunk + c + 1)
                    for i in range(TOGETHER):
                        if c == 0:
                            pe.wait_ge(sem("split_low"), e0 + i + 1)
                        w = piece(e0 + i)
                        for k in (2 * c, 2 * c + 1):
                            mm = three(ps[:, FFN_BANK[i // 2], i % 2 * S:(i % 2 + 1) * S], at2(w, ALL, k, ALL),
                                       at2(given, ALL, k, ALL), k == 0 and i % 2 == 0, k == KD - 1, skip_group_check=True)
                        if c == KD // 2 - 1:
                            mm.then_inc(sem("piece_used"), 1)

            def gate_up(j, it=0):
                for i in range(2):
                    if 2 * j + i < TOGETHER:
                        continue
                    e = e0 + max(3 * j - 1, 0) + i
                    pe.wait_ge(sem("split_low"), e + 1 + it * RAW)
                    w = piece(e)
                    for k in range(KD):
                        mm = three(ps[:, FFN_BANK[j % 2], i * S:(i + 1) * S], at2(w, ALL, k, ALL), at2(given, ALL, k, ALL),
                                   k == 0, k == KD - 1)
                    mm.then_inc(sem("piece_used"), 1)

            def down(j, it=0, last=False):
                e = e0 + (FFN_PIECES - 1 if last else 3 * j + 4)
                pe.wait_ge(sem("split_low"), e + 1 + it * RAW)
                pe.wait_ge(sem("hidden_ready"), n * TILES + j + 1 + it * 2)
                w = piece(e, 1)
                for i in range(KD):
                    mm = three(ps[:, i // 2, (i % 2) * S:(i % 2 + 1) * S], at2(w, ALL, 0, slice(i * P, (i + 1) * P)),
                               at2((hid_hi, hid_lo), ALL, j % 2, ALL), j == 0 and i % 2 == 0, last, skip_group_check=True)
                    if last and i in (1, 3, 5):
                        mm.then_inc(sem("ffn_out"), 1)
                mm.then_inc(sem("piece_used"), 1)

            begin()
            first()
            gate_up(1)
            down(0)
            with pe.Fori(0, TILES // 2 - 1) as it:
                for j in (2, 3):
                    gate_up(j, it)
                    down(j - 1, it)
            down(TILES - 1, last=True)

        def pe_linear(pe, q0, e0, groups, chunk, together=1):
            e, begun = e0, []
            for i, group in enumerate(groups):
                q = q0 + i
                if q >= 4:
                    pe.wait_ge(sem("linear_taken"), q - 3)
                for products in group(4 + q % 4, e):
                    pe.wait_ge(sem("split_low"), e + 1)
                    e += 1
                    begun.append(products)
                    if e < e0 + together:
                        continue
                    pairs = sorted({k // 2 for k, *_ in products})
                    for c in pairs:
                        if e == e0 + together:
                            pe.wait_ge(sem("in_ready"), chunk + c - pairs[0] + 1)
                        for one in begun:
                            for k, o, left, right, first, last in one:
                                if k // 2 == c:
                                    mm = three(o, left, right, first, last, skip_group_check=True)
                            if c == pairs[-1]:
                                mm.then_inc(sem("piece_used"), 1)
                    begun = []

        def features(bank, e):
            return [[(k, ps[:, bank, c * S:(c + 1) * S], at2(piece(e + c), ALL, k, ALL), at2(given, ALL, k, ALL),
                      k == 0 and c == 0, k == KD - 1) for k in range(KD)] for c in range(2)]

        def tokens(bank, e):
            return [[(k, ps[:, bank, t * S:(t + 1) * S], at2(given, ALL, k, slice(t * P, (t + 1) * P)),
                      at2(piece(e + c, KD // 2), ALL, k - KD // 2 * c, ALL), k == 0 and t == 0, k == KD - 1)
                     for t in range(HALF) for k in range(KD // 2 * c, KD // 2 * (c + 1))] for c in range(2)]

        def branch(tile):
            def group(bank, e):
                return [[(tile + k, ps[:, bank, c * S:(c + 1) * S], at2(piece(e, 4), ALL, k, slice(c * P, (c + 1) * P)),
                          at2(given, ALL, tile + k, ALL), k == 0 and c == 0, k == 3 and c == 1) for c in range(2) for k in range(4)]]
            return group

        def pe_branches(pe):
            pe.wait_ge(sem("filling_taken"), MIX_SLOTS - FIRST_SLOTS)
            for i in range(8):
                e = E_BRANCH + i
                if i >= 2:
                    pe.wait_ge(sem("branch_taken"), i - 1)
                if i % 4 == 0:
                    pe.wait_ge(sem("in_ready"), C_AB + 2 + i // 2)
                pe.wait_ge(sem("split_low"), e + 1)
                for _, o, left, right, first, last in branch(i // 4 * 4)(2 + i % 2, e)[0]:
                    mm = three(o, left, right, first, last)
                mm.then_inc(sem("piece_used"), 1)

        class Filling:

            def __init__(self, pe):
                self.pe, self.quarter = pe, 0

            def __call__(self, pieces):
                end = min(self.quarter + int(4 * pieces), 4 * (E_BRANCH - E_FILL))
                for x in range(self.quarter, end):
                    i, part = divmod(x, 4)
                    e = E_FILL + i
                    q, c = divmod(e - E_IN, 2)
                    if part == 0:
                        if c == 0 and q >= FIRST_SLOTS + 2:
                            self.pe.wait_ge(sem("filling_taken"), q - FIRST_SLOTS - 1)
                        self.pe.wait_ge(sem("split_low"), e + 1)
                    layout = tokens if FILL_GLA + 2 <= q < FILL_GLA + 4 else features
                    for _, o, left, right, first, last in layout(2 + q % 2, e - c)[c][2 * part:2 * part + 2]:
                        mm = three(o, left, right, first, last, skip_group_check=True)
                    if part == 3:
                        mm.then_inc(sem("piece_used"), 1)
                self.quarter = end

            def until(self, slot):
                self(2 * (slot - FIRST_SLOTS) - self.quarter / 4)

        def pe_stat(pe, bank, src, tag, chunk):
            for k in range(KD):
                if k % 2 == 0:
                    pe.wait_ge(sem(tag), chunk + k // 2 + 1)
                mm = nc.tensor.matmul(ps[:, bank, 0:S], ones[:, 0:P], src[:, k, :], start=(k == 0), stop=(k == KD - 1))
            mm.then_inc(sem("stat_sum"), 1)

        def pe_ln(pe, n, bank):
            pe_stat(pe, bank, zT, "ln_in", 4 * n)
            pe_stat(pe, bank + 1, sq, "ln_square", 4 * n)

        def two_tiles(bank):
            return ps[:, bank, :].rearrange("p (c t) -> p c t", c=2)

        def pe_attention(pe, tag, heads, scores, values, fill=lambda n: None):
            for i in range(heads + 3):
                if i < heads:
                    if i >= 2:
                        pe.wait_ge(sem(tag + "_biased"), i - 1)
                    for t in range(HALF):
                        pieces = scores(i, t)
                        for m, (q, k) in enumerate(pieces):
                            mm = nc.tensor.matmul(ps[:, 4 + i % 2, t * S:(t + 1) * S], q, k,
                                                  start=(m == 0), stop=(m == len(pieces) - 1))
                    mm.then_inc(sem(tag + "_scores"), 1)
                fill(1)
                h = i - 2
                if 0 <= h < heads:
                    pe.wait_ge(sem(tag + "_probs"), h + 1)
                    if h >= 2:
                        pe.wait_ge(sem(tag + "_turned"), h - 1)
                    for t in range(HALF):
                        for kt in range(HALF):
                            mm = nc.tensor.transpose(ps[:, 6 + h % 2, kt * S + t * P:kt * S + (t + 1) * P],
                                                     att_p[:, h % 4, t, kt * P:(kt + 1) * P], ident)
                    mm.then_inc(sem(tag + "_transposed"), 1)
                h = i - 3
                if 0 <= h < heads:
                    pe.wait_ge(sem(tag + "_turned"), h + 1)
                    if h >= 2:
                        pe.wait_ge(sem(tag + "_out"), h - 1)
                    for o, v in values(h):
                        for kt in range(HALF):
                            mm = nc.tensor.matmul(o, v(kt), att_pT[:, h % 2, kt, :], start=(kt == 0),
                                                  stop=(kt == HALF - 1))
                    mm.then_inc(sem(tag + "_values"), 1)

        def ffn_out(eng, n, end):
            return lambda c: eng.wait_ge(*((sem("ffn_out"), 3 * n + c + 1) if c < 3 else (sem("piece_used"), end)))

        def act_split(act, e, it=0):
            if e >= RAW:
                act.wait_ge(HERE[e % RAW], 16 * (e // RAW) + it * 16)
            if e >= SPLIT:
                act.wait_ge(sem("piece_used"), e - SPLIT + 1 + it * RAW)
            nc.scalar.activation(w_hi[:, e % SPLIT, :], raw[:, e % RAW, :], ACT.Copy).then_inc(sem("split_high"), 1)

        def act_in_split(act, n, src, ready, tile=0):
            for c in range(src.shape[1] // 2):
                ready(c)
                nc.scalar.activation(in_hi[:, tile + 2 * c:tile + 2 * c + 2, :], src[:, 2 * c:2 * c + 2, :], ACT.Copy)\
                    .then_inc(sem("in_high"), 1)

        def last_use(before, e):
            return before - (before - 1 - e) % SPLIT

        def first_order(before):
            return sorted(range(SPLIT), key=lambda e: last_use(before, e))

        def act_first(act, layer, pieces, before=None):
            for e in pieces:
                act.wait_ge(FIRST_HERE[e], 16 + layer * 16)
                if before is not None:
                    act.wait_ge(sem("piece_used"), last_use(before, e))
                nc.scalar.activation(w_hi[:, e, :], raw[:, e, :], ACT.Copy).then_inc(first_high, 1)

        def act_layer(act, layer):
            act.sem_inc(sem("split_high"), SPLIT)
            act.wait_ge(first_rest_here, 16 * (RAW - SPLIT) + layer * (16 * (RAW - SPLIT)))

        def act_silu_table(act):
            nc.scalar.activation(spare[:, :], ones[:, 0:1], ACT.Silu)

        def act_ffn(act, n, e0, end, first=None):
            def after(e, up=None, whole=None, it=0):
                if up is not None:
                    if up == 0 and first is not None:
                        first()
                    if first is not None:
                        act.wait_ge(sem("gate_up_scaled"), n * TILES + up + 1 + it * 2)
                        gate = gate_up[:, up % 2, 0, :]
                    else:
                        act.wait_ge(sem("piece_used"), e0 + e + 1 + it * RAW)
                        gate = ps[:, FFN_BANK[up % 2], 0:S]
                    nc.scalar.activation(silu[:, up % 2, :], gate, ACT.Silu).then_inc(sem("silu_ready"), 1)
                if e0 + e + SPLIT < end:
                    act_split(act, e0 + e + SPLIT, it)

            ffn_steps(act, after)

        def ffn_steps(eng, after):
            def tile(j, it=0):
                if j == 0:
                    after(0)
                    after(1, 0, 0)
                    return
                after(3 * j - 1, None, None, it)
                after(3 * j, j, None, it)
                after(3 * j + 1, None, j, it)

            tile(0)
            tile(1)
            with eng.Fori(0, TILES // 2 - 2) as it:
                tile(2, it)
                tile(3, it)
            tile(TILES - 2)
            tile(TILES - 1)
            after(FFN_PIECES - 1)

        def act_linear(act, q0, e0, dests, square=False):
            for i, dst in enumerate(dests):
                e = e0 + 2 * i
                act_split(act, e + SPLIT)
                act.wait_ge(sem("piece_used"), e + 2)
                src = two_tiles(4 + (q0 + i) % 4)
                if square:
                    nc.scalar.activation(sq[:, 2 * i:2 * i + 2, :], src, ACT.Square).then_inc(sem("rms_square"), 1)
                nc.scalar.activation(dst, src, ACT.Copy).then_inc(sem("linear_taken"), 1)
                act_split(act, e + 1 + SPLIT)

        class Taking:

            def __init__(self, act):
                self.act, self.quarter = act, 0

            def __call__(self, pieces):
                end = min(self.quarter + int(4 * pieces), 4 * (E_BRANCH - E_FILL))
                for x in range(self.quarter // 8, end // 8):
                    q = FIRST_SLOTS + x
                    self.act.wait_ge(sem("piece_used"), E_FILL + 2 * x + 2)
                    dst, f = self.dest(q)
                    nc.scalar.activation(dst, ps[:, 2 + q % 2, :].rearrange("p (c t) -> p c t", c=2), f)\
                        .then_inc(sem("filling_taken"), 1)
                self.quarter = end

            def until(self, slot):
                self(2 * (slot - FIRST_SLOTS) - self.quarter / 4)

            def dest(self, q):
                if q < FILL_GLA + 2:
                    return (gla_q, gla_k)[q - FILL_GLA][:, :, :], ACT.Copy
                if q < FILL_GLA + 4:
                    c = (q - FILL_GLA - 2) * S
                    return gla_v[:, :, c:c + S], ACT.Copy
                for first, end, dst, f in ((FILL_GLA + 4, FILL_RWKV, gla_g, ACT.Copy),
                                           (FILL_RWKV, FILL_GATES, rz[:, :, 1:], ACT.Copy),
                                           (FILL_GATES, MIX_SLOTS, gates, ACT.Sigmoid)):
                    if first <= q < end:
                        return dst[:, 2 * (q - first):2 * (q - first) + 2, :], f

        def act_std(act, s, n, bank, eps):
            act.wait_ge(sem("stat_sum"), s + 1)
            nc.scalar.activation(std[:, :], ps[:, bank, 0:S], ACT.Sqrt, bias=cst(eps, 1), scale=1.0 / D)\
                .then_inc(sem("stat_std"), 1)

        def act_ln(act, n, bank, eps):
            for c in range(KD // 2):
                act.wait_ge(sem("ln_centred"), 4 * n + c + 1)
                nc.scalar.activation(sq[:, 2 * c:2 * c + 2, :], zT[:, 2 * c:2 * c + 2, :], ACT.Square)\
                    .then_inc(sem("ln_square"), 1)
            act_std(act, 2 * n + 1, n, bank + 1, eps)

        def act_attention(act, tag, heads, outs, take=lambda n: None):
            for i in range(heads + 3):
                if i < heads:
                    act.wait_ge(sem(tag + "_biased"), i + 1)
                    for t in range(HALF):
                        e = nc.scalar.activation(att_p[:, i % 4, t, :], att_p[:, i % 4, t, :], ACT.Exp,
                                                 bias=att_max[:, i % 4, t:t + 1], accum_out=att_sum[:, i % 4, t:t + 1])
                        e.then_inc(sem(tag + "_exp"), 1)
                h = i - 2
                if 0 <= h < heads:
                    act.wait_ge(sem(tag + "_transposed"), h + 1)
                    if h >= 2:
                        act.wait_ge(sem(tag + "_values"), h - 1)
                    nc.scalar.activation(att_pT[:, h % 2, :, :], ps[:, 6 + h % 2, :].rearrange("p (c t) -> p c t", c=2),
                                         ACT.Copy).then_inc(sem(tag + "_turned"), 1)
                h = i - 3
                if 0 <= h < heads:
                    act.wait_ge(sem(tag + "_values"), h + 1)
                    dst, src = outs(h)
                    nc.scalar.activation(dst, src, ACT.Copy).then_inc(sem(tag + "_out"), 1)
                take(1)

        class Steps:

            def __init__(self, eng, name):
                self.eng, self.sem, self.n = eng, sem(name), 0

            def link(self, ins):
                self.n += 1
                ins.then_inc(self.sem, 1)
                self.eng.wait_ge(self.sem, self.n)

        def low_part(eng, e, it=0):
            eng.wait_ge(sem("split_high"), e + 1 + it * RAW)
            eng.tensor_tensor(w_lo[:, e % SPLIT, :], raw[:, e % RAW, :],
                                                 w_hi[:, e % SPLIT, :].bitcast(F32), ALU.subtract)\
                .then_inc(sem("split_low"), 1)

        def pool_low(pool, e0, n):
            if e0:
                pool.wait_ge(sem("split_low"), e0)
            if n >= RAW:
                with pool.Fori(0, n // RAW) as it:
                    for e in range(e0, e0 + RAW):
                        low_part(pool, e, it)
            for e in range(e0 + n // RAW * RAW, e0 + n):
                low_part(pool, e)

        def low_first(eng, layer, pieces):
            for i, e in enumerate(pieces):
                eng.wait_ge(first_high, i + 1 + layer * SPLIT)
                eng.tensor_tensor(w_lo[:, e, :], raw[:, e, :], w_hi[:, e, :].bitcast(F32), ALU.subtract)\
                    .then_inc(first_low, 1)

        def pool_layer(pool, layer):
            pool.wait_ge(first_low, SPLIT + layer * SPLIT)
            pool.sem_inc(sem("split_low"), SPLIT)

        def pool_filling(pool):
            one = ones[:, 0:1].broadcast_to([P, PIECE])
            pool.wait_ge(sem("split_high"), E_FILL)
            for e in range(E_FILL, E_BRANCH + SPLIT):
                pool.wait_ge(HERE[e % RAW], 16 * (e // RAW))
                pool.wait_ge(sem("piece_used"), e - SPLIT + 1)
                pool.tensor_tensor(w_hi[:, e % SPLIT, :], raw[:, e % RAW, :], one, ALU.mult).then_inc(sem("split_high"), 1)
                low_part(pool, e)

        def dve_in_split(dve, n, src, produce=None, tile=0):
            chunks = src.shape[1] // 2
            if produce is not None:
                produce(0)
            for c in range(chunks):
                if produce is not None and c + 1 < chunks:
                    produce(c + 1)
                dve.wait_ge(sem("in_high"), n + c + 1)
                lo, hi = tile + 2 * c, tile + 2 * c + 2
                nc.vector.tensor_tensor(in_lo[:, lo:hi, :], src[:, 2 * c:2 * c + 2, :], in_hi[:, lo:hi, :].bitcast(F32),
                                        ALU.subtract).then_inc(sem("in_ready"), 1)

        def pool_in_low(pool, n, src):
            for c in range(KD // 2):
                two = slice(2 * c, 2 * c + 2)
                pool.wait_ge(sem("in_high"), n + c + 1)
                pool.tensor_tensor(in_lo[:, two, :], src[:, two, :], in_hi[:, two, :].bitcast(F32), ALU.subtract)\
                    .then_inc(sem("in_ready"), 1)

        def dve_ffn(dve, n, e0, first=None):
            def hidden(whole, it):
                j, count = whole % 2, n * TILES + whole + 1 + it * 2
                dve.wait_ge(sem("silu_ready"), count)
                up_part = ps[:, FFN_BANK[j], S:2 * S] if first is None else gate_up[:, j, 1, :]
                nc.vector.tensor_tensor(hid[:, j, :], silu[:, j, :], up_part, ALU.mult)\
                    .then_inc(sem("hidden_whole"), 1)
                dve.wait_ge(sem("hidden_whole"), count)
                nc.vector.tensor_copy(hid_hi[:, j, :], hid[:, j, :]).then_inc(sem("hidden_high"), 1)
                dve.wait_ge(sem("hidden_high"), count)
                nc.vector.tensor_tensor(hid_lo[:, j, :], hid[:, j, :], hid_hi[:, j, :].bitcast(F32), ALU.subtract)\
                    .then_inc(sem("hidden_ready"), 1)

            def after(e, up=None, whole=None, it=0):
                if up is not None and first is not None:
                    if up == 0:
                        first()
                    dve.wait_ge(sem("piece_used"), e0 + e + 1 + it * RAW)
                    nc.vector.tensor_tensor(gate_up[:, up % 2, :, :], two_tiles(FFN_BANK[up % 2]), over_two(rstd[:, :]),
                                            ALU.mult).then_inc(sem("gate_up_scaled"), 1)
                if up == 0:
                    hidden(whole, it)
                if e + SPLIT < FFN_PIECES:
                    low_part(dve, e0 + e + SPLIT, it)
                if up is None and whole is not None:
                    hidden(whole, it)

            dve.wait_ge(sem("split_low"), e0 + SPLIT)
            ffn_steps(dve, after)

        def dve_inverse(dve, steps, n):
            dve.wait_ge(sem("stat_std"), n + 1)
            steps.link(nc.vector.reciprocal(rstd[:, :], std[:, :]))

        def over_two(v):
            return v.rearrange("p (o t) -> p o t", o=1).broadcast_to([P, 2, S])

        def dve_ln(dve, steps, n, bank, alpha, y, ready):
            pairs = [slice(2 * c, 2 * c + 2) for c in range(KD // 2)]
            for c, two in enumerate(pairs):
                ready(c)
                nc.vector.scalar_tensor_tensor(zT[:, two, :], xT[:, two, :], alpha, y(c), ALU.mult, ALU.add)\
                    .then_inc(sem("ln_in"), 1)
            dve.wait_ge(sem("stat_sum"), 2 * n + 1)
            dve.wait_ge(sem("ln_in"), 4 * n + 4)
            for two in pairs:
                nc.vector.scalar_tensor_tensor(zT[:, two, :], over_two(ps[:, bank, 0:S]), -1.0 / D, zT[:, two, :], ALU.mult,
                                               ALU.add)\
                    .then_inc(sem("ln_centred"), 1)
            dve_inverse(dve, steps, n)
            dve.wait_ge(sem("ln_centred"), 4 * n + 4)
            g, b = V1["ln_g"] + n * KD, V1["ln_b"] + n * KD

            def produce(c):
                steps.link(nc.vector.tensor_tensor(zT[:, pairs[c], :], zT[:, pairs[c], :], over_two(rstd[:, :]), ALU.mult))
                for k in (2 * c, 2 * c + 1):
                    ins = nc.vector.tensor_scalar(xT[:, k, :], zT[:, k, :], vec1[:, g + k:g + k + 1],
                                                  vec1[:, b + k:b + k + 1], ALU.mult, ALU.add)
                ins.then_inc(sem("x_ready"), 1)

            for c in range(KD // 2):
                produce(c)

        def dve_attention(dve, steps, tag, heads, scale, bias):
            for i in range(heads + 1):
                if i < heads:
                    dve.wait_ge(sem(tag + "_scores"), i + 1)
                    if i >= 4:
                        dve.wait_ge(sem(tag + "_transposed"), i - 3)
                    for t in range(HALF):
                        s = ps[:, 4 + i % 2, t * S:(t + 1) * S]
                        b = bias(i, t)
                        if b is None:
                            ins = nc.vector.tensor_scalar(att_p[:, i % 4, t, :], s, scale, None, ALU.mult)
                        else:
                            ins = nc.vector.scalar_tensor_tensor(att_p[:, i % 4, t, :], s, scale, b, ALU.mult, ALU.add)
                    steps.link(ins)
                    nc.vector.tensor_reduce(att_max[:, i % 4, :], att_p[:, i % 4, :, :], AX.X, ALU.max,
                                            negate=True).then_inc(sem(tag + "_biased"), 1)
                h = i - 1
                if 0 <= h < heads:
                    dve.wait_ge(sem(tag + "_exp"), HALF * (h + 1))
                    steps.link(nc.vector.reciprocal(att_rec[:, h % 4, :], att_sum[:, h % 4, :]))
                    for t in range(HALF):
                        ins = nc.vector.tensor_scalar(att_p[:, h % 4, t, :], att_p[:, h % 4, t, :],
                                                      att_rec[:, h % 4, t:t + 1], None, ALU.mult)
                    ins.then_inc(sem(tag + "_probs"), 1)

        def col2(name, i=0, p=P, lo=0):
            return vec2[lo:lo + p, V2[name] + i:V2[name] + i + 1]

        def bank2(b, p=P, lo=0):
            return ps[lo:lo + p, b:b + 2, :].rearrange("p b (c t) -> p (b c) t", c=2)

        RMS_BANK = (6, 6, 7, 2, 0, 1, 0, 6, 6)

        def pe_rms(pe, n):
            pe_stat(pe, RMS_BANK[n], sq, "rms_square", 4 * n)

        def act_rms(act, n, src, ready):
            for c in range(KD // 2):
                ready(c)
                nc.scalar.activation(sq[:, 2 * c:2 * c + 2, :], src(c), ACT.Square).then_inc(sem("rms_square"), 1)

        def act_gained(act, ready, gain, whole=None):
            for c in range(KD // 2):
                ready(c)
                for k in (2 * c, 2 * c + 1):
                    if whole is not None:
                        nc.scalar.activation(whole[:, k, :], xT[:, k, :], ACT.Copy, scale=gain(k))
                    ins = nc.scalar.activation(in_hi[:, k, :], xT[:, k, :], ACT.Copy, scale=gain(k))
                ins.then_inc(sem("in_high"), 1)

        def act_rms_std(act, n):
            act_std(act, n, n, RMS_BANK[n], "eps_rms")

        def dve_rms(dve, steps, n, src, gain, dst, chunk=None, tag="in_raw"):
            dve_inverse(dve, steps, n)

            def produce(c):
                for k in (2 * c, 2 * c + 1):
                    ins = nc.vector.scalar_tensor_tensor(dst[:, k, :], src[:, k, :], gain(k), rstd[:, :], ALU.mult,
                                                         ALU.mult)
                ins.then_inc(sem(tag), 1)

            if chunk is not None:
                dve_in_split(dve, chunk, dst, produce)
            else:
                for c in range(KD // 2):
                    produce(c)

        def dve_residual(dve, steps, n, r, y, gain, scale):
            dve_inverse(dve, steps, n)
            for c in range(KD // 2 + 1):
                if c < KD // 2:
                    for j in range(2):
                        k = 2 * c + j
                        ins = nc.vector.scalar_tensor_tensor(zT[:, k, :], y(c)[:, j, :], gain(k), rstd[:, :],
                                                             ALU.mult, ALU.mult)
                    ins.then_inc(sem("residual_scaled"), 1)
                if c:
                    dve.wait_ge(sem("residual_scaled"), 4 * r + c)
                    two = slice(2 * c - 2, 2 * c)
                    nc.vector.scalar_tensor_tensor(xT[:, two, :], zT[:, two, :], scale, xT[:, two, :], ALU.mult, ALU.add)\
                        .then_inc(sem("x_ready"), 1)

        ROPE = 32

        def pe_mla(pe, fill):
            fill(1)
            pe.wait_ge(sem("mla_square"), 2)
            for i, tiles in enumerate(((0, 1), (2,))):
                for t in tiles:
                    mm = nc.tensor.matmul(ps[:, 0, i * S:(i + 1) * S], ones[:, 0:P], sq[:, t, :], start=(t == tiles[0]),
                                          stop=(t == tiles[-1]))
            mm.then_inc(sem("mla_sum"), 1)
            fill(2)
            pe.wait_ge(sem("mla_normed"), 3)
            pe.wait_ge(sem("small_here"), 7 * 16)
            pe.wait_ge(sem("linear_taken"), FIRST_SLOTS)
            for t in (4, 5, 6, 7, 0, 1, 2, 3):
                for k in range(2):
                    mm = nc.tensor.matmul(ps[:, (0, 1, 4, 5)[t // 2], (t % 2) * S:(t % 2 + 1) * S], w_uq[:, k, t * P:(t + 1) * P],
                                          c_q[:, k, :], start=(k == 0), stop=(k == 1))
            mm.then_inc(sem("mla_q_ready"), 1)
            for t in range(4):
                nc.tensor.matmul(ps[:, 6 + t // 2, (t % 2) * S:(t % 2 + 1) * S], w_ukv[:, t * P:(t + 1) * P], c_kv[:, 0, :],
                                 start=True, stop=True)
            pe.wait_ge(sem("mla_taken"), 1)
            for t in range(HALF):
                mm = nc.tensor.matmul(ps[:, 4 + t, :], c_kv[:, 0, t * P:(t + 1) * P], w_ukv[:, 512:1024], start=True,
                                      stop=True)
            mm.then_inc(sem("mla_kv_ready"), 1)
            fill(1)
            pe.wait_ge(sem("mla_taken"), 4)
            pe.wait_ge(sem("mla_rope"), 2)

            def scores(h, t):
                o, r = 64 * (h % 2), ROPE * (h % 4)
                return [(mla_qn[o:o + 64, h // 2, t * P:(t + 1) * P], mla_kn[o:o + 64, h // 2, :]),
                        (mla_qr[r:r + ROPE, h // 4, t * P:(t + 1) * P], k_rope[r:r + ROPE, 0, :])]

            def values(h):
                o = 64 * (h % 2)
                return [(ps[o:o + 64, h % 2, 0:S], lambda kt: mla_v[:, kt, h * 64:(h + 1) * 64])]

            pe_attention(pe, "mla", MLA_HEADS, scores, values, fill)

        def act_mla(act, take):
            act.wait_ge(sem("linear_taken"), 2)
            act.wait_ge(sem("narrow_taken"), 1)
            nc.scalar.activation(sq[:, 0:2, :], c_q[:, :, :], ACT.Square).then_inc(sem("mla_square"), 1)
            nc.scalar.activation(sq[:, 2:3, :], c_kv[:, :, :], ACT.Square).then_inc(sem("mla_square"), 1)
            act.wait_ge(sem("mla_sum"), 1)
            nc.scalar.activation(zT[:, 0, :], ps[:, 0, 0:S], ACT.Sqrt, bias=cst("eps_rms", 1), scale=1.0 / 256)\
                .then_inc(sem("mla_std"), 1)
            nc.scalar.activation(zT[:, 1, :], ps[:, 0, S:2 * S], ACT.Sqrt, bias=cst("eps_rms", 1), scale=1.0 / P)\
                .then_inc(sem("mla_std"), 1)
            take(3)
            act.wait_ge(sem("mla_q_ready"), 1)
            nc.scalar.activation(mla_qr[:, :, :], bank2(4), ACT.Copy).then_inc(sem("mla_taken"), 1)
            nc.scalar.activation(mla_qn[:, :, :], bank2(0), ACT.Copy).then_inc(sem("mla_taken"), 1)
            act.wait_ge(sem("mla_kv_ready"), 1)
            nc.scalar.activation(mla_kn[:, :, :], bank2(6), ACT.Copy).then_inc(sem("mla_taken"), 1)
            nc.scalar.activation(mla_v[:, :, :], ps[:, 4:6, :], ACT.Copy).then_inc(sem("mla_taken"), 1)
            take(1)

            def outs(h):
                o = 64 * (h % 2)
                return o_mla[o:o + 64, h // 2, :], ps[o:o + 64, h % 2, 0:S]

            act_attention(act, "mla", MLA_HEADS, outs, take)

        def dve_mla(dve, steps):
            dve.wait_ge(sem("mla_std"), 2)
            steps.link(nc.vector.reciprocal(zT[:, 2:4, :], zT[:, 0:2, :]))
            for k in range(2):
                nc.vector.scalar_tensor_tensor(c_q[:, k, :], c_q[:, k, :], col2("mla_q_norm", k), zT[:, 2, :], ALU.mult,
                                               ALU.mult).then_inc(sem("mla_normed"), 1)
            nc.vector.scalar_tensor_tensor(c_kv[:, 0, :], c_kv[:, 0, :], col2("mla_kv_norm"), zT[:, 3, :], ALU.mult,
                                           ALU.mult).then_inc(sem("mla_normed"), 1)
            cos1, sin1 = cos.rearrange("p (o t) -> p o t", o=1), sin.rearrange("p (o t) -> p o t", o=1)
            dve.wait_ge(sem("linear_taken"), 3)
            for buf, n, ready in ((k_rope, 1, None), (mla_qr, 2, sem("mla_taken"))):
                if ready is not None:
                    dve.wait_ge(ready, 1)
                nc.vector.tensor_tensor(buf[:, 0:n, :], buf[:, 0:n, :], cos1.broadcast_to([P, n, S]), ALU.mult)
                steps.link(nc.vector.tensor_tensor(buf[:, n:2 * n, :], buf[:, n:2 * n, :], sin1.broadcast_to([P, n, S]),
                                                   ALU.mult))
                nc.vector.tensor_tensor(buf[:, 0:n, :], buf[:, 0:n, :], buf[:, n:2 * n, :], ALU.add)\
                    .then_inc(sem("mla_rope"), 1)
            causal = cst("causal", 2 * S)
            dve_attention(dve, steps, "mla", MLA_HEADS, 96 ** -0.5, lambda h, t: causal[:, t * S:(t + 1) * S])

        GLA_AT = [CHUNK * i * (i + 1) // 2 for i in range(CHUNKS)]
        PIECES = [(1, 0, P, 0), (2, 0, P, 64), (3, 0, P, 128), (3, 1, P, 192), (0, 0, 64, 256), (2, 1, 64, 320)]

        def pe_gla(pe, fill):
            for c in range(2):
                mm = nc.tensor.matmul(ps[:, 6, c * S:(c + 1) * S], w_alpha[0:16, c * P:(c + 1) * P], rz[0:16, 14, 1:],
                                      start=True, stop=True)
            mm.then_inc(sem("gla_logit"), 1)
            fill(4)
            pe.wait_ge(sem("gla_scaled"), 1)
            for h in range(GLA_HEADS):
                o, c = 64 * (h % 2), h // 2
                for i, jt, n, col in PIECES:
                    k0 = GLA_AT[i] + jt * P
                    mm = nc.tensor.matmul(ps[0:n, 4 + h, col:col + CHUNK], gla_kd[o:o + 64, c, k0:k0 + n],
                                          gla_qd[o:o + 64, c, i * CHUNK:(i + 1) * CHUNK], start=True, stop=True)
                mm.then_inc(sem("gla_scores"), 1)
            pe.wait_ge(sem("mla_out"), MLA_HEADS)
            pe.wait_ge(sem("filling_taken"), FILL_GLA + 4 - FIRST_SLOTS)
            for h in range(GLA_HEADS):
                fill(1)
                pe.wait_ge(sem("gla_masked"), h + 1)
                for i in range(CHUNKS):
                    mine = [x for x in PIECES if x[0] == i]
                    for m, (_, jt, n, col) in enumerate(mine):
                        out_at = (h % 2) * S + i * CHUNK
                        mm = nc.tensor.matmul(ps[:, h // 2, out_at:out_at + CHUNK], gla_v[0:n, jt, h * P:(h + 1) * P],
                                              gla_at[0:n, h, col:col + CHUNK], start=(m == 0), stop=(m == len(mine) - 1))
            mm.then_inc(sem("gla_out"), 1)
            fill(1)
            pe.wait_ge(sem("gla_square"), 1)
            for h in range(GLA_HEADS):
                mm = nc.tensor.matmul(ps[:, 4 + h // 2, (h % 2) * S:(h % 2 + 1) * S], ones[:, 0:P], sq[:, h, :],
                                      start=True, stop=True)
            mm.then_inc(sem("gla_sum"), 1)

        def act_gla(act, take):
            act.wait_ge(sem("gla_logit"), 1)
            for c in range(2):
                ins = nc.scalar.activation(gla_tmp[:, 0, c, :], ps[:, 6, c * S:(c + 1) * S], ACT.Abs, bias=col2("gla_b_alpha", c))
            ins.then_inc(sem("gla_log"), 1)
            act.wait_ge(sem("gla_log"), 1)
            nc.scalar.activation(gla_tmp[:, 0, :, :], gla_tmp[:, 0, :, :], ACT.Exp, scale=-1.0).then_inc(sem("gla_log"), 1)
            act.wait_ge(sem("gla_log"), 2)
            nc.scalar.activation(gla_tmp[:, 0, :, :], gla_tmp[:, 0, :, :], ACT.Ln, bias=1.0).then_inc(sem("gla_log"), 1)
            take(4)
            act.wait_ge(sem("gla_summed"), 1)
            for i in range(CHUNKS):
                for c in range(2):
                    n = CHUNK * (i + 1)
                    nc.scalar.activation(gla_ek[:, c, GLA_AT[i]:GLA_AT[i] + n], gla_b[:, c, 1:n + 1], ACT.Exp,
                                         bias=gla_mid[:, 0, c, i:i + 1], scale=-1.0 / GLA_GATE)
                    ins = nc.scalar.activation(gla_qd[:, c, i * CHUNK:(i + 1) * CHUNK],
                                               gla_b[:, c, i * CHUNK + 1:(i + 1) * CHUNK + 1], ACT.Exp,
                                               bias=gla_mid[:, 1, c, i:i + 1], scale=1.0 / GLA_GATE)
            ins.then_inc(sem("gla_decay"), 1)
            take(4)
            act.wait_ge(sem("filling_taken"), FILL_RWKV - FIRST_SLOTS)
            nc.scalar.activation(gla_g[:, :, :], gla_g[:, :, :], ACT.Silu).then_inc(sem("gla_gate"), 1)
            act.wait_ge(sem("gla_out"), 1)
            nc.scalar.activation(sq[:, 0:4, :], bank2(0), ACT.Square).then_inc(sem("gla_square"), 1)
            take(1)
            act.wait_ge(sem("gla_sum"), 1)
            nc.scalar.activation(zT[:, 0:4, :], bank2(4), ACT.Sqrt, bias=cst("eps_rms", 1), scale=1.0 / P)\
                .then_inc(sem("gla_std"), 1)

        def dve_gla(dve, steps):
            dve.wait_ge(sem("gla_log"), 1)
            steps.link(nc.vector.memset(gla_b[:, :, 0:1], 0.0))
            for c in range(2):
                ins = nc.vector.tensor_scalar(gla_tmp[:, 1, c, :], ps[:, 6, c * S:(c + 1) * S], col2("gla_b_alpha", c), 0.0,
                                              ALU.add, ALU.min)
            steps.link(ins)
            dve.wait_ge(sem("gla_log"), 3)
            steps.link(nc.vector.tensor_tensor(gla_tmp[:, 1, :, :], gla_tmp[:, 1, :, :], gla_tmp[:, 0, :, :], ALU.subtract))
            for c in range(2):
                ins = nc.vector.tensor_tensor_scan(gla_b[:, c, 1:], ones[:, :], gla_tmp[:, 1, c, :], 0.0, ALU.mult, ALU.add)
            steps.link(ins)
            mid = gla_b[:, :, 1:].rearrange("p c (n t) -> p c n t", t=CHUNK)[:, :, :, CHUNK // 2 - 1]
            nc.vector.tensor_scalar(gla_mid[:, 0, :, :], mid, 1.0 / GLA_GATE, None, ALU.mult)
            nc.vector.tensor_scalar(gla_mid[:, 1, :, :], mid, -1.0 / GLA_GATE, None, ALU.mult).then_inc(sem("gla_summed"), 1)
            dve.wait_ge(sem("gla_decay"), 1)
            dve.wait_ge(sem("filling_taken"), FILL_GLA + 2 - FIRST_SLOTS)
            for i in range(CHUNKS):
                n, at = CHUNK * (i + 1), GLA_AT[i]
                nc.vector.tensor_tensor(gla_kd[:, :, at:at + n], gla_ek[:, :, at:at + n], gla_k[:, :, 0:n], ALU.mult)
            nc.vector.scalar_tensor_tensor(gla_qd[:, :, :], gla_q[:, :, :], 64 ** -0.5, gla_qd[:, :, :], ALU.mult, ALU.mult)\
                .then_inc(sem("gla_scaled"), 1)
            for h in range(GLA_HEADS):
                dve.wait_ge(sem("gla_scores"), h + 1)
                nc.vector.tensor_tensor(gla_at[:, h, 0:256], ps[:, 4 + h, 0:256], cst("gla_full", 256), ALU.mult)
                nc.vector.tensor_tensor(gla_at[0:64, h, 256:384], ps[0:64, 4 + h, 256:384], cst("gla_half", P, 64), ALU.mult)\
                    .then_inc(sem("gla_masked"), 1)
        def dve_gla_end(dve, steps):
            dve.wait_ge(sem("gla_std"), 1)
            steps.link(nc.vector.reciprocal(zT[:, 0:4, :], zT[:, 0:4, :]))
            for b in range(2):
                ins = nc.vector.scalar_tensor_tensor(o_gla[:, 2 * b:2 * b + 2, :],
                                                     ps[:, b, :].rearrange("p (c t) -> p c t", c=2), col2("gla_norm"),
                                                     zT[:, 2 * b:2 * b + 2, :], ALU.mult, ALU.mult)
            steps.link(ins)
            dve.wait_ge(sem("gla_gate"), 1)
            nc.vector.tensor_tensor(o_gla, o_gla, gla_g[:, :, :], ALU.mult).then_inc(sem("gla_done"), 1)

        POWERS = 5
        W = CHUNK

        HEADS = [(t, slice(64 * half, 64 * half + 64)) for t in range(4) for half in range(2)]

        def pe_halves(pe, src, bank):
            for t in range(4):
                mm = nc.tensor.matmul(ps[:, bank + t // 2, (t % 2) * S:(t % 2 + 1) * S], cst("halves", P), src(t), start=True,
                                      stop=True)
            return mm

        def four(bank):
            return ps[:, bank, 0:4 * W].rearrange("p (t c) -> p t c", t=4)

        def pe_rwkv(pe, fill):
            fill.until(FILL_GATES)
            fill(5)
            pe.wait_ge(sem("rw_tanh"), 1)
            for t in range(4):
                nc.tensor.matmul(ps[:, 4 + t // 2, (t % 2) * S:(t % 2 + 1) * S], w_lora[0:64, t * P:(t + 1) * P],
                                 rz[0:64, 12, 1:], start=True, stop=True)
            for t in range(4):
                mm = nc.tensor.matmul(ps[:, 6 + t // 2, (t % 2) * S:(t % 2 + 1) * S], w_lora[64:P, t * P:(t + 1) * P],
                                      rz[64:P, 12, 1:], start=True, stop=True)
            mm.then_inc(sem("rw_logits"), 1)
            fill(1)
            pe.wait_ge(sem("rw_square"), 1)
            pe.wait_ge(sem("gla_done"), 1)
            pe_halves(pe, lambda t: sq[:, t, :], 0).then_inc(sem("rw_norm"), 1)
            fill(7)
            pe.wait_ge(sem("rw_scaled"), 1)
            pe.wait_ge(sem("rw_sigmoid"), 8)
            for n in range(CHUNKS):
                at = slice(n * W, (n + 1) * W)
                pe.wait_ge(sem("rw_chunk_in"), n + 1)
                rw_c = rw_c2[n % 2]
                for t, o in HEADS:
                    for b, src in enumerate((rz[o, 8 + t, 1 + n * W:1 + (n + 1) * W], rw_c[o, 2, t, :], rw_c[o, 3, t, :])):
                        col = (b % 2) * 4 * W + t * W
                        mm = nc.tensor.matmul(ps[o, b // 2, col:col + W], src, const[o, CONST["ident"] + o.start:
                                              CONST["ident"] + o.stop], start=True, stop=True)
                mm.then_inc(sem("rw_turned"), 1)
                if n:
                    pe.wait_ge(sem("rw_y_taken"), n)
                for t, o in HEADS:
                    for bank, keys in ((4, rw_bh), (6, rw_kh)):
                        nc.tensor.matmul(ps[o, bank, 2 * W * t:2 * W * (t + 1)].rearrange("p (a c) -> p a c", a=2),
                                         keys[o, t, at], rw_pr[o, t, :, at], start=True, stop=True)
                    mm = nc.tensor.matmul(ps[o, 7, t * W:(t + 1) * W], rw_pr[o, t, 0, at], rw_bh[o, t, at], start=True,
                                          stop=True)
                mm.then_inc(sem("rw_grams"), 1)
                fill(1)
                pe.wait_ge(sem("rw_grams_taken"), n + 1)

                def power(i, t, o):
                    return (rw_pow[o, 2 * (i % 2), t, :],
                            rw_pow[o, 2 * (i % 2) + 1, t, :] if i else rw_g[o, 0, t, 0:W])

                pe.wait_ge(sem("rw_tok"), 2 * (n + 1))
                pe.wait_ge(sem("rw_state"), n + 1)
                for t, o in HEADS:
                    x = ps[o, 7, t * W:(t + 1) * W]
                    nc.tensor.matmul(x, rw_c[o, 0, t, :], rw_st[o, t, :], start=True, stop=False)
                    mm = nc.tensor.matmul(x, rw_g[o, 1, t, 0:W], rw_tok[o, 0, t, :], start=False, stop=True)
                mm.then_inc(sem("rw_x"), 1)
                for i in range(1, POWERS + 1):
                    if i > 1:
                        pe.wait_ge(sem("rw_pow_a"), POWERS * n + i - 1)
                        pe.wait_ge(sem("rw_pow_b"), (POWERS - 1) * n + i - 1)
                    for t, o in HEADS:
                        a, b = power(i - 1, t, o)
                        mm = nc.tensor.matmul(ps[o, 0, t * W:(t + 1) * W], b, a, start=True, stop=True)
                        if i < POWERS:
                            mm = nc.tensor.matmul(ps[o, 1, t * W:(t + 1) * W], a, b, start=True, stop=True)
                    mm.then_inc(sem("rw_pow"), 1)
                    fill(0.25)
                    pe.wait_ge(sem("rw_pow_a"), POWERS * n + i)
                    if i > 1:
                        pe.wait_ge(sem("rw_inv"), POWERS * n + i - 1)
                    for t, o in HEADS:
                        mm = nc.tensor.matmul(ps[o, 5, t * W:(t + 1) * W], power(i, t, o)[0], rw_t[o, (i - 1) % 2, t, :],
                                              start=True, stop=True)
                    mm.then_inc(sem("rw_inv_mm"), 1)
                pe.wait_ge(sem("rw_x_taken"), n + 1)
                pe.wait_ge(sem("rw_inv"), POWERS * (n + 1))
                for t, o in HEADS:
                    mm = nc.tensor.matmul(ps[o, 0, t * W:(t + 1) * W], rw_t[o, POWERS % 2, t, :], rw_x[o, t, :], start=True,
                                          stop=True)
                mm.then_inc(sem("rw_u"), 1)
                for t, o in HEADS:
                    y, state = ps[o, 4, t * W:(t + 1) * W], ps[o, 5, t * W:(t + 1) * W]
                    nc.tensor.matmul(y, rw_st[o, t, :], rw_c[o, 1, t, :], start=(t == 0), stop=False, skip_group_check=True)
                    nc.tensor.matmul(y, rw_tok[o, 0, t, :], rw_g[o, 1, t, W:2 * W], start=False, stop=False,
                                     skip_group_check=True)
                    nc.tensor.matmul(state, rw_tok[o, 1, t, :], rw_tok[o, 0, t, :], start=(t == 0), stop=False,
                                     skip_group_check=True)
                pe.wait_ge(sem("rw_u_taken"), n + 1)
                for t, o in HEADS:
                    y, state = ps[o, 4, t * W:(t + 1) * W], ps[o, 5, t * W:(t + 1) * W]
                    nc.tensor.matmul(y, rw_u[o, t, :], rw_g[o, 0, t, W:2 * W], start=False, stop=True, skip_group_check=True)
                    mm = nc.tensor.matmul(state, rw_tok[o, 2, t, :], rw_u[o, t, :], start=False, stop=True,
                                          skip_group_check=True)
                mm.then_inc(sem("rw_y"), 1)
            fill.until(MIX_SLOTS)
            pe.wait_ge(sem("rw_y_taken"), CHUNKS)
            pe_halves(pe, lambda t: rw_kk[:, t, :], 0).then_inc(sem("gn_mean"), 1)
            pe.wait_ge(sem("rw_bonus"), 1)
            pe.wait_ge(sem("rw_state"), CHUNKS + 1)
            pe_halves(pe, lambda t: rw_bh[:, t, :], 4).then_inc(sem("rw_bonus_sum"), 1)
            for t in range(4):
                o = ps[:, 6 + t // 2, (t % 2) * S:(t % 2 + 1) * S]
                nc.tensor.matmul(o, w_rgate[:, 0, t * P:(t + 1) * P], rz[:, 13, 1:], start=True, stop=False)
                mm = nc.tensor.matmul(o, w_rgate[32:64, 1, t * P:(t + 1) * P], rz[32:64, 14, 1:], start=False, stop=True)
            mm.then_inc(sem("rw_gate"), 1)
            pe.wait_ge(sem("gn_square"), 1)
            pe_halves(pe, lambda t: sq[:, t, :], 0).then_inc(sem("gn_var"), 1)
            pe_branches(pe)

        def act_rwkv(act, take):
            take.until(FILL_GATES)
            act.wait_ge(sem("rw_mixed"), 15)
            nc.scalar.activation(rz[0:64, 12, 1:], rz[0:64, 12, 1:], ACT.Tanh).then_inc(sem("rw_tanh"), 1)
            nc.scalar.activation(rz[:, 13, 1:], rz[:, 13, 1:], ACT.Sigmoid).then_inc(sem("rw_gate_in"), 1)
            nc.scalar.activation(rz[32:64, 14, 1:], rz[32:64, 14, 1:], ACT.Sigmoid).then_inc(sem("rw_gate_in"), 1)
            take(5)
            act.wait_ge(sem("rw_logits"), 1)
            for t in range(4):
                nc.scalar.activation(rw_tmp[:, t, :], ps[:, 4 + t // 2, (t % 2) * S:(t % 2 + 1) * S], ACT.Sigmoid,
                                     bias=col2("rwkv_w0", t)).then_inc(sem("rw_sigmoid"), 1)
            for t in range(4):
                nc.scalar.activation(rw_a[:, t, :], ps[:, 6 + t // 2, (t % 2) * S:(t % 2 + 1) * S], ACT.Sigmoid,
                                     bias=col2("rwkv_a0", t)).then_inc(sem("rw_sigmoid"), 1)
            take(1)
            act.wait_ge(sem("rw_kk_raw"), 4)
            nc.scalar.activation(sq[:, 0:4, :], rw_kk[:, :, :], ACT.Square).then_inc(sem("rw_square"), 1)
            act.wait_ge(sem("rw_norm"), 1)
            nc.scalar.activation(zT[:, 0:4, :], bank2(0), ACT.Sqrt, bias=cst("eps_0", 1)).then_inc(sem("rw_norm_root"), 1)
            act.wait_ge(sem("rw_logs"), 1)
            nc.scalar.activation(rw_pr[:, :, 1, :], rw_bh[:, :, :], ACT.Exp, scale=-DECAY_SCALE)
            nc.scalar.activation(rw_kh[:, :, :], rw_bh[:, :, :], ACT.Exp, scale=DECAY_SCALE)
            nc.scalar.activation(rw_edge[:, 0:2], rw_edge[:, 0:2], ACT.Exp, scale=-DECAY_SCALE)
            nc.scalar.activation(rw_pr[:, :, 0, :], rw_pr[:, :, 0, :], ACT.Exp, scale=-DECAY_SCALE)\
                .then_inc(sem("rw_decay"), 1)
            take(7)
            for n in range(CHUNKS):
                act.wait_ge(sem("rw_turned"), n + 1)
                nc.scalar.activation(rw_tok[:, 0:2], ps[:, 0, :].rearrange("p (b t c) -> p b t c", b=2, t=4), ACT.Copy)\
                    .then_inc(sem("rw_tok"), 1)
                nc.scalar.activation(rw_tok[:, 2], four(1), ACT.Copy).then_inc(sem("rw_tok"), 1)
                take(1)
                act.wait_ge(sem("rw_x"), n + 1)
                nc.scalar.activation(rw_x, four(7), ACT.Copy).then_inc(sem("rw_x_taken"), 1)
                for i in range(1, POWERS + 1):
                    act.wait_ge(sem("rw_pow"), POWERS * n + i)
                    nc.scalar.activation(rw_pow[:, 2 * (i % 2)], four(0), ACT.Copy).then_inc(sem("rw_pow_a"), 1)
                    take(0.25)
                act.wait_ge(sem("rw_y"), n + 1)
                nc.scalar.activation(rw_kk[:, :, n * W:(n + 1) * W], four(4), ACT.Copy).then_inc(sem("rw_y_taken"), 1)
            take.until(MIX_SLOTS)

            def heads_done(c):
                act.wait_ge(*((sem("mla_out"), MLA_HEADS) if c < 2 else (sem("gla_done"), 1)))
                act.wait_ge(sem("piece_used"), E_BRANCH)

            act_in_split(act, C_AB, two_branches, heads_done)
            act.wait_ge(sem("gn_centred"), 1)
            nc.scalar.activation(sq[:, 0:4, :], rw_kk[:, :, :], ACT.Square).then_inc(sem("gn_square"), 1)
            act.wait_ge(sem("gn_var"), 1)
            nc.scalar.activation(zT[:, 4:8, :], bank2(0), ACT.Sqrt, bias=cst("eps_gn", 1), scale=1.0 / 64)\
                .then_inc(sem("gn_std"), 1)
            act.wait_ge(sem("split_high"), E_BRANCH + SPLIT)
            for i in range(8):
                act_split(act, E_BRANCH + i + SPLIT)
                act.wait_ge(sem("piece_used"), E_BRANCH + i + 1)
                dst = (y_mla, y_gla)[i // 4][:, 2 * (i % 4):2 * (i % 4) + 2, :]
                nc.scalar.activation(dst, two_tiles(2 + i % 2), ACT.Copy).then_inc(sem("branch_taken"), 1)

        def dve_rwkv(dve, steps):
            r, k, v = (rz[:, 4 * i:4 * i + 4, 1:] for i in range(3))
            dve.wait_ge(sem("filling_taken"), FILL_GATES - FIRST_SLOTS)
            dve.wait_ge(sem("gla_out"), 1)
            diff = view(0, 15, S, of=work)
            steps.link(nc.vector.tensor_tensor(diff, rz[:, :, 0:S], rz[:, :, 1:], ALU.subtract))
            for t in range(15):
                lo, n = (0, P) if t < 14 else (32, 32)
                nc.vector.scalar_tensor_tensor(rz[lo:lo + n, t, 1:], diff[lo:lo + n, t, :], col2("rwkv_mu", t, n, lo),
                                               rz[lo:lo + n, t, 1:], ALU.mult, ALU.add).then_inc(sem("rw_mixed"), 1)
            dve.wait_ge(sem("rw_mixed"), 15)
            for t in range(4):
                nc.vector.tensor_scalar(rw_kk[:, t, :], k[:, t, :], col2("rwkv_k_k", t), None, ALU.mult)\
                    .then_inc(sem("rw_kk_raw"), 1)
            dve_gla_end(dve, steps)
            dve.wait_ge(sem("gla_done"), 1)
            steps.link(nc.vector.memset(rw_L[:, :, 0:1], 0.0))
            steps.link(nc.vector.memset(rw_st[:, :, :], 0.0))
            dve.wait_ge(sem("rw_sigmoid"), 8)
            for t in range(4):
                ins = nc.vector.tensor_tensor_scan(rw_L[:, t, 1:], ones[:, :], rw_tmp[:, t, :], 0.0, ALU.mult, ALU.add)
            steps.link(ins)
            inc = rw_L[:, :, 1:].rearrange("p c (n t) -> p c n t", t=W)
            exc = rw_L[:, :, 0:S].rearrange("p c (n t) -> p c n t", t=W)
            mid = inc[:, :, :, W // 2 - 1:W // 2]
            nc.vector.tensor_tensor(rw_bh[:, :, :].rearrange("p c (n t) -> p c n t", t=W), inc,
                                    mid.broadcast_to([P, 4, CHUNKS, W]), ALU.subtract)
            nc.vector.tensor_tensor(rw_pr[:, :, 0, :].rearrange("p c (n t) -> p c n t", t=W), exc,
                                    mid.broadcast_to([P, 4, CHUNKS, W]), ALU.subtract)
            nc.vector.tensor_tensor(rw_edge[:, 0], mid[:, :, :, 0], exc[:, :, :, 0], ALU.subtract)
            nc.vector.tensor_tensor(rw_edge[:, 1], inc[:, :, :, W - 1], mid[:, :, :, 0], ALU.subtract)\
                .then_inc(sem("rw_logs"), 1)
            dve.wait_ge(sem("rw_norm_root"), 1)
            steps.link(nc.vector.tensor_scalar(zT[:, 0:4, :], zT[:, 0:4, :], 1e-12, None, ALU.max))
            steps.link(nc.vector.reciprocal(zT[:, 0:4, :], zT[:, 0:4, :]))
            steps.link(nc.vector.tensor_tensor(rw_kk[:, :, :], rw_kk[:, :, :], zT[:, 0:4, :], ALU.mult))
            for t in range(4):
                ins = nc.vector.tensor_scalar(zT[:, t, :], rw_a[:, t, :], -1.0, col2("rwkv_k_a", t), ALU.add, ALU.mult)
            steps.link(ins)
            nc.vector.scalar_tensor_tensor(k, zT[:, 0:4, :], 1.0, k, ALU.add, ALU.mult)
            steps.link(nc.vector.scalar_tensor_tensor(rw_a[:, :, :], rw_kk[:, :, :], -1.0, rw_a[:, :, :], ALU.mult, ALU.mult))
            dve.wait_ge(sem("rw_decay"), 1)
            nc.vector.tensor_tensor(rw_pr[:, :, 0, :], rw_pr[:, :, 0, :], rw_kk[:, :, :], ALU.mult)
            nc.vector.tensor_tensor(rw_pr[:, :, 1, :], rw_pr[:, :, 1, :], r, ALU.mult)
            nc.vector.tensor_tensor(rw_edge[:, 2], rw_edge[:, 0], rw_edge[:, 1], ALU.mult)
            steps.link(nc.vector.tensor_tensor(rw_bh[:, :, :], rw_kh[:, :, :], rw_a[:, :, :], ALU.mult))
            steps.link(nc.vector.tensor_tensor(rw_kh[:, :, :], rw_kh[:, :, :], k, ALU.mult))
            nc.vector.tensor_copy(rw_tmp[:, 0, 0:1], rw_st[:, 0, 0:1]).then_inc(sem("rw_scaled"), 1)
            dve.sem_inc(sem("rw_state"), 1)

            def edge(e, n):
                return rw_edge[:, e, :, n:n + 1].broadcast_to([P, 4, W])

            def chunk_in(n):
                at, rw_c = slice(n * W, (n + 1) * W), rw_c2[n % 2]
                nc.vector.tensor_tensor(rw_c[:, 0], rw_pr[:, :, 0, at], edge(0, n), ALU.mult)
                nc.vector.tensor_tensor(rw_c[:, 1], rw_pr[:, :, 1, at], edge(0, n), ALU.mult)
                nc.vector.tensor_tensor(rw_c[:, 2], rw_kh[:, :, at], edge(1, n), ALU.mult)
                nc.vector.tensor_tensor(rw_c[:, 3], rw_bh[:, :, at], edge(1, n), ALU.mult).then_inc(sem("rw_chunk_in"), 1)

            chunk_in(0)
            for n in range(CHUNKS):
                dve.wait_ge(sem("rw_grams"), n + 1)
                def blocks(name, w):
                    return cst(name, w).rearrange("p (o c) -> p o c", o=1).broadcast_to([P, 4, w])

                for b in range(2):
                    ins = nc.vector.tensor_tensor(rw_g[:, b], ps[:, 4 + 2 * b, :].rearrange("p (h c) -> p h c", h=4),
                                                  blocks("strict", 2 * W), ALU.mult)
                steps.link(ins)
                nc.vector.tensor_tensor(rw_t[:, 0], rw_g[:, 0, :, 0:W], blocks("eye2", W), ALU.add)
                nc.vector.tensor_tensor(rw_pow[:, 0], four(7), blocks("lower", W), ALU.mult)\
                    .then_inc(sem("rw_grams_taken"), 1)
                for i in range(1, POWERS + 1):
                    if i < POWERS:
                        dve.wait_ge(sem("rw_pow"), POWERS * n + i)
                        nc.vector.tensor_copy(rw_pow[:, 2 * (i % 2) + 1], four(1)).then_inc(sem("rw_pow_b"), 1)
                    dve.wait_ge(sem("rw_inv_mm"), POWERS * n + i)
                    if i > 1:
                        dve.wait_ge(sem("rw_inv"), POWERS * n + i - 1)
                    nc.vector.tensor_tensor(rw_t[:, i % 2], four(5), rw_t[:, (i - 1) % 2], ALU.add)\
                        .then_inc(sem("rw_inv"), 1)
                    if i == 1 and n + 1 < CHUNKS:
                        chunk_in(n + 1)
                dve.wait_ge(sem("rw_u"), n + 1)
                nc.vector.tensor_copy(rw_u, four(0)).then_inc(sem("rw_u_taken"), 1)
                dve.wait_ge(sem("rw_y"), n + 1)
                steps.link(nc.vector.tensor_tensor(rw_st[:, :, :], rw_st[:, :, :], edge(2, n), ALU.mult))
                nc.vector.tensor_tensor(rw_st[:, :, :], rw_st[:, :, :], four(5), ALU.add).then_inc(sem("rw_state"), 1)
                dve.wait_ge(sem("rw_state"), n + 2)
            for t in range(4):
                ins = nc.vector.scalar_tensor_tensor(rw_bh[:, t, :], r[:, t, :], col2("rwkv_r_k", t), k[:, t, :], ALU.mult,
                                                     ALU.mult)
            ins.then_inc(sem("rw_bonus"), 1)
            dve.wait_ge(sem("gn_mean"), 1)
            steps.link(nc.vector.tensor_scalar(zT[:, 0:4, :], bank2(0), 1.0 / 64, None, ALU.mult))
            nc.vector.tensor_tensor(rw_kk[:, :, :], rw_kk[:, :, :], zT[:, 0:4, :], ALU.subtract).then_inc(sem("gn_centred"), 1)
            dve_in_split(dve, C_AB, two_branches)
            dve.wait_ge(sem("gn_std"), 1)
            steps.link(nc.vector.reciprocal(zT[:, 0:4, :], zT[:, 4:8, :]))
            steps.link(nc.vector.tensor_tensor(rw_kk[:, :, :], rw_kk[:, :, :], zT[:, 0:4, :], ALU.mult))
            for t in range(4):
                nc.vector.tensor_scalar(rw_kk[:, t, :], rw_kk[:, t, :], col2("rwkv_ln_w", t), col2("rwkv_ln_b", t), ALU.mult,
                                        ALU.add)
            dve.wait_ge(sem("rw_bonus_sum"), 1)
            steps.link(nc.vector.tensor_tensor(zT[:, 0:4, :], v, bank2(4), ALU.mult))
            steps.link(nc.vector.tensor_tensor(rw_kk[:, :, :], rw_kk[:, :, :], zT[:, 0:4, :], ALU.add))
            dve.wait_ge(sem("rw_gate"), 1)
            nc.vector.tensor_tensor(o_rwkv, rw_kk[:, :, :], bank2(6), ALU.mult).then_inc(sem("rw_done"), 1)

        def layer_end(eng, n):
            eng.drain().then_inc(arrived, 1)
            if eng is not nc.sync:
                eng.wait_ge(cleared, n)
                return
            eng.wait_ge(arrived, 5 * n)
            eng.sem_inc(all_arrived, 1)
            ids = sorted(s.num for k, s in sems.items() if k not in WHOLE)
            assert ids == list(range(ids[0], ids[-1] + 1))
            eng.sem_clear(range(ids[0], ids[-1] + 1))
            eng.drain().then_inc(cleared, 1)

        @block.tensor
        def _(pe):
            pe.wait_ge(ones_set, 1)
            with pe.Fori(0, LAYERS) as l:
                pe_ffn(pe, 0, E1_FFN1, C1_FFN1)
                pe_ln(pe, 0, 6)
                pe_linear(pe, 0, E1_IN, [features] * 8 + [tokens] * 2, C1_IN, TOGETHER)
                pe.wait_ge(const_here, 32)
                pe.wait_ge(sem("pooled"), 1)
                pe.wait_ge(sem("pool_w_here"), 64)
                for c in range(2):
                    mm = nc.tensor.matmul(ps[:, 2, c * S:(c + 1) * S], pool_w[:, c, :], pooled[:, c, :],
                                          start=True, stop=True)
                mm.then_inc(sem("pool_ready"), 1)
                pe.wait_ge(sem("linear_taken"), 10)

                def scores(h, t):
                    o = 64 * (h % 2)
                    return [(na_q[o:o + 64, h // 2, t * P:(t + 1) * P], na_k[o:o + 64, h // 2, :])]

                def values(h):
                    o = 64 * (h % 2)
                    return [(ps[o:o + 64, h % 2, 0:S], lambda kt: na_v[:, kt, h * 64:(h + 1) * 64])]

                pe_attention(pe, "na", NA_HEADS, scores, values)
                pe_linear(pe, 10, E1_OUT, [features] * 4, C1_OUT, TOGETHER)
                pe_ln(pe, 1, 0)
                pe_ffn(pe, 1, E1_FFN2, C1_FFN2)
                pe_ln(pe, 2, 6)
                layer_end(pe, l + 1)
            with pe.Fori(0, LAYERS) as l:
                pe_ffn(pe, 0, E_FFN1, C_FFN1, lambda: pe_rms(pe, 0))
                pe_rms(pe, 1)
                pe_rms(pe, 2)
                pe_linear(pe, Q_IN, E_IN, [features] * FIRST_SLOTS, C_IN)
                fill = Filling(pe)
                pe_mla(pe, fill)
                pe_gla(pe, fill)
                pe_rwkv(pe, fill)
                pe.wait_ge(sem("mla_out"), MLA_HEADS)
                pe.wait_ge(sem("gla_done"), 1)
                pe.wait_ge(sem("rw_done"), 1)

                pe_linear(pe, Q_BRANCH, E_BRANCH + 8, [branch(0)] * 4, C_RW)
                pe_rms(pe, 3)
                pe_linear(pe, Q_OUT, E_OUT, [features] * 2, C_OUT)
                pe_linear(pe, Q_OUT + 2, E_OUT + 4, [features] * 2, C_OUT)
                pe_rms(pe, 4)
                pe.wait_ge(sem("linear_taken"), Q_KV)
                pe_linear(pe, Q_KV, E_KV, [features] * 2, C_KV)
                pe_linear(pe, Q_KV + 2, E_KV + 4, [features] * 2 + [tokens], C_KV)
                pe_rms(pe, 5)
                pe_linear(pe, Q_KV + 5, E_KV + 10, [tokens] * 2, C_KV)
                pe_linear(pe, Q_KV + 7, E_KV + 14, [tokens], C_KV)
                pe_linear(pe, Q_Q, E_Q, [features] * 4, C_Q)
                pe.wait_ge(sem("linear_taken"), Q_O)

                def mem_scores(h, t):
                    return [(mem_q[:, 2 * h + c, t * P:(t + 1) * P], mem_k[:, 2 * h + c, :]) for c in range(2)]

                def mem_values(h):
                    return [(ps[:, h % 2, c * S:(c + 1) * S],
                             lambda kt, c=c: mem_v[:, kt, (2 * h + c) * P:(2 * h + c + 1) * P]) for c in range(2)]

                pe_attention(pe, "mem", MEM_HEADS, mem_scores, mem_values)
                pe_linear(pe, Q_O, E_O, [features] * 4, C_O)
                pe_rms(pe, 6)
                pe_ffn(pe, 1, E_FFN2, C_FFN2, lambda: pe_rms(pe, 7))
                pe_rms(pe, 8)
                layer_end(pe, l + 1 + LAYERS)

        @block.scalar
        def _(act):
            act.wait_ge(sem("angle_ready"), 1)
            nc.scalar.activation(sin, sq[:, 2, :], ACT.Sin).then_inc(sem("rope_sin"), 1)
            nc.scalar.activation(sq[:, 3, :], sq[:, 2, :], ACT.Abs).then_inc(sem("rope_sin"), 1)
            act.wait_ge(sem("angle_ready"), 2)
            nc.scalar.activation(cos, sq[:, 4, :], ACT.Sin).then_inc(sem("rope_sin"), 1)
            act_first(act, 0, range(SPLIT))
            act.wait_ge(ones_set, 1)
            act.wait_ge(x_here, 16)
            with act.Fori(0, LAYERS) as l:
                act_silu_table(act)
                act_in_split(act, C1_FFN1, xT, lambda c: None)
                act_layer(act, l)
                act_ffn(act, 0, E1_FFN1, E1_END)
                act.wait_ge(const_here, 32)
                act_ln(act, 0, 6, "eps_ln4")
                act_in_split(act, C1_IN, xT, lambda c: act.wait_ge(sem("x_ready"), c + 1))
                act.wait_ge(sem("pool_pads"), 1)
                dests = [pool_in[:, :, POOL_PAD:POOL_PAD + S], gate_b[:, :, :], gate_c[:, :, :], conv_h[:, :, :],
                         na_q[:, 0:2, :], na_q[:, 2:4, :], na_k[:, 0:2, :], na_k[:, 2:4, :],
                         na_v[:, :, 0:S], na_v[:, :, S:2 * S]]
                act_linear(act, 0, E1_IN, dests)
                act.wait_ge(sem("pool_ready"), 1)
                for c in range(2):
                    nc.scalar.activation(mix1[:, c, :], ps[:, 2, c * S:(c + 1) * S], ACT.Copy,
                                         scale=vec1[:, V1["pool_scale"] + c:V1["pool_scale"] + c + 1])\
                        .then_inc(sem("pool_out"), 1)

                def outs(h):
                    o = 64 * (h % 2)
                    return mix1[o:o + 64, 4 + h // 2, :], ps[o:o + 64, h % 2, 0:S]

                act_attention(act, "na", NA_HEADS, outs)

                def mixed(c):
                    act.wait_ge(*((sem("pool_out"), 2), (sem("conv_out"), 1), (sem("na_out"), 6),
                                  (sem("na_out"), NA_HEADS))[c])

                act_in_split(act, C1_OUT, mix1, mixed)
                for e in range(E1_OUT, E1_FFN2):
                    act_split(act, e + SPLIT)
                act_ln(act, 1, 0, "eps_ln")
                act_silu_table(act)
                act_in_split(act, C1_FFN2, xT, lambda c: act.wait_ge(sem("x_ready"), KD // 2 + c + 1))
                act_ffn(act, 1, E1_FFN2, E1_END)
                order = first_order(E1_END)
                act_first(act, l + 1, order[:1], E1_END)
                act_ln(act, 2, 6, "eps_ln4")
                act_first(act, l + 1, order[1:], E1_END)
                layer_end(act, l + 1)
            def layer2(l, last):
                act_layer(act, l + LAYERS)
                x_pair = lambda c: xT[:, 2 * c:2 * c + 2, :]
                act.wait_ge(sem("first_gain"), 1)
                act_gained(act, lambda c: None, lambda k: first_gain[:, k:k + 1])
                act_rms(act, 0, x_pair, lambda c: None)
                in_raw = lambda n: lambda c: act.wait_ge(sem("in_raw"), 4 * n + c + 1)
                act_ffn(act, 0, E_FFN1, E_END, lambda: act_rms_std(act, 0))
                act.wait_ge(sem("gains_here"), 16)
                act_rms(act, 1, two_tiles, ffn_out(act, 0, E_IN))
                act_rms_std(act, 1)
                act_rms(act, 2, x_pair, lambda c: act.wait_ge(sem("x_ready"), c + 1))
                act_rms_std(act, 2)
                act_in_split(act, C_IN, zT, in_raw(0))
                for e in range(E_IN + SPLIT, E_FILL):
                    act_split(act, e)
                act.wait_ge(sem("rz_cleared"), 1)
                for q, dst in enumerate((c_q, None, k_rope)):
                    act.wait_ge(sem("piece_used"), E_IN + 2 * q + 2)
                    two = ps[:, 4 + q, :].rearrange("p (c t) -> p c t", c=2)
                    if q == 1:
                        nc.scalar.activation(c_kv[:, 0, :], two[:, 0, :], ACT.Copy).then_inc(sem("narrow_taken"), 1)
                        nc.scalar.activation(rz[:, 14, 1:], two[:, 1, :], ACT.Copy).then_inc(sem("linear_taken"), 1)
                    else:
                        nc.scalar.activation(dst[:, :, :], two, ACT.Copy).then_inc(sem("linear_taken"), 1)
                take = Taking(act)
                act_mla(act, take)
                act_gla(act, take)
                act_rwkv(act, take)

                def rwkv_done(c):
                    act.wait_ge(sem("rw_done"), 1)
                    act.wait_ge(sem("piece_used"), E_BRANCH + 4)

                act_in_split(act, C_RW, o_rwkv, rwkv_done)
                for e in range(E_BRANCH + 8, E_OUT):
                    act_split(act, e + SPLIT)
                act_rms(act, 3, lambda c: mem_n[:, 2 * c:2 * c + 2, :], lambda c: act.wait_ge(sem("mem_here"), 16))
                act_rms_std(act, 3)
                act_in_split(act, C_OUT, merged, lambda c: act.wait_ge(sem("merged"), c + 1))
                act_linear(act, Q_OUT, E_OUT, [yT[:, 2 * i:2 * i + 2, :] for i in range(4)], square=True)

                def mem_normed(c):
                    act.wait_ge(sem("mem_ready"), c + 1)
                    act.wait_ge(sem("piece_used"), E_KV)

                act_in_split(act, C_KV, mem_n, mem_normed)
                act_rms_std(act, 4)
                mem_kv = [mem_k[:, 2 * i:2 * i + 2, :] for i in range(4)] + [mem_v[:, :, i * S:(i + 1) * S] for i in range(4)]
                act_linear(act, Q_KV, E_KV, mem_kv[:4])
                act_rms(act, 5, x_pair, lambda c: act.wait_ge(sem("x_ready"), 4 + c + 1))
                act_linear(act, Q_KV + 4, E_KV + 8, mem_kv[4:5])
                act_rms_std(act, 5)
                act_linear(act, Q_KV + 5, E_KV + 10, mem_kv[5:])
                act_in_split(act, C_Q, zT, in_raw(1))
                act_linear(act, Q_Q, E_Q, [mem_q[:, 2 * i:2 * i + 2, :] for i in range(4)])

                def outs(h):
                    return mem_o[:, 2 * h:2 * h + 2, :], ps[:, h % 2, :].rearrange("p (c t) -> p c t", c=2)

                act_attention(act, "mem", MEM_HEADS, outs)
                act_in_split(act, C_O, mem_o, lambda c: act.wait_ge(sem("mem_out"), c + 1))
                def out_ready(c):
                    act_split(act, E_O + 2 * c + SPLIT)
                    act.wait_ge(sem("piece_used"), E_O + 2 * c + 2)
                    act_split(act, E_O + 2 * c + 1 + SPLIT)

                act_rms(act, 6, mem_y, out_ready)
                act_rms_std(act, 6)
                act_gained(act, lambda c: act.wait_ge(sem("x_ready"), 8 + c + 1), lambda k: col2("norm_g", 6 * KD + k), yT)
                act_rms(act, 7, x_pair, lambda c: act.wait_ge(sem("x_ready"), 12))
                act_ffn(act, 1, E_FFN2, E_END, lambda: act_rms_std(act, 7))
                order = first_order(E_END)
                if not last:
                    act_first(act, l + 1 + LAYERS, order[:1], E_END)
                act_rms(act, 8, two_tiles, ffn_out(act, 1, E_END))
                act_rms_std(act, 8)
                if not last:
                    act_first(act, l + 1 + LAYERS, order[1:], E_END)
                layer_end(act, l + 1 + LAYERS)

            with act.Fori(0, LAYERS - 1) as l:
                layer2(l, False)
            layer2(LAYERS - 1, True)

        @block.vector
        def _(dve):
            nc.vector.memset(ones[:, :], 1.0).then_inc(ones_set, 1)
            dve.wait_ge(ones_set, 1)
            steps = Steps(dve, "rope_step")
            dve.wait_ge(positions_here, 16)
            dve.wait_ge(rope_here, 16)
            steps.link(nc.vector.tensor_scalar(sq[:, 0, :], pos_i[:, :], cst("inv_freq", 1), None, ALU.mult))
            steps.link(nc.vector.tensor_scalar(sq[:, 1, :], sq[:, 0, :], 1.0 / (2 * PI), ROUND, ALU.mult, ALU.add))
            steps.link(nc.vector.tensor_scalar(sq[:, 1, :], sq[:, 1, :], ROUND, None, ALU.subtract))
            for part in (TURN1, TURN2, TURN3):
                steps.link(nc.vector.scalar_tensor_tensor(sq[:, 0, :], sq[:, 1, :], -part, sq[:, 0, :], ALU.mult, ALU.add))
            nc.vector.tensor_scalar(sq[:, 2, :], sq[:, 0, :], 3.1415925, -3.1415925, ALU.min, ALU.max)\
                .then_inc(sem("angle_ready"), 1)
            dve.wait_ge(sem("rope_sin"), 2)
            nc.vector.tensor_scalar(sq[:, 4, :], sq[:, 3, :], -1.0, PI / 2, ALU.mult, ALU.add)\
                .then_inc(sem("angle_ready"), 1)
            dve.wait_ge(sem("rope_sin"), 3)
            nc.vector.tensor_scalar(sin, sin, cst("rope_sign", 1), None, ALU.mult).then_inc(rope_set, 1)
            dve.wait_ge(rope_set, 1)
            low_first(dve, 0, range(SPLIT))
            dve.wait_ge(x_here, 16)
            with dve.Fori(0, LAYERS) as l:
                steps = Steps(dve, "vector_step")
                dve_in_split(dve, C1_FFN1, xT)
                nc.vector.memset(pool_in[:, :, :], 0.0).then_inc(sem("pool_pads"), 1)
                steps.link(nc.vector.memset(conv_z[:, :, :], 0.0))
                dve_ffn(dve, 0, E1_FFN1)
                dve.wait_ge(const_here, 32)
                dve.wait_ge(sem("vec_here"), 16)
                dve_ln(dve, steps, 0, 6, 2 * ALPHA, two_tiles, ffn_out(dve, 0, E1_IN))
                dve.wait_ge(sem("linear_taken"), 1)
                n = S + 2 * POOL_PAD
                steps.link(nc.vector.tensor_tensor(sum2[:, :, 0:n - 1], pool_in[:, :, 0:n - 1], pool_in[:, :, 1:n], ALU.add))
                steps.link(nc.vector.tensor_tensor(sum4[:, :, 0:n - 3], sum2[:, :, 0:n - 3], sum2[:, :, 2:n - 1], ALU.add))
                steps.link(nc.vector.tensor_tensor(sum8[:, :, 0:n - 7], sum4[:, 1:2, 0:n - 7], sum4[:, 1:2, 4:n - 3], ALU.add))
                steps.link(nc.vector.tensor_tensor(sum16[:, :, 0:n - 15], sum8[:, :, 0:n - 15], sum8[:, :, 8:n - 7], ALU.add))
                cnt = cst("pool_cnt", 2 * S).rearrange("p (c t) -> p c t", c=2)
                for g, (w, sums) in enumerate(zip(POOL_W, (sum2[:, 0], sum4[:, 0], sum8[:, 0], sum16[:, 0]))):
                    o = 64 * (g % 2)
                    lo = POOL_PAD - w // 2
                    ins = nc.vector.tensor_tensor(pooled[o:o + 64, g // 2, :], sums[o:o + 64, lo:lo + S],
                                                  cnt[o:o + 64, g // 2, :], ALU.mult)
                steps.link(ins)
                nc.vector.tensor_tensor(pooled[:, :, :], pooled[:, :, :], pool_in[:, :, POOL_PAD:POOL_PAD + S],
                                        ALU.subtract).then_inc(sem("pooled"), 1)
                dve.wait_ge(sem("linear_taken"), 4)
                steps.link(nc.vector.tensor_tensor(conv_z[:, :, 1:S + 1], gate_c[:, :, :], conv_h[:, :, :], ALU.mult))
                for tap in (1, 0, 2):
                    for c in range(2):
                        w = vec1[:, V1["conv_w"] + 2 * tap + c:V1["conv_w"] + 2 * tap + c + 1]
                        z = conv_z[:, c, tap:tap + S]
                        if tap == 1:
                            ins = nc.vector.tensor_scalar(conv_y[:, c, :], z, w, None, ALU.mult)
                        else:
                            ins = nc.vector.scalar_tensor_tensor(conv_y[:, c, :], z, w, conv_y[:, c, :], ALU.mult, ALU.add)
                    steps.link(ins)
                nc.vector.tensor_tensor(mix1[:, 2:4, :], gate_b[:, :, :], conv_y[:, :, :], ALU.mult)\
                    .then_inc(sem("conv_out"), 1)
                dve.wait_ge(sem("bias_here"), 16 * 2 * NA_HEADS)
                strips = na_bias.rearrange("p h (e k) -> p (h e) k", k=GRID)
                mask = cst("na_mask", GRID).rearrange("p (o k) -> p o k", o=1).broadcast_to([P, NA_HEADS * STRIPS, GRID])
                steps.link(nc.vector.tensor_tensor(strips[:, :, ::-1], na_raw, mask, ALU.min))
                dve_attention(dve, steps, "na", NA_HEADS, 64 ** -0.5,
                              lambda h, t: na_bias[:, h, (2 - 2 * t) * GRID:(6 - 2 * t) * GRID])
                dve_in_split(dve, C1_OUT, mix1)
                dve_ln(dve, steps, 1, 0, ALPHA, lambda c: two_tiles(4 + (10 + c) % 4),
                       lambda c: dve.wait_ge(sem("piece_used"), E1_OUT + 2 * c + 2))
                dve_ffn(dve, 1, E1_FFN2)
                dve_ln(dve, steps, 2, 6, 2 * ALPHA, two_tiles, ffn_out(dve, 1, E1_END))
                layer_end(dve, l + 1)
            with dve.Fori(0, LAYERS) as l:
                steps = Steps(dve, "mix_step")
                dve.wait_ge(first_gains_here, 16)
                nc.vector.tensor_copy(first_gain[:, :], first_gains[:, bass.ds(l, 1), :].rearrange("p o k -> p (o k)"))\
                    .then_inc(sem("first_gain"), 1)
                nc.vector.memset(rz[:, :, 0:1], 0.0).then_inc(sem("rz_cleared"), 1)
                dve.wait_ge(sem("first_gain"), 1)
                for c in range(KD // 2):
                    dve.wait_ge(sem("in_high"), C_FFN1 + c + 1)
                    for k in (2 * c, 2 * c + 1):
                        ins = nc.vector.scalar_tensor_tensor(in_lo[:, k, :], xT[:, k, :], first_gain[:, k:k + 1],
                                                             in_hi[:, k, :].bitcast(F32), ALU.mult, ALU.subtract)
                    ins.then_inc(sem("in_ready"), 1)
                dve_ffn(dve, 0, E_FFN1, lambda: dve_inverse(dve, steps, 0))
                dve.wait_ge(sem("gains_here"), 16)
                dve_residual(dve, steps, 1, 0, two_tiles, lambda k: col2("norm_g", KD + k), 0.5)
                dve_rms(dve, steps, 2, xT, lambda k: col2("norm_g", 2 * KD + k), zT)
                dve_mla(dve, steps)
                dve_gla(dve, steps)
                dve_rwkv(dve, steps)
                dve_in_split(dve, C_RW, o_rwkv)
                dve.wait_ge(sem("filling_taken"), MIX_SLOTS - FIRST_SLOTS)
                gates_b = [gates[:, b * KD:(b + 1) * KD, :] for b in range(3)]
                for b, y in enumerate((y_mla, y_gla)):
                    dve.wait_ge(sem("branch_taken"), 4 * b + 4)
                    steps.link(nc.vector.tensor_tensor(gates_b[b], gates_b[b], y, ALU.mult))
                steps.link(nc.vector.tensor_tensor(merged, merged, gates_b[1], ALU.add))
                for i in range(4):
                    q = Q_BRANCH + i
                    two = slice(2 * i, 2 * i + 2)
                    dve.wait_ge(sem("piece_used"), E_BRANCH + 8 + i + 1)
                    nc.vector.tensor_tensor(gates_b[2][:, two, :], gates_b[2][:, two, :], two_tiles(4 + q % 4), ALU.mult)\
                        .then_inc(sem("linear_taken"), 1)
                    dve.wait_ge(sem("linear_taken"), q + 1)
                    nc.vector.tensor_tensor(merged[:, two, :], merged[:, two, :], gates_b[2][:, two, :], ALU.add)\
                        .then_inc(sem("merged"), 1)
                dve_in_split(dve, C_OUT, merged)
                dve_rms(dve, steps, 3, mem_n, lambda k: col2("mem_norm", k), mem_n, C_KV, "mem_ready")
                dve_residual(dve, steps, 4, 1, lambda c: yT[:, 2 * c:2 * c + 2, :], lambda k: col2("norm_g", 3 * KD + k), 1.0)
                dve_rms(dve, steps, 5, xT, lambda k: col2("norm_g", 4 * KD + k), zT, C_Q)
                dve_attention(dve, steps, "mem", MEM_HEADS, 256 ** -0.5, lambda h, t: None)
                dve_in_split(dve, C_O, mem_o)
                dve_residual(dve, steps, 6, 2, mem_y, lambda k: col2("norm_g", 5 * KD + k), 1.0)
                dve_ffn(dve, 1, E_FFN2, lambda: dve_inverse(dve, steps, 7))
                dve_residual(dve, steps, 8, 3, two_tiles, lambda k: col2("norm_g", 7 * KD + k), 0.5)
                layer_end(dve, l + 1 + LAYERS)

        @block.gpsimd
        def _(pool):
            pool.memset(pool_w[:, :, :], 0.0).then_inc(sem_pw, 1)
            with pool.Fori(0, LAYERS) as l:
                pool_layer(pool, l)
                pool_low(pool, E1_IN, SPLIT)
                pool_in_low(pool, C1_IN, xT)
                pool_low(pool, E1_IN + SPLIT, E1_FFN2 - E1_IN)
                pool_in_low(pool, C1_FFN2, xT)
                low_first(pool, l + 1, first_order(E1_END))
                layer_end(pool, l + 1)

            def layer2(l, last):
                pool_layer(pool, l + LAYERS)
                pool_low(pool, E_IN, SPLIT)
                pool_in_low(pool, C_IN, zT)
                pool_low(pool, E_IN + SPLIT, E_FILL - E_IN - SPLIT)
                pool_filling(pool)
                pool_low(pool, E_BRANCH + SPLIT, E_FFN2 - E_BRANCH)
                pool_in_low(pool, C_FFN2, yT)
                if not last:
                    low_first(pool, l + 1 + LAYERS, first_order(E_END))
                layer_end(pool, l + 1 + LAYERS)

            with pool.Fori(0, LAYERS - 1) as l:
                layer2(l, False)
            layer2(LAYERS - 1, True)

        @block.sync
        def _(sp):
            g1 = a["ffn1_w_gate"].rearrange("l (k p) f -> l p k f", p=P)
            u1 = a["ffn1_w_up"].rearrange("l (k p) f -> l p k f", p=P)
            d1 = a["ffn1_w_down"].rearrange("l (j p) d -> l p j d", p=P)
            g2 = a["ffn2_w_gate"].rearrange("l (k p) f -> l p k f", p=P)
            u2 = a["ffn2_w_up"].rearrange("l (k p) f -> l p k f", p=P)
            d2 = a["ffn2_w_down"].rearrange("l (j p) d -> l p j d", p=P)
            w_in = a["w_in"].rearrange("l (k p) f -> l p k f", p=P)
            w_out = a["w_out"].rearrange("l (k p) f -> l p k f", p=P)

            f_in = a["w_ffn_in_2"].rearrange("l n (k p) f -> l n p k f", p=P)
            f_out = a["w_ffn_out_2"].rearrange("l n (j p) d -> l n p j d", p=P)
            mix_in = a["w_mix"].rearrange("l (k p) f -> l p k f", p=P)
            w_branch = a["w_branch_2"].rearrange("l (b k p) f -> l b p k f", p=P, k=4)
            w_out2 = a["w_out_2"].rearrange("l (k p) f -> l p k f", p=P)
            wkv = a["mem_wkv_2"].rearrange("l (k p) f -> l p k f", p=P)
            wq = a["mem_wq_2"].rearrange("l (k p) f -> l p k f", p=P)
            wo = a["mem_wo_2"].rearrange("l (k p) f -> l p k f", p=P)

            def sources(g, u, d, up_at=0):
                return (lambda c: g[:, :, bass.ds(c, P)], lambda c: u[:, :, bass.ds(c + up_at, P)], lambda c: d_rows(d, c))

            def d_rows(d, c):
                return d[:, c // P:c // P + 1, :] if isinstance(c, int) else d[:, bass.ds(c // P, 1), :]

            def columns(w, n, token_slots=()):
                for i in range(n):
                    c = i * S
                    for h in range(2):
                        yield (w[:, h * KD // 2:(h + 1) * KD // 2, c:c + S] if i in token_slots else
                               w[:, :, c + h * P:c + (h + 1) * P])

            def ffn1(l):
                return sources(g1[l], u1[l], d1[l])

            def ffn2(l, n):
                return sources(f_in[l, n], f_in[l, n], f_out[l, n], F)

            two = slice(CONST["inv_freq"], CONST["rope_sign"] + 1)
            sp.dma_start(const[:, two], a["const"][:, two]).then_inc(rope_here, 16)
            pos = a["positions"]
            sp.dma_start(pos_i[:, :], bass.AP(tensor=pos.tensor, offset=pos.offset, ap=[[0, P], [1, S]])).then_inc(positions_here, 16)
            sp_first(sp, *ffn1(0))
            for rest in (slice(0, two.start), slice(two.stop, CONST_N)):
                sp.dma_start(const[:, rest], a["const"][:, rest]).then_inc(const_here, 16)
            sp.dma_start(first_gains[:, :, :], a["vec2"][:, :, 0:KD].rearrange("l p k -> p l k")).then_inc(first_gains_here, 16)

            def layer1(l, following):
                sp_ffn(sp, E1_FFN1, *ffn1(l))
                sp.dma_start(vec1[:, :], a["vec1"][l]).then_inc(sem("vec_here"), 16)
                sp.wait_ge(sem_pw, 1)
                for g in range(4):
                    o = 64 * (g % 2)
                    sp.dma_start(pool_w[o:o + 64, g // 2, o:o + 64], a["pool_w"][l][g]).then_inc(sem("pool_w_here"), 16)
                for half in range(2):
                    for h in range(NA_HEADS):
                        row = a["rpb"][l][h]
                        src = bass.AP(tensor=row.tensor, offset=row.offset + (5 - half) * RPB_C + 15 - (GRID - 1),
                                      ap=[[1, GRID], [RPB_C, STRIPS], [1, GRID]])
                        sp.dma_start(na_raw[64 * half:64 * half + 64, h * STRIPS:(h + 1) * STRIPS, :],
                                     src).then_inc(sem("bias_here"), 16)
                sp_linear(sp, E1_IN, columns(w_in[l], 10, (8, 9)))
                sp_linear(sp, E1_OUT, columns(w_out[l], 4))
                sp_ffn(sp, E1_FFN2, *sources(g2[l], u2[l], d2[l]))
                sp_first(sp, *following, before=E1_END)
                layer_end(sp, l + 1)

            with sp.Fori(0, LAYERS - 1) as l:
                layer1(l, ffn1(l + 1))
            layer1(LAYERS - 1, ffn2(0, 0))

            def layer2(l, following=None):
                sp.dma_start(vec2, a["vec2"][l]).then_inc(sem("gains_here"), 16)
                sp_ffn(sp, E_FFN1, *ffn2(l, 0))
                for dst, src in ((w_uq, a["w_uq"][l].rearrange("(k p) c -> p k c", p=P)),
                                 (w_ukv, a["w_ukv"][l]), (w_alpha[0:16, :], a["gla_w_alpha_2"][l]),
                                 (w_lora[0:64, :], a["rwkv_w_decay_2"][l]), (w_lora[64:P, :], a["rwkv_w_iclr_2"][l]),
                                 (w_rgate[:, 0, :], a["rwkv_w_gate_2"][l][0:P, :]),
                                 (w_rgate[32:64, 1, :], a["rwkv_w_gate_2"][l][P:P + 32, :])):
                    sp.dma_start(dst, src).then_inc(sem("small_here"), 16)
                sp_linear(sp, E_IN, columns(mix_in[l], MIX_SLOTS, (FILL_GLA + 2, FILL_GLA + 3)))
                sp_linear(sp, E_BRANCH, [w_branch[l, b][:, :, i * S:(i + 1) * S] for b in range(3) for i in range(4)])
                sp.wait_ge(sem("rw_done"), 1)
                sp.dma_start(mem_n, a["memT"]).then_inc(sem("mem_here"), 16)
                for w, e0, n, token_slots in ((w_out2, E_OUT, 4, ()), (wkv, E_KV, 8, range(4, 8)), (wq, E_Q, 4, ()), (wo, E_O, 4, ())):
                    sp_linear(sp, e0, columns(w[l], n, token_slots))
                sp_ffn(sp, E_FFN2, *ffn2(l, 1))
                if following is not None:
                    sp_first(sp, *following, before=E_END)
                layer_end(sp, l + 1 + LAYERS)

            with sp.Fori(0, LAYERS - 1) as l:
                layer2(l, ffn2(l + 1, 0))
            layer2(LAYERS - 1)
            sp.dma_start(out, xT[:, :, :]).then_inc(stored, 16)
            sp.wait_ge(stored, 16)


def host_arrays(i):
    L = LAYERS
    arr = {"const": constants()}

    def fm(x):
        return np.ascontiguousarray(np.asarray(x)[0].T.reshape(KD, P, S).transpose(1, 0, 2))

    def cols(v):
        v = np.asarray(v)
        v = v.reshape(L, -1, P)
        return v.transpose(0, 2, 1)

    arr["xT"] = fm(i["x"])
    arr["memT"] = fm(i["mem_2"])
    arr["positions"] = np.ascontiguousarray(np.asarray(i["positions_2"]).reshape(S))
    w = np.asarray(i["w_in_2"])
    rope = w[:, :, 384:416]
    swapped = np.concatenate([rope[:, :, 16:], rope[:, :, :16]], axis=2)
    narrow = np.zeros((L, D, P), w.dtype)
    narrow[:, :, 0:16] = w[:, :, 1952:1968]
    narrow[:, :, 32:64] = w[:, :, 3760:3792]
    arr["w_mix"] = np.concatenate([w[:, :, 0:384], narrow] + [rope] * 4 + [swapped] * 4 + [w[:, :, 416:1952],
                                  w[:, :, 1968:3760], w[:, :, 3792:]], axis=2)
    w = np.asarray(i["mla_w_uq_2"]).reshape(L, 256, MLA_HEADS, 96)
    parts = [w[..., :64], w[..., 64:], np.concatenate([w[..., 80:], w[..., 64:80]], axis=3)]
    arr["w_uq"] = np.concatenate([p.reshape(L, 256, -1) for p in parts], axis=2)
    w = np.asarray(i["mla_w_ukv_2"]).reshape(L, P, MLA_HEADS, 2, 64)
    arr["w_ukv"] = np.ascontiguousarray(w.transpose(0, 1, 3, 2, 4).reshape(L, P, -1))
    mu = np.asarray(i["rwkv_mu_2"])
    last = np.zeros((L, P), mu.dtype)
    last[:, 32:64] = mu[:, 1792:]
    arr["vec2"] = np.ascontiguousarray(np.concatenate(
        [cols(i["norm_g_2"]), cols(i["mem_norm_2"]), cols(i["mla_q_norm_2"]), cols(i["mla_kv_norm_2"]),
         cols(i["gla_b_alpha_2"]), cols(i["gla_norm_2"]), cols(mu[:, :1792]), cols(last)] +
        [cols(i["rwkv_" + n + "_2"]) for n in ("w0", "a0", "k_k", "k_a", "r_k", "ln_w", "ln_b")], axis=2))
    arr["vec1"] = np.ascontiguousarray(np.concatenate([cols(i["ln_g"]), cols(i["ln_b"]), cols(i["pool_scale"]),
                                                       cols(i["conv_w"])], axis=2))
    arr["rpb"] = np.ascontiguousarray(np.asarray(i["rpb"])[..., ::-1])
    for n in ("ffn1_w_gate", "ffn1_w_up", "ffn1_w_down", "ffn2_w_gate", "ffn2_w_up", "ffn2_w_down", "w_in", "pool_w",
              "w_out", "w_ffn_in_2", "w_ffn_out_2", "gla_w_alpha_2", "rwkv_w_decay_2", "rwkv_w_iclr_2",
              "rwkv_w_gate_2", "w_branch_2", "w_out_2", "mem_wq_2", "mem_wkv_2", "mem_wo_2"):
        arr[n] = np.ascontiguousarray(i[n])
    return arr


def kernel(**inputs):
    import concourse.bacc as bacc
    from concourse.bass_utils import run_bass_kernel_spmd

    nc = bacc.Bacc("TRN2", target_bir_lowering=False, num_devices=1, dynamic_dma_scratch_size=1024)
    arrays = host_arrays(inputs)
    aps = {n: nc.dram_tensor(f"in_{n}", v.shape, mybir.dt.from_np(v.dtype), kind="ExternalInput").ap()
           for n, v in arrays.items()}
    out = nc.dram_tensor("out_xT", (P, KD, S), F32, kind="ExternalOutput").ap()
    build(nc, aps, out)
    r = run_bass_kernel_spmd(nc, [{f"in_{n}": v for n, v in arrays.items()}], core_ids=[0])
    y = r.results[0]["out_xT"]
    return np.ascontiguousarray(y.transpose(1, 0, 2).reshape(D, S).T)[None]
```
